# Optimizing a Trainium2 kernel written in Bass

```python
import jax
import jax.numpy as jnp
from jax import lax
import numpy as np
import jax, jax.numpy as jnp

D_MODEL = 1024
BATCH = 1
SEQ = 512
DEPTH = 2

CTX_LEN = 256
GRID_W = 64
EPS = 1e-6

D_CONV = 512
CONV_WIDTH = 31
GLA_HEADS = 4
GLA_DK = 64
GLA_DV = 128
GLA_QK = GLA_HEADS * GLA_DK
GLA_V = GLA_HEADS * GLA_DV
GLA_RANK = 16
GLA_GATE_NORM = 16.0
GLA_CHUNK = 64
ATT_HEADS = 8
ATT_KV_HEADS = 2
ATT_GROUP = ATT_HEADS // ATT_KV_HEADS
ATT_HD = 64
ATT_Q = ATT_HEADS * ATT_HD
ATT_KV = ATT_KV_HEADS * ATT_HD
ATT_BLOCK = 128
ROPE_AXIS_DIM = ATT_HD // 2
ROPE_THETA = 10000.0

IN_SPLITS = (D_CONV, D_CONV, D_CONV,
             GLA_QK, GLA_QK, GLA_V, GLA_V, GLA_RANK, GLA_RANK,
             ATT_Q, ATT_KV, ATT_KV, ATT_Q,
             D_MODEL, D_MODEL, D_MODEL)
N_IN = sum(IN_SPLITS)


def rms_norm(x, g):
    xf = x.astype(jnp.float32)
    y = xf * lax.rsqrt(jnp.mean(xf * xf, axis=-1, keepdims=True) + EPS)
    return (y * g.astype(jnp.float32)).astype(x.dtype)

def layer_norm(x, g, b):
    xf = x.astype(jnp.float32)
    mu = jnp.mean(xf, axis=-1, keepdims=True)
    var = jnp.mean(jnp.square(xf - mu), axis=-1, keepdims=True)
    y = (xf - mu) * lax.rsqrt(var + EPS)
    return (y * g.astype(jnp.float32) + b.astype(jnp.float32)).astype(x.dtype)

def split_cols(p):
    idx = np.cumsum(np.array(IN_SPLITS))[:-1].tolist()
    return jnp.split(p, idx, axis=-1)

def conv_module(val, glu, gate, dw_w, dw_b, ln_g, ln_b, w_o):
    u = val * jax.nn.sigmoid(glu)
    pad = CONV_WIDTH // 2
    u = lax.conv_general_dilated(u, dw_w[:, None, :], window_strides=(1,),
                                 padding=[(pad, pad)],
                                 dimension_numbers=('NWC', 'WIO', 'NWC'),
                                 feature_group_count=D_CONV) + dw_b
    u = jax.nn.silu(layer_norm(u, ln_g, ln_b)) * jax.nn.silu(gate)
    return u @ w_o

def gla_scan(q, k, v, log_a, s0):
    b_, t_, h_, _ = q.shape
    dv = v.shape[-1]
    n = t_ // GLA_CHUNK

    def chunks(z):
        return z.astype(jnp.float32).reshape(b_, n, GLA_CHUNK, h_, z.shape[-1])

    q, k, v, log_a = chunks(q), chunks(k), chunks(v), chunks(log_a)
    cum = jnp.cumsum(log_a, axis=2)
    last = cum[:, :, -1]
    q_in = q * jnp.exp(cum)
    k_in = k * jnp.exp(-cum)
    mask = jnp.tril(jnp.ones((GLA_CHUNK, GLA_CHUNK), dtype=bool))
    att = jnp.where(mask, jnp.einsum('bnihd,bnjhd->bnhij', q_in, k_in), 0.0)
    o_intra = jnp.einsum('bnhij,bnjhe->bnihe', att, v)
    k_state = k * jnp.exp(last[:, :, None] - cum)
    contrib = jnp.einsum('bnjhd,bnjhe->bnhde', k_state, v)
    decay = jnp.exp(last)

    def step(s, inp):
        dec, con = inp
        return dec[..., None] * s + con, s

    s_fin, s_prev = lax.scan(step, s0, (jnp.swapaxes(decay, 0, 1), jnp.swapaxes(contrib, 0, 1)))
    o_inter = jnp.einsum('bnihd,bnhde->bnihe', q_in, jnp.swapaxes(s_prev, 0, 1))
    return (o_intra + o_inter).reshape(b_, t_, h_, dv), s_fin

def gla_heads(q, k, v):
    b_, t_, _ = q.shape
    return (q.reshape(b_, t_, GLA_HEADS, GLA_DK) * (GLA_DK ** -0.5),
            k.reshape(b_, t_, GLA_HEADS, GLA_DK),
            v.reshape(b_, t_, GLA_HEADS, GLA_DV))

def gla_log_gate(lr, w_up, b_up):
    b_, t_, _ = lr.shape
    z = (lr @ w_up + b_up).astype(jnp.float32)
    return (jax.nn.log_sigmoid(z) / GLA_GATE_NORM).reshape(b_, t_, GLA_HEADS, GLA_DK)

def gla_output(o, gate, norm_g, w_o):
    b_, t_ = o.shape[:2]
    o = rms_norm(o, norm_g).reshape(b_, t_, GLA_V).astype(gate.dtype)
    return (o * jax.nn.silu(gate)) @ w_o

def gla_branch(xp, cp, w_up, b_up, norm_g, w_o, need_ctx):
    xq, xk, xv, xg, xlf, xlb = xp
    cq, ck, cv, cg, clf, clb = cp
    xq, xk, xv = gla_heads(xq, xk, xv)
    cq, ck, cv = gla_heads(cq, ck, cv)
    s0 = jnp.zeros((xq.shape[0], GLA_HEADS, GLA_DK, GLA_DV), jnp.float32)

    def flip(z):
        return jnp.flip(z, axis=1)

    oc_f, sc_f = gla_scan(cq, ck, cv, gla_log_gate(clf, w_up[0], b_up[0]), s0)
    ox_f, _ = gla_scan(xq, xk, xv, gla_log_gate(xlf, w_up[0], b_up[0]), sc_f)
    oc_b, sc_b = gla_scan(flip(cq), flip(ck), flip(cv),
                          flip(gla_log_gate(clb, w_up[1], b_up[1])), s0)
    ox_b, _ = gla_scan(flip(xq), flip(xk), flip(xv),
                       flip(gla_log_gate(xlb, w_up[1], b_up[1])), sc_b)
    y_x = gla_output(ox_f + flip(ox_b), xg, norm_g, w_o)
    y_c = gla_output(oc_f + flip(oc_b), cg, norm_g, w_o) if need_ctx else None
    return y_x, y_c

def rope_tables(t_):
    n_rows = t_ // GRID_W
    row = jnp.repeat(jnp.arange(n_rows, dtype=jnp.float32), GRID_W)
    col = jnp.tile(jnp.arange(GRID_W, dtype=jnp.float32), n_rows)
    n_freq = ROPE_AXIS_DIM // 2
    freqs = ROPE_THETA ** (-jnp.arange(n_freq, dtype=jnp.float32) / n_freq)
    ang_r = row[:, None] * freqs
    ang_c = col[:, None] * freqs
    return jnp.cos(ang_r), jnp.sin(ang_r), jnp.cos(ang_c), jnp.sin(ang_c)

def rotate_half(x, cos, sin):
    x1, x2 = jnp.split(x, 2, axis=-1)
    cos = cos[:, None, :]
    sin = sin[:, None, :]
    return jnp.concatenate([x1 * cos - x2 * sin, x2 * cos + x1 * sin], axis=-1)

def rope_2d(x, tabs):
    cr, sr, cc, sc = tabs
    xr, xcol = jnp.split(x.astype(jnp.float32), 2, axis=-1)
    return jnp.concatenate([rotate_half(xr, cr, sr), rotate_half(xcol, cc, sc)], axis=-1).astype(x.dtype)

def attn_heads(q, k, v, qn_g, kn_g, tabs):
    b_, t_, _ = q.shape
    q = rms_norm(q.reshape(b_, t_, ATT_HEADS, ATT_HD), qn_g)
    k = rms_norm(k.reshape(b_, t_, ATT_KV_HEADS, ATT_HD), kn_g)
    if tabs is not None:
        q, k = rope_2d(q, tabs), rope_2d(k, tabs)
    return (q.reshape(b_, t_, ATT_KV_HEADS, ATT_GROUP, ATT_HD), k,
            v.reshape(b_, t_, ATT_KV_HEADS, ATT_HD))

def gqa_attend(q, k, v):
    s = jnp.einsum('bqkgd,bskd->bkgqs', q, k).astype(jnp.float32) * (ATT_HD ** -0.5)
    p = jax.nn.softmax(s, axis=-1).astype(v.dtype)
    return jnp.einsum('bkgqs,bskd->bqkgd', p, v)

def attn_branch(xp, cp, qn_g, kn_g, w_o, need_ctx):
    xq, xk, xv, xg = xp
    cq, ck, cv, cg = cp
    b_, t_, _ = xq.shape
    xq, xk, xv = attn_heads(xq, xk, xv, qn_g, kn_g, rope_tables(t_))
    cq, ck, cv = attn_heads(cq, ck, cv, qn_g, kn_g, None)
    k_all = jnp.concatenate([ck, xk], axis=1)
    v_all = jnp.concatenate([cv, xv], axis=1)
    n_blk = t_ // ATT_BLOCK
    q_blk = jnp.swapaxes(xq.reshape(b_, n_blk, ATT_BLOCK, ATT_KV_HEADS, ATT_GROUP, ATT_HD), 0, 1)
    o = lax.map(lambda qb: gqa_attend(qb, k_all, v_all), q_blk)
    o = jnp.swapaxes(o, 0, 1).reshape(b_, t_, ATT_Q)
    y_x = (o * jax.nn.silu(xg)) @ w_o
    y_c = None
    if need_ctx:
        oc = gqa_attend(cq, ck, cv).reshape(b_, cq.shape[1], ATT_Q)
        y_c = (oc * jax.nn.silu(cg)) @ w_o
    return y_x, y_c

def hybrid_layer(xs, cs, c, c_ctx, norm_g, w_mod, b_mod, w_in, b_in, dw_w, dw_b, ln_g, ln_b,
                 w_conv_out, gla_w_gate, gla_b_gate, gla_norm_g, w_gla_out, q_norm_g, k_norm_g,
                 w_attn_out, w_out, need_ctx):
    shift_x, scale_x, gate_x = jnp.split(jax.nn.silu(c) @ w_mod + b_mod, 3, axis=-1)
    shift_c, scale_c, gate_c = jnp.split(jax.nn.silu(c_ctx) @ w_mod + b_mod, 3, axis=-1)
    hx = rms_norm(xs, norm_g) * (1 + scale_x[:, None]) + shift_x[:, None]
    hc = rms_norm(cs, norm_g) * (1 + scale_c) + shift_c
    px = split_cols(hx @ w_in + b_in)
    pc = split_cols(hc @ w_in + b_in)

    ya_x = conv_module(*px[0:3], dw_w, dw_b, ln_g, ln_b, w_conv_out)
    yb_x, yb_c = gla_branch(px[3:9], pc[3:9], gla_w_gate, gla_b_gate, gla_norm_g, w_gla_out, need_ctx)
    yc_x, yc_c = attn_branch(px[9:13], pc[9:13], q_norm_g, k_norm_g, w_attn_out, need_ctx)

    def merge(p, ya, yb, yc):
        return (jax.nn.sigmoid(p[13]) * ya + jax.nn.sigmoid(p[14]) * yb
                + jax.nn.sigmoid(p[15]) * yc) @ w_out

    xs = xs + gate_x[:, None] * merge(px, ya_x, yb_x, yc_x)
    if need_ctx:
        ya_c = conv_module(*pc[0:3], dw_w, dw_b, ln_g, ln_b, w_conv_out)
        cs = cs + gate_c * merge(pc, ya_c, yb_c, yc_c)
    return xs, cs

def first_inputs(seed: int = 0) -> dict:
    key = jax.random.key(seed)
    ks = jax.random.split(key, 22)

    def nrm(k, shape, s):
        return jax.random.normal(k, shape, jnp.float32) * s

    return {
        'x': nrm(ks[0], (BATCH, SEQ, D_MODEL), 1.0),
        'c': nrm(ks[1], (BATCH, D_MODEL), 1.0),
        'ctx': nrm(ks[2], (BATCH, CTX_LEN, D_MODEL), 1.0),
        'c_ctx': nrm(ks[3], (D_MODEL,), 1.0),
        'norm_g': 1.0 + nrm(ks[4], (DEPTH, D_MODEL), 0.02),
        'w_mod': nrm(ks[5], (DEPTH, D_MODEL, 3 * D_MODEL), 0.5 * D_MODEL ** -0.5),
        'b_mod': nrm(ks[6], (DEPTH, 3 * D_MODEL), 0.01),
        'w_in': nrm(ks[7], (DEPTH, D_MODEL, N_IN), D_MODEL ** -0.5),
        'b_in': nrm(ks[8], (DEPTH, N_IN), 0.01),
        'conv_dw_w': nrm(ks[9], (DEPTH, CONV_WIDTH, D_CONV), CONV_WIDTH ** -0.5),
        'conv_dw_b': nrm(ks[10], (DEPTH, D_CONV), 0.01),
        'conv_ln_g': 1.0 + nrm(ks[11], (DEPTH, D_CONV), 0.02),
        'conv_ln_b': nrm(ks[12], (DEPTH, D_CONV), 0.01),
        'w_conv_out': nrm(ks[13], (DEPTH, D_CONV, D_MODEL), D_CONV ** -0.5),
        'gla_w_gate': nrm(ks[14], (DEPTH, 2, GLA_RANK, GLA_QK), GLA_RANK ** -0.5),
        'gla_b_gate': nrm(ks[15], (DEPTH, 2, GLA_QK), 0.1),
        'gla_norm_g': 1.0 + nrm(ks[16], (DEPTH, GLA_DV), 0.02),
        'w_gla_out': nrm(ks[17], (DEPTH, GLA_V, D_MODEL), GLA_V ** -0.5),
        'q_norm_g': 1.0 + nrm(ks[18], (DEPTH, ATT_HD), 0.02),
        'k_norm_g': 1.0 + nrm(ks[19], (DEPTH, ATT_HD), 0.02),
        'w_attn_out': nrm(ks[20], (DEPTH, ATT_Q, D_MODEL), ATT_Q ** -0.5),
        'w_out': nrm(ks[21], (DEPTH, D_MODEL, D_MODEL), D_MODEL ** -0.5),
    }

def first_block(x, c, ctx, c_ctx, norm_g, w_mod, b_mod, w_in, b_in, conv_dw_w, conv_dw_b,
              conv_ln_g, conv_ln_b, w_conv_out, gla_w_gate, gla_b_gate, gla_norm_g, w_gla_out,
              q_norm_g, k_norm_g, w_attn_out, w_out):
    xs, cs = x, ctx
    for l in range(DEPTH):
        xs, cs = hybrid_layer(xs, cs, c, c_ctx, norm_g[l], w_mod[l], b_mod[l], w_in[l], b_in[l],
                              conv_dw_w[l], conv_dw_b[l], conv_ln_g[l], conv_ln_b[l], w_conv_out[l],
                              gla_w_gate[l], gla_b_gate[l], gla_norm_g[l], w_gla_out[l],
                              q_norm_g[l], k_norm_g[l], w_attn_out[l], w_out[l],
                              need_ctx=(l < DEPTH - 1))
    return xs


D_INNER = 2 * D_MODEL
D_MLSTM = D_INNER // 2
D_RET = D_INNER - D_MLSTM
N_HEADS_MLSTM = 4
N_HEADS_RET = 4
HD_M = D_MLSTM // N_HEADS_MLSTM
HD_R = D_RET // N_HEADS_RET
CONV_K = 4
CHUNK = 64
ROPE_BASE = 10000.0
D_IN_PROJ = 5 * D_MLSTM + 2 * N_HEADS_MLSTM + 4 * D_RET


def rmsnorm(x, g):
    xf = x.astype(jnp.float32)
    y = xf * lax.rsqrt(jnp.mean(xf * xf, axis=-1, keepdims=True) + EPS)
    return (y * g.astype(jnp.float32)).astype(x.dtype)

def head_layernorm(h, g, n_heads):
    B, S, W = h.shape
    hf = h.astype(jnp.float32).reshape(B, S, n_heads, W // n_heads)
    mu = jnp.mean(hf, axis=-1, keepdims=True)
    var = jnp.mean(jnp.square(hf - mu), axis=-1, keepdims=True)
    y = ((hf - mu) * lax.rsqrt(var + EPS)).reshape(B, S, W)
    return (y * g.astype(jnp.float32)).astype(h.dtype)

def causal_dwconv(x, w, b):
    S = x.shape[1]
    xp = jnp.pad(x, ((0, 0), (CONV_K - 1, 0), (0, 0)))
    y = xp[:, 0:S] * w[0]
    for t in range(1, CONV_K):
        y = y + xp[:, t:t + S] * w[t]
    return y + b

def split_cols_2(p):
    sizes = [D_MLSTM] * 5 + [N_HEADS_MLSTM] * 2 + [D_RET] * 4
    idx = np.cumsum(sizes)[:-1].tolist()
    return jnp.split(p, idx, axis=-1)

def to_chunks(t):
    B, S, H, d = t.shape
    return t.reshape(B, S // CHUNK, CHUNK, H, d).transpose(1, 0, 3, 2, 4)

def from_chunks(t):
    NC, B, H, L, d = t.shape
    return t.transpose(1, 0, 3, 2, 4).reshape(B, NC * L, H * d)

def gate_chunks(t):
    B, S, H = t.shape
    return t.reshape(B, S // CHUNK, CHUNK, H).transpose(1, 0, 3, 2)

def rotary(t, positions):
    d = t.shape[-1]
    inv_freq = 1.0 / (ROPE_BASE ** jnp.linspace(0.0, 1.0, d // 2, dtype=jnp.float32))
    ang = positions.astype(jnp.float32)[..., None] * inv_freq
    cos = jnp.cos(ang)[:, :, None, :].astype(t.dtype)
    sin = jnp.sin(ang)[:, :, None, :].astype(t.dtype)
    t1, t2 = jnp.split(t, 2, axis=-1)
    return jnp.concatenate([t1 * cos - t2 * sin, t2 * cos + t1 * sin], axis=-1)

def mlstm_chunkwise(q, k, v, i_pre, f_pre):
    B, S, H, d = q.shape
    k = k * (d ** -0.5)
    li = gate_chunks(i_pre.astype(jnp.float32))
    lf = gate_chunks(jax.nn.log_sigmoid(f_pre.astype(jnp.float32)))
    causal = jnp.tril(jnp.ones((CHUNK, CHUNK), dtype=bool))

    def step(carry, inp):
        C, n, m = carry
        qj, kj, vj, lij, lfj = inp
        b = jnp.cumsum(lfj, axis=-1)
        a = b + m[..., None]
        g = b[..., :, None] - b[..., None, :] + lij[..., None, :]
        g = jnp.where(causal, g, -jnp.inf)
        m_row = jnp.maximum(a, jnp.max(g, axis=-1))
        w_intra = jnp.exp(g - m_row[..., None])
        w_inter = jnp.exp(a - m_row)
        s = jnp.einsum('bhld,bhsd->bhls', qj, kj) * w_intra
        num = (jnp.einsum('bhls,bhsv->bhlv', s, vj)
               + w_inter[..., None] * jnp.einsum('bhvk,bhlk->bhlv', C, qj))
        den = jnp.sum(s, axis=-1) + w_inter * jnp.einsum('bhk,bhlk->bhl', n, qj)
        h = num / jnp.maximum(jnp.abs(den), jnp.exp(-m_row))[..., None]
        bL = b[..., -1]
        g_end = bL[..., None] - b + lij
        m_new = jnp.maximum(bL + m, jnp.max(g_end, axis=-1))
        w_end = jnp.exp(g_end - m_new[..., None])
        decay = jnp.exp(bL + m - m_new)
        C_new = decay[..., None, None] * C + jnp.einsum('bhs,bhsv,bhsk->bhvk', w_end, vj, kj)
        n_new = decay[..., None] * n + jnp.einsum('bhs,bhsk->bhk', w_end, kj)
        return (C_new, n_new, m_new), h.astype(q.dtype)

    init = (jnp.zeros((B, H, d, d), jnp.float32),
            jnp.zeros((B, H, d), jnp.float32),
            jnp.zeros((B, H), jnp.float32))
    _, hs = lax.scan(step, init, (to_chunks(q), to_chunks(k), to_chunks(v), li, lf))
    return from_chunks(hs)

def retention_chunkwise(q, k, v):
    B, S, H, d = q.shape
    k = k * (d ** -0.5)
    log_gamma = jnp.log(1.0 - 2.0 ** (-5.0 - jnp.arange(H, dtype=jnp.float32)))
    pos = jnp.arange(CHUNK, dtype=jnp.float32)
    diff = pos[:, None] - pos[None, :]
    Dmat = jnp.where(diff >= 0, jnp.exp(log_gamma[:, None, None] * jnp.maximum(diff, 0.0)), 0.0)
    xi = jnp.exp(log_gamma[:, None] * (pos + 1.0))
    zeta = jnp.exp(log_gamma[:, None] * (CHUNK - 1.0 - pos))
    g_chunk = jnp.exp(log_gamma * CHUNK)

    def step(R, inp):
        qj, kj, vj = inp
        s = jnp.einsum('bhld,bhsd->bhls', qj, kj) * Dmat
        o = (jnp.einsum('bhls,bhsv->bhlv', s, vj)
             + xi[..., None] * jnp.einsum('bhlk,bhkv->bhlv', qj, R))
        R_new = g_chunk[:, None, None] * R + jnp.einsum('bhsk,bhsv->bhkv', kj * zeta[..., None], vj)
        return R_new, o.astype(q.dtype)

    init = jnp.zeros((B, H, d, d), jnp.float32)
    _, os_ = lax.scan(step, init, (to_chunks(q), to_chunks(k), to_chunks(v)))
    return from_chunks(os_)

def second_inputs(seed: int = 0) -> dict:
    key = jax.random.key(seed)
    ks = jax.random.split(key, 16)
    f32 = jnp.float32
    x = jax.random.normal(ks[0], (BATCH, SEQ, D_MODEL), f32)
    c = jax.random.normal(ks[1], (BATCH, D_MODEL), f32)
    offset = jax.random.randint(ks[2], (BATCH, 1), 0, 4096, dtype=jnp.int32)
    positions = offset + jnp.arange(SEQ, dtype=jnp.int32)[None, :]
    w_ada = jax.random.normal(ks[3], (DEPTH, D_MODEL, 3 * D_MODEL), f32) * (0.5 * D_MODEL ** -0.5)
    b_ada = jax.random.normal(ks[4], (DEPTH, 3 * D_MODEL), f32) * 0.02
    norm_g = 1.0 + 0.02 * jax.random.normal(ks[5], (DEPTH, D_MODEL), f32)
    w_in = jax.random.normal(ks[6], (DEPTH, D_MODEL, D_IN_PROJ), f32) * (D_MODEL ** -0.5)
    conv_w = jax.random.normal(ks[7], (DEPTH, CONV_K, 2 * D_MLSTM), f32) * (CONV_K ** -0.5)
    conv_b = jax.random.normal(ks[8], (DEPTH, 2 * D_MLSTM), f32) * 0.02
    b_igate = jax.random.normal(ks[9], (DEPTH, N_HEADS_MLSTM), f32) * 0.1
    b_fgate = (jnp.linspace(3.0, 6.0, N_HEADS_MLSTM, dtype=f32)[None, :]
               + 0.1 * jax.random.normal(ks[10], (DEPTH, N_HEADS_MLSTM), f32))
    gn_m = 1.0 + 0.02 * jax.random.normal(ks[11], (DEPTH, D_MLSTM), f32)
    gn_r = 1.0 + 0.02 * jax.random.normal(ks[12], (DEPTH, D_RET), f32)
    w_out = jax.random.normal(ks[13], (DEPTH, D_INNER, D_MODEL), f32) * (D_INNER ** -0.5)
    final_g = 1.0 + 0.02 * jax.random.normal(ks[14], (D_MODEL,), f32)
    return {'x': x, 'c': c, 'positions': positions, 'w_ada': w_ada, 'b_ada': b_ada,
            'norm_g': norm_g, 'w_in': w_in, 'conv_w': conv_w, 'conv_b': conv_b,
            'b_igate': b_igate, 'b_fgate': b_fgate, 'gn_m': gn_m, 'gn_r': gn_r,
            'w_out': w_out, 'final_g': final_g}

def second_block(x, c, positions, w_ada, b_ada, norm_g, w_in, conv_w, conv_b,
              b_igate, b_fgate, gn_m, gn_r, w_out, final_g):
    B, S, _ = x.shape
    c_act = jax.nn.silu(c)
    for l in range(DEPTH):
        ada = c_act @ w_ada[l] + b_ada[l]
        shift, scale, gate = jnp.split(ada, 3, axis=-1)
        h = rmsnorm(x, norm_g[l]) * (1.0 + scale[:, None, :]) + shift[:, None, :]
        p = h @ w_in[l]
        mq, mk, mv, mo, mz, mi, mf, rq, rk, rv, rz = split_cols_2(p)

        qk = jax.nn.silu(causal_dwconv(jnp.concatenate([mq, mk], axis=-1), conv_w[l], conv_b[l]))
        mq_c, mk_c = jnp.split(qk, 2, axis=-1)
        cell = mlstm_chunkwise(mq_c.reshape(B, S, N_HEADS_MLSTM, HD_M),
                               mk_c.reshape(B, S, N_HEADS_MLSTM, HD_M),
                               mv.reshape(B, S, N_HEADS_MLSTM, HD_M),
                               mi + b_igate[l], mf + b_fgate[l])
        y_m = jax.nn.sigmoid(mo) * head_layernorm(cell, gn_m[l], N_HEADS_MLSTM) * jax.nn.silu(mz)

        rq_h = rotary(rq.reshape(B, S, N_HEADS_RET, HD_R), positions)
        rk_h = rotary(rk.reshape(B, S, N_HEADS_RET, HD_R), positions)
        ret = retention_chunkwise(rq_h, rk_h, rv.reshape(B, S, N_HEADS_RET, HD_R))
        y_r = head_layernorm(ret, gn_r[l], N_HEADS_RET) * jax.nn.silu(rz)

        y = jnp.concatenate([y_m, y_r], axis=-1) @ w_out[l]
        x = x + gate[:, None, :] * y
    return rmsnorm(x, final_g)


def setup_inputs(seed=0):
    out = dict(first_inputs(seed))
    for name, value in second_inputs(seed + 1).items():
        if name != "x":
            out[name + "_2"] = value
    return out


def reference(
    x, c, ctx, c_ctx, norm_g, w_mod, b_mod, w_in, b_in, conv_dw_w, conv_dw_b, conv_ln_g,
    conv_ln_b, w_conv_out, gla_w_gate, gla_b_gate, gla_norm_g, w_gla_out, q_norm_g, k_norm_g,
    w_attn_out, w_out, c_2, positions_2, w_ada_2, b_ada_2, norm_g_2, w_in_2, conv_w_2, conv_b_2,
    b_igate_2, b_fgate_2, gn_m_2, gn_r_2, w_out_2, final_g_2,
):
    x = first_block(
        x, c, ctx, c_ctx, norm_g, w_mod, b_mod, w_in, b_in, conv_dw_w, conv_dw_b, conv_ln_g,
        conv_ln_b, w_conv_out, gla_w_gate, gla_b_gate, gla_norm_g, w_gla_out, q_norm_g,
        k_norm_g, w_attn_out, w_out,
    )
    return second_block(
        x, c_2, positions_2, w_ada_2, b_ada_2, norm_g_2, w_in_2, conv_w_2, conv_b_2, b_igate_2,
        b_fgate_2, gn_m_2, gn_r_2, w_out_2, final_g_2,
    )


_drawn_inputs = setup_inputs


def setup_inputs(seed=0):
    import zlib

    import numpy as np

    out = dict(_drawn_inputs(seed))
    spreads = {}
    factors = {'c_ctx': 2.73,
     'norm_g': 8.0,
     'b_mod': 6.256,
     'b_in': 8.0,
     'conv_dw_b': 8.0,
     'conv_ln_g': 8.0,
     'conv_ln_b': 8.0,
     'gla_b_gate': 7.698,
     'gla_norm_g': 8.0,
     'q_norm_g': 8.0,
     'k_norm_g': 8.0,
     'norm_g_2': 6.852,
     'conv_b_2': 190.577,
     'b_igate_2': 64.0,
     'gn_m_2': 60.093,
     'gn_r_2': 38.239,
     'final_g_2': 22.253}
    for name, (base, spread) in spreads.items():
        noise = np.random.default_rng([zlib.crc32(name.encode()), seed]).standard_normal(out[name].shape)
        drawn = base * np.exp(spread * noise) if base else spread * noise
        out[name] = jnp.asarray(drawn.astype(out[name].dtype))
    for name, factor in factors.items():
        out[name] = (out[name] * factor).astype(out[name].dtype)
    return out
```

```python
from contextlib import ExitStack

import numpy as np

import concourse.bass as bass
from concourse import mybir

F32 = mybir.dt.float32
I32 = mybir.dt.int32
ALU = mybir.AluOpType
ACT = mybir.ActivationFunctionType
AX = mybir.AxisListType

P = 128
D = 1024
KD = D // P
TC, TX = 256, 512
T = TC + TX
DEPTH = 2
EPS = 1e-6
HALF_PI = float(np.pi / 2)

C_VAL, C_GLU, C_CGATE, C_GQ, C_GK, C_GV, C_GG, C_LR, C_AQ, C_AK, C_AV, C_AG, C_M = (
    0, 512, 1024, 1536, 1792, 2048, 2560, 3072, 3104, 3616, 3744, 3872, 4384)
TAPS, PAD = 31, 15
GLA_CHUNK = 64
RANK = 16
C_MI, C_RQ = 5120, 5128
HEADS2, HD2, TAPS2 = 4, 256, 4
CH = 128
NCH = TX // CH

K_ID, K_HALF, K_ONE, K_PERM, K_CAUS, K_ANTI, K_NEG, K_DEC, K_XI, K_ZETA, K_GCH, K_FREQ, K_SEL, K_END = np.cumsum(
    [0, 128, 128, 128, 128, 128, 128, 128, 512, 4, 4, 4, 1, 512]).tolist()


def shape_constants():
    c = np.zeros((P, K_END), np.float32)
    i = np.arange(P)
    c[:, K_ID:K_ID + P] = np.eye(P)
    c[:, K_HALF:K_HALF + P] = (i[:, None] // 64 == i[None] // 64) / 64.0
    c[:, K_ONE:K_ONE + P] = 1.0
    for p in range(P):
        if p % 32 < 16:
            c[p + 16, K_PERM + p] = -1.0
        else:
            c[p - 16, K_PERM + p] = 1.0
    same = i[:, None] // GLA_CHUNK == i[None] // GLA_CHUNK
    c[:, K_CAUS:K_CAUS + P] = same & (i[:, None] <= i[None])
    c[:, K_ANTI:K_ANTI + P] = same & (i[:, None] >= i[None])
    c[:, K_NEG:K_NEG + P] = np.where(i[:, None] <= i[None], 0.0, -1e30)
    lg = np.log(1.0 - 2.0 ** (-5.0 - np.arange(HEADS2)))
    for h in range(HEADS2):
        d = i[None] - i[:, None]
        c[:, K_DEC + h * P:K_DEC + (h + 1) * P] = np.where(d >= 0, np.exp(lg[h] * np.maximum(d, 0)), 0.0)
        c[:, K_XI + h] = np.exp(lg[h] * (i + 1.0))
        c[:, K_ZETA + h] = np.exp(lg[h] * (CH - 1.0 - i)) / 16.0
        c[:, K_GCH + h] = np.exp(lg[h] * CH)
        c[h, K_SEL + h * P:K_SEL + (h + 1) * P] = 1.0
    c[:, K_FREQ] = (1.0 / (np.float32(10000.0) ** np.linspace(0.0, 1.0, P, dtype=np.float32))).astype(np.float32)
    m = np.ones((P, T), np.float32)
    m[:, ::GLA_CHUNK] = 0.0
    t = np.arange(TX)
    f = (np.float32(10000.0) ** (-np.arange(16, dtype=np.float32) / 16)).astype(np.float32)
    pos = np.where((i[:, None] % 64) < 32, t[None] // 64, t[None] % 64).astype(np.float32)
    ang = pos * f[i % 16][:, None]
    rope = np.stack([np.cos(ang), np.sin(ang)], 1).astype(np.float32)
    m2 = np.ones((P, TX), np.float32)
    m2[:, ::CH] = 0.0
    return c, m, rope, m2


def steps2():
    def proj(n):
        yield [("load", n, 0), ("qk", n, 0)]
        yield [("qk", n, 1)]
        yield [("load", n, 1), ("qk", n, 2)]
        yield [("qk", n, 3)]
        yield [("load", n, 2), ("v", n, 0), ("v", n, 1)]
        yield [("v", n, 2), ("v", n, 3)]
        for b in range(1 if n // 4 else 2):
            yield [("load", n, 3 + b), ("gate", n, b, 0)]
            yield [("gate", n, b, 1)]

    def core(n):
        for c in range(NCH):
            yield ([("ub", n)] if c == 0 and n < 4 else []) + [("scores", n, c)]
            yield [("values", n, c)]
            yield [("turn", n, c)]

    for s in proj(0):
        yield from s
    yield ("gates", 0)
    for n in range(1, HEADS2 * 2 + 1):
        a = list(proj(n)) if n < HEADS2 * 2 else []
        b = list(core(n - 1))
        for i in range(max(len(a), len(b))):
            for part in (a, b):
                if i < len(part):
                    yield from part[i]


class Counts:

    def __init__(self, nc, ctx, known):
        self.nc, self.ctx, self.known, self.at, self.sems = nc, ctx, known, {}, {}

    def sem(self, name):
        if name not in self.sems:
            self.sems[name] = self.ctx.enter_context(self.nc.semaphore(name))
        return self.sems[name]

    def mark(self, key, name, count):
        assert key not in self.at, key
        self.at[key] = (name, count)

    def reached(self, key):
        if self.known is None:
            return self.sem("draft"), 1
        name, count = self.known[key]
        return self.sem(name), count


class Lane:

    def __init__(self, counts, eng, who):
        self.m, self.eng, self.who, self.name, self.n = counts, eng, who, None, {}

    def stage(self, name):
        self.name = f"{self.who}_{name}"
        self.n.setdefault(self.name, 0)

    def tell(self, key=None):
        self.n[self.name] += 1
        if key is not None:
            self.m.mark(key, self.name, self.n[self.name])
        return self.m.sem(self.name), 1

    def link(self, ins, key=None):
        ins.then_inc(*self.tell(key))
        self.eng.wait_ge(self.m.sem(self.name), self.n[self.name])


def write_program(nc, I, out, known):
    with ExitStack() as ctx:
        def sb(name, shape, dt=F32):
            return ctx.enter_context(nc.sbuf_tensor(name, shape, dt))

        m = Counts(nc, ctx, known)
        at = m.reached

        const = sb("const", [P, K_END])
        xT = sb("xT", [P, KD, T])
        hT = sb("hT", [P, KD, T])
        RING, SLOT = 4, 2048
        wring = sb("wring", [P, RING, SLOT])
        NSET = 7
        cols = sb("cols", [P, NSET, P])
        cT = sb("cT", [P, 24])
        modT = sb("modT", [P, 2, 24, 2])
        posi = sb("posi", [P, TX], I32)
        gsT = sb("gsT", [P, KD, 2])
        rstd = sb("rstd", [P, T])
        rope = sb("rope", [P, 2, TX])
        eps = sb("eps", [P, 1])
        small = sb("small", [P, 96])
        A0, A1, A2 = 12 * T, 13312, 3328
        arena = sb("arena", [P, A0 + A1 + A2])

        def cut(at, *shape):
            n = int(np.prod(shape))
            v = arena[:, at:at + n]
            if len(shape) == 2:
                v = v.rearrange("p (a b) -> p a b", b=shape[1])
            elif len(shape) == 3:
                v = v.rearrange("p (a b c) -> p a b c", b=shape[1], c=shape[2])
            return v, at + n

        res, _ = cut(0, 12, T)
        gq, o = cut(A0, 2, T)
        gk, o = cut(o, 2, T)
        gv, o = cut(o, 6, 512)
        lr, o = cut(o, T)
        bA, o = cut(o, T)
        bC, o = cut(o, T)
        bE, o = cut(o, T)
        bQ, o = cut(o, T)
        bK, o = cut(o, T)
        bS, o = cut(o, T)
        kst, o = cut(o, 6, P)
        ST, o = cut(o, 2, 256)
        AM, o = cut(o, 2, 256)
        assert o <= A0 + A1, o
        bQz = [bQ, rstd[:, :]]
        gup = sb("gup", [P, 256])
        gscan = sb("gscan", [P, T])
        ak, o = cut(A0, 2, T)
        av, o = cut(o, 6, P)
        pr, o = cut(o, 2, T)
        pt, o = cut(o, 2, 6, 512)
        sq, o = cut(o, T)
        rs, o = cut(o, T)
        tmp, o = cut(o, T)
        assert o <= A0 + A1, o
        UW = TC + TX + 4 * PAD
        up, o = cut(A0 + A1, 4, UW)
        UO = {"c": 0, "x": TC + 2 * PAD}
        cg, _ = cut(A0 + A1, 4, T)
        mT, o = cut(A0, KD, T)
        mg, o = cut(o, 6, T)
        my, o = cut(o, 6, T)
        assert o <= A0 + A1 + A2, o
        xin, _ = cut(A0, 6, D)
        rows, _ = cut(0, NSET, P)
        xout, _ = cut(0, 4, D)
        ys, o = cut(0, 16, TX)
        pre, o = cut(o, 4, TX + TAPS2 - 1 + 1)
        qk2, vv = [None] * 2, [None] * 2
        for b in range(2):
            qk2[b], o = cut(o, 4, TX)
            vv[b], o = cut(o, NCH, 260)
        zt, o = cut(o, TX)
        WT, o = cut(o, TX)
        SW, o = cut(o, P)
        NI, o = cut(o, 260)
        NM, o = cut(o, 260)
        HN, o = cut(o, 256)
        KW, o = cut(o, 256)
        C2, o = cut(o, 2, 260)
        UBs, o = cut(o, TX)
        rI, o = cut(o, TX)
        rF, o = cut(o, TX)
        rM, o = cut(o, TX)
        rB, o = cut(o, TX)
        rU, o = cut(o, TX)
        rW, o = cut(o, TX)
        assert o <= A0 + A1 + A2, (o, A0 + A1 + A2)
        qcol = sb("qcol", [P, NCH, 4, 4])
        decc = sb("decc", [P, 4, NCH])

        ps = ctx.enter_context(nc.psum_tensor("ps", [P, 8, 512], F32))
        bank = [ps[:, i, :] for i in range(8)]
        RINGS = {"A": [0, 1], "V": [2, 3]}
        job_no, owner, bank_of = {"A": 0, "V": 0}, {"A": [], "V": []}, {}

        ident = const[:, K_ID:K_ID + P]
        ones = const[:, K_ONE:K_ONE + P]
        block = ctx.enter_context(nc.Block())
        landed = [0] * RING
        starts, plan = [], []
        SEG = {"x": (TC, TX), "c": (0, TC)}

        def segs(l):
            return ["x", "c"] if l < DEPTH - 1 else ["x"]

        def set1(l):
            return [(I["norm_g"][l], 0, 8), (I["b_mod"][l], 8, 24),
                    (I["b_in"][l, 0:C_LR], 32, 24), (I["b_in"][l, C_AQ:C_AK], 56, 4),
                    (I["b_in"][l, C_AG:C_M], 60, 4), (I["b_in"][l, C_M:C_M + 3 * D], 64, 24),
                    (I["conv_dw_b"][l], 88, 4), (I["conv_ln_g"][l], 92, 4), (I["conv_ln_b"][l], 96, 4),
                    (I["gla_b_gate"][l, 0], 100, 2), (I["gla_b_gate"][l, 1], 102, 2),
                    (I["gla_norm_g"][l], 104, 1)]

        def set1h(l):
            b = I["b_in"][l]
            return [(b[C_AK:C_AK + 64], 105), (b[C_AK + 64:C_AK + 128], 106),
                    (I["q_norm_g"][l], 107), (I["k_norm_g"][l], 108)]

        N_G, B_MOD, B_IN, B_AQ, B_AG, B_M, CW_B, LN_G, LN_B, G_B, G_N, B_AK, QN, KN, B_LR = (
            0, 8, 32, 56, 60, 64, 88, 92, 96, 100, 104, 105, 107, 108, 109)

        def set2(l):
            return [(I["norm_g_2"][l], 0, 8), (I["b_ada_2"][l], 8, 24),
                    (I["conv_w_2"][l].rearrange("a b -> (a b)"), 32, 64), (I["conv_b_2"][l], 96, 16),
                    (I["gn_m_2"][l], 112, 8), (I["gn_r_2"][l], 120, 8)]

        def col(s, r):
            return cols[:, s, r:r + 1]

        @block.tensor
        def _(eng):
            pe = Lane(m, eng, "pe")
            pe.stage("start")

            def job(ring, key, mms):
                n = job_no[ring]
                job_no[ring] += 1
                b = RINGS[ring][n % len(RINGS[ring])]
                if n >= len(RINGS[ring]):
                    eng.wait_ge(*at(("free", owner[ring][n - len(RINGS[ring])])))
                owner[ring].append(key)
                bank_of[key] = bank[b]
                mms(bank[b]).then_inc(*pe.tell(("full", key)))

            def weights(view, K, C, parts=None):
                n = len(plan)
                slot = wring[:, n % RING, 0:K * C].rearrange("p (k c) -> p k c", c=C)
                plan.append([parts(slot) if parts else [(slot, view)], None])
                landed[n % RING] += 16 * len(plan[n][0])
                eng.wait_ge(m.sem(f"w_slot{n % RING}"), landed[n % RING])
                return wring[:, n % RING, 0:K * C].rearrange("p (k c) -> p k c", c=C)

            def used(key):
                plan[-1][1] = key

            def wv(t, c0, C):
                return t[:, c0:c0 + C].rearrange("(k p) c -> p k c", p=P)

            def acc(parts):
                def mms(out):
                    for i, (o_, a, b_) in enumerate(parts):
                        last = eng.matmul(o_(out), a, b_, start=(i == 0), stop=(i == len(parts) - 1))
                    return last
                return mms

            def project(key, w, c, src, K, sg, ring="A", M=P):
                t0, n = SEG[sg]
                job(ring, key, acc([(lambda o_: o_[0:M, 0:n], w[:, k, c:c + M], src[:, k, t0:t0 + n])
                                    for k in range(K)]))

            def tiles(name, l, wt, c0, ntile, seg, src=hT, K=KD, ring="A", width=2):
                for j0 in range(0, ntile, width):
                    k = min(width, ntile - j0)
                    w = weights(wv(wt, c0 + j0 * P, k * P), K, k * P)
                    for j in range(k):
                        for sg in seg:
                            project((name, l, j0 + j, sg), w, j * P, src, K, sg, ring)
                    used(("full", (name, l, j0 + k - 1, seg[-1])))

            eng.wait_ge(*at("const in"))
            eng.wait_ge(m.sem("x_in"), 16 * 2)
            for k in range(KD):
                for g, u0, nu in (("x", 2, 4), ("c", 0, 2)):
                    def mms(o_, k=k, u0=u0, nu=nu):
                        for u in range(nu):
                            last = eng.transpose(o_[:, u * P:(u + 1) * P], xin[:, u0 + u, k * P:(k + 1) * P], ident)
                        return last
                    job("A", ("xT", k, g), mms)
            eng.wait_ge(*at("rows in"))
            for s in range(NSET):
                job("A", ("cols", s), lambda o_: eng.transpose(o_[:, 0:P], rows[:, s, :], ident))

            def modulation(key, wt, col0, ncol):
                eng.wait_ge(*at(("cT",)))
                for g in range(12):
                    w = weights(wv(wt, g * 256, 256), KD, 256)
                    for j in range(2):
                        job("A", (key, g, j), acc([(lambda o_: o_[:, 0:ncol], w[:, k, j * P:(j + 1) * P],
                                                    cT[:, col0 + k:col0 + k + 8 * (ncol - 1) + 1:8])
                                                   for k in range(KD)]))
                    used(("full", (key, g, 1)))

            def square_sum(key, l, seg):
                for sg in seg:
                    t0, n = SEG[sg]
                    eng.wait_ge(*at(("squares", l, sg)))
                    job("A", (key, l, sg), acc([(lambda o_: o_[:, 0:n], ones, hT[:, k, t0:t0 + n])
                                                for k in range(KD)]))

            def gla_core(l, p, d):
                pe.stage("gla_core")
                key = (l, p, d)
                for half in range(2):
                    def mms(o_, half=half):
                        for u in range(3):
                            last = eng.transpose(o_[:, u * P:(u + 1) * P],
                                                 bS[:, (half * 3 + u) * P:(half * 3 + u + 1) * P], ident)
                        return last
                    eng.wait_ge(*at(("gla ks", key)))
                    job("A", ("kst", key, half), mms)
                order = [0, 1, 2, 3, 4, 5] if d == 0 else [1, 0, 5, 4, 3, 2]
                steps = [2 * u + c for u in order for c in ((0, 1) if d == 0 else (1, 0))]
                accs = {"x": [bank[4], bank[5]], "c": [bank[6], bank[6]]}
                if d == 0 and (l, p) != (0, 0):
                    eng.wait_ge(*at(("gla out read", l if p else l - 1, 1 - p)))
                def att(u):
                    if u is not None and ("c" if u < 2 else "x") in segs(l):
                        eng.wait_ge(*at(("gla qi", key)))
                        eng.wait_ge(*at(("gla ki", key)))
                        job("V", ("att", key, u), acc_two(key, slice(u * P, u * P + P)))
                att(order[0])
                for ui, u in enumerate(order):
                    sg = "c" if u < 2 else "x"
                    outs = sg in segs(l)
                    col0 = u * P if u < 2 else (u - 2) * P
                    att(order[ui + 1] if ui < 5 else None)
                    if outs:
                        eng.wait_ge(*at(("att masked", key, u)))
                        eng.wait_ge(*at(("gla v", l)))
                        for hh in range(2):
                            h = 2 * p + hh
                            c1 = col0 + (hh * 256 if sg == "c" else 0)
                            first = d == 0 and ((sg == "x" and u == 2) or (sg == "c" and u == 0 and hh == 0))
                            last = eng.matmul(accs[sg][hh][:, c1:c1 + P], gv[:, u, h * P:(h + 1) * P],
                                              AM[:, ui % 2, hh * P:(hh + 1) * P], start=first, stop=False,
                                              skip_group_check=True)
                        last.then_inc(*pe.tell(("att used", key, u)))
                    for c in ((0, 1) if d == 0 else (1, 0)):
                        ch = 2 * u + c
                        si = steps.index(ch)
                        if outs and si > 0:
                            eng.wait_ge(*at(("state", key, si)))
                            for hh in range(2):
                                c1 = col0 + c * 64 + (hh * 256 if sg == "c" else 0)
                                last = eng.matmul(accs[sg][hh][:, c1:c1 + 64],
                                                  ST[:, si % 2, hh * P:(hh + 1) * P],
                                                  bQz[hh][:, ch * 64:ch * 64 + 64],
                                                  start=False, skip_group_check=True,
                                                  stop=d == 1 and c == 0 and (u == 2 or (u == 0 and hh == 1)))
                        if outs:
                            if si == 0:
                                m.mark(("state used", key, si), *m.at[("att used", key, u)])
                            else:
                                last.then_inc(*pe.tell(("state used", key, si)))
                        if si < 11:
                            eng.wait_ge(*at(("kst", key, 1)))
                            eng.wait_ge(*at(("gla v", l)))
                            job("V", ("con", key, si),
                                lambda o_: eng.matmul(o_[:, 0:256], kst[c * 64:c * 64 + 64, u, :],
                                                      gv[c * 64:c * 64 + 64, u, p * 256:p * 256 + 256],
                                                      start=True, stop=True))
                            if not outs:
                                m.mark(("state used", key, si), *m.at[("full", ("con", key, si))])
                m.mark(("gla core", key), *m.at[("state used", key, 11)])

            def acc_two(key, tk):
                def mms(o_):
                    for hh in range(2):
                        last = eng.matmul(o_[:, hh * P:(hh + 1) * P], bK[:, tk], bQz[hh][:, tk], start=True, stop=True)
                    return last
                return mms

            def gla_gate(l, p, d):
                pe.stage("gla_gate")
                for sg in ("x", "c"):
                    t0, n = SEG[sg]
                    eng.wait_ge(*at(("gup", l)))
                    eng.wait_ge(*at(("lr", l, "c", 1)))
                    job("A", ("z", (l, p, d), sg),
                        lambda o_: eng.matmul(o_[:, 0:n], gup[32 * d:32 * d + RANK, p * P:(p + 1) * P],
                                              lr[32 * d:32 * d + RANK, t0:t0 + n], start=True, stop=True))

            def gla_out_norm(l, p):
                pe.stage("gla_norm")
                for hh in range(2):
                    for sg in segs(l):
                        t0, n = SEG[sg]
                        eng.wait_ge(*at(("gla sq", l, 2 * p + hh)))
                        job("A", ("gss", l, 2 * p + hh, sg),
                            lambda o_: eng.matmul(o_[:, 0:n], ones, bC[:, t0:t0 + n], start=True, stop=True))

            def attend(l, sg):
                pe.stage("attend")
                nq, nkt = (4, 6) if sg == "x" else (2, 2)
                q0 = SEG[sg][0]
                keys = nkt * P
                cnt = [0]

                def scores(h, qb):
                    i = att_no[0]
                    att_no[0] += 1
                    g = h // 4
                    r = slice((h % 2) * 64, (h % 2) * 64 + 64)
                    b0 = 4 + 2 * (i % 2)
                    if i >= 2:
                        eng.wait_ge(*at(("probs", i - 2)))
                    eng.wait_ge(*at(("q ready", l, h // 2, sg)))
                    eng.wait_ge(*at(("k ready", l, g)))
                    w = 384 if sg == "x" else 256
                    for half in range(keys // w):
                        last = eng.matmul(bank[b0 + half][:, 0:w], res[r, 8 + h // 2, q0 + qb * P:q0 + qb * P + P],
                                          ak[r, g, half * w:(half + 1) * w], start=True, stop=True)
                    last.then_inc(*pe.tell(("scores", i)))
                    return i

                def turn(h, qb, i):
                    for half in range(2 if sg == "x" else 1):
                        nb = 3 if sg == "x" else 2

                        def mms(o_, half=half):
                            for u in range(nb):
                                kt = half * nb + u
                                last = eng.transpose(o_[:, u * P:(u + 1) * P], pr[:, i % 2, kt * P:(kt + 1) * P], ident)
                            return last
                        eng.wait_ge(*at(("probs norm", i)))
                        job("V", ("pT", i, half), mms)

                def values(h, hn):
                    g = h // 4
                    r0 = (h % 2) * 64

                    def mms(o_):
                        for kt in range(nkt):
                            last = eng.matmul(o_[r0:r0 + 64, 0:nq * P], av[:, kt, g * 64:(g + 1) * 64],
                                              pt[:, hn % 2, kt, 0:nq * P], start=(kt == 0), stop=(kt == nkt - 1))
                        return last
                    eng.wait_ge(*at(("pt", l, h, sg)))
                    eng.wait_ge(*at(("av", l)))
                    job("A", ("o", l, h, sg), mms)

                seq = [(h, qb) for h in range(8) for qb in range(nq)]
                ids = {}
                for n_, (h, qb) in enumerate(seq):
                    ids[n_] = scores(h, qb)
                    if n_ >= 1:
                        hp, qp = seq[n_ - 1]
                        turn(hp, qp, ids[n_ - 1])
                        if qp == nq - 1:
                            values(hp, head_no[0])
                            head_no[0] += 1
                hp, qp = seq[-1]
                turn(hp, qp, ids[len(seq) - 1])
                values(hp, head_no[0])
                head_no[0] += 1

            att_no, head_no = [0], [0]

            for l in range(DEPTH):
                starts.append(len(plan))
                pe.stage("proj1")
                modulation(("mod", l), I["w_mod"][l], 0, 2)
                square_sum("ss", l, ["x", "c"])
                eng.wait_ge(*at(("h ready", l, "x")))
                eng.wait_ge(*at(("h ready", l, "c")))
                both = ["x", "c"]
                wi = I["w_in"][l]
                w = weights(wv(wi, C_LR, 32), KD, 32)
                for sg in both:
                    for d in range(2):
                        t0, n = SEG[sg]
                        job("A", ("lr", l, sg, d), acc([(lambda o_: o_[32 * d:32 * d + RANK, 0:n],
                                                         w[:, k, d * RANK:(d + 1) * RANK], hT[:, k, t0:t0 + n])
                                                        for k in range(KD)]))
                used(("full", ("lr", l, "c", 1)))
                gla_gate(l, 0, 0)
                pe.stage("proj1")
                tiles("gq", l, wi, C_GQ, 2, segs(l))
                tiles("gk", l, wi, C_GK, 2, both)

                def value_rows(name, c0, width, row, bc):
                    eng.wait_ge(*at("vrow in"))
                    for g0 in range(0, width, 256):
                        cw = min(256, width - g0)
                        w = weights(wv(wi, c0 + g0, cw), KD, cw)
                        for u in range(6):
                            job("A", (name, l, g0 // 256, u), acc(
                                [(lambda o_: o_[:, 0:cw], hT[:, k, u * P:(u + 1) * P], w[:, k, :]) for k in range(KD)]
                                + [(lambda o_: o_[:, 0:cw], ones[row:row + 1, :], const[row:row + 1, K_SEL + bc + g0:K_SEL + bc + g0 + cw])]))
                        used(("full", (name, l, g0 // 256, 5)))
                value_rows("gv", C_GV, 512, 32 * (l + 1), 0)
                tiles("gg", l, wi, C_GG, 4, segs(l))
                gla_core(l, 0, 0)
                gla_gate(l, 0, 1)
                pe.stage("proj1")
                tiles("val", l, wi, C_VAL, 4, segs(l))
                gla_core(l, 0, 1)
                pe.stage("proj1")
                tiles("glu", l, wi, C_GLU, 4, segs(l))
                gla_out_norm(l, 0)
                gla_gate(l, 1, 0)
                pe.stage("proj1")
                tiles("aq", l, wi, C_AQ, 4, segs(l))
                gla_core(l, 1, 0)
                gla_gate(l, 1, 1)
                pe.stage("proj1")
                gla_core(l, 1, 1)
                gla_out_norm(l, 1)
                pe.stage("attn_proj")
                def twice(slot):
                    out_ = []
                    for g in range(2):
                        for hf in range(2):
                            c1 = g * P + hf * 64
                            out_.append((slot[:, :, c1:c1 + 64], wv(wi, C_AK + g * 64, 64)))
                    return out_
                w = weights(None, KD, 256, twice)
                for g in range(2):
                    for sg in both:
                        t0, n = SEG[sg]
                        job("A", ("ak", l, g, sg), acc(
                            [(lambda o_: o_[:, 0:n],
                              w[:, k, g * P:(g + 1) * P],
                              hT[:, k, t0:t0 + n]) for k in range(KD)]))
                used(("full", ("ak", l, 1, "c")))
                value_rows("av", C_AV, 128, 96, l * P)
                for j, name in ((0, "k"), (1, "k"), (0, "q"), (1, "q"), (2, "q"), (3, "q")):
                    for sg in (both if name == "k" else segs(l)):
                        t0, n = SEG[sg]
                        eng.wait_ge(*at(("hsq", l, name, j)))
                        job("A", ("hss", l, name, j, sg),
                            lambda o_: eng.matmul(o_[:, 0:n], const[:, K_HALF:K_HALF + P], sq[:, t0:t0 + n],
                                                  start=True, stop=True))
                    src = ak[:, j, TC:T] if name == "k" else res[:, 8 + j, TC:T]
                    eng.wait_ge(*at(("normed", l, name, j)))
                    job("V", ("rot", l, name, j),
                        lambda o_: eng.matmul(o_[:, 0:TX], const[:, K_PERM:K_PERM + P], src, start=True, stop=True))
                if l < DEPTH - 1:
                    attend(l, "c")
                attend(l, "x")
                pe.stage("conv_ln")
                for sg in segs(l):
                    t0, n = SEG[sg]
                    eng.wait_ge(*at(("conv", l)))
                    job("A", ("csum", l, sg), acc([(lambda o_: o_[:, 0:n], ones, res[:, j, t0:t0 + n])
                                                   for j in range(4)]))
                for sg in segs(l):
                    t0, n = SEG[sg]
                    eng.wait_ge(*at(("conv squares", l, sg)))
                    job("A", ("csq", l, sg), acc([(lambda o_: o_[:, 0:n], ones, mg[:, j, t0:t0 + n])
                                                  for j in range(4)]))
                pe.stage("merge")
                tiles("ag", l, wi, C_AG, 4, segs(l))
                tiles("cgate", l, wi, C_CGATE, 4, segs(l))
                for a in range(4):
                    for b_ in range(3):
                        w = weights(wv(wi, C_M + b_ * D + a * 256, 256), KD, 256)
                        for j in range(2):
                            for sg in segs(l):
                                project(("mgate", l, a, b_, j, sg), w, j * P, hT, KD, sg)
                        used(("full", ("mgate", l, a, b_, 1, segs(l)[-1])))
                    for b_, nm in enumerate(("w_conv_out", "w_gla_out", "w_attn_out")):
                        if a == 0:
                            eng.wait_ge(*at(("branch", l, b_)))
                        w = weights(wv(I[nm][l], a * 256, 256), 4, 256)
                        for j in range(2):
                            for sg in segs(l):
                                project(("mout", l, a, b_, j, sg), w, j * P, res[:, 4 * b_:4 * b_ + 4, :], 4, sg)
                        used(("full", ("mout", l, a, b_, 1, segs(l)[-1])))
                eng.wait_ge(*at(("merged", l, KD - 1)))
                tiles("y", l, I["w_out"][l], 0, 8, segs(l), src=mT, ring="V")

            for l in range(DEPTH):
                L = 2 + l
                starts.append(len(plan))
                wi = I["w_in_2"][l]
                pe.stage("proj2")
                modulation(("mod", L), I["w_ada_2"][l], 16, 1)
                square_sum("ss", L, ["x"])
                eng.wait_ge(*at(("h ready", L, "x")))
                w = weights(wv(wi, C_MI, 8), KD, 8)
                for g in range(2):
                    job("A", ("if", l, g), acc([(lambda o_: o_[0:4, 0:TX], w[:, k, 4 * g:4 * g + 4],
                                                 hT[:, k, TC:T]) for k in range(KD)]))
                used(("full", ("if", l, 1)))

                def gate_cols():
                    def mms(o_):
                        for c in range(NCH):
                            for q_, r_ in enumerate((rI, rM, rF, rW)):
                                o4 = (c * 4 + q_) * 4
                                last = eng.transpose(o_[:, o4:o4 + 4], r_[0:4, c * P:(c + 1) * P], ident[0:4, 0:4])
                        return last
                    eng.wait_ge(*at(("gate rows", l)))
                    job("A", ("gcols", l), mms)

                    def mms2(o_):
                        for h in range(4):
                            last = eng.matmul(o_[:, h * NCH:(h + 1) * NCH], const[0:4, K_SEL + h * P:K_SEL + (h + 1) * P],
                                              rI[0:4, P - 1:TX:P], start=True, stop=True)
                        return last
                    job("A", ("decay", l), mms2)

                w2 = None
                for kind, n, *x in steps2():
                    h, r, b = n % 4, n // 4, n % 2
                    base = C_RQ if r else 0
                    q, v = qk2[b], vv[b]
                    if kind == "gates":
                        gate_cols()
                    elif kind == "load":
                        w2 = weights(wv(wi, base + x[0] * D + h * HD2, HD2), KD, HD2)
                    elif kind == "qk":
                        project(("qk", l, n, x[0]), w2, (x[0] % 2) * P, hT, KD, "x")
                        used(("full", ("qk", l, n, x[0])))
                    elif kind == "v":
                        u = x[0]
                        job("A", ("v2", l, n, u), acc([(lambda o_: o_[:, 0:HD2], hT[:, k, TC + u * P:TC + (u + 1) * P],
                                                        w2[:, k, :]) for k in range(KD)]))
                        used(("full", ("v2", l, n, u)))
                    elif kind == "gate":
                        project(("gate2", l, n, x[0], x[1]), w2, x[1] * P, hT, KD, "x")
                        used(("full", ("gate2", l, n, x[0], x[1])))
                    elif kind == "ub":
                        eng.wait_ge(*at(("gate rows", l)))
                        job("V", ("ub", l, n), lambda o_: eng.matmul(o_[:, 0:TX], const[0:4, K_SEL + h * P:K_SEL + (h + 1) * P],
                                                                     rU[0:4, :], start=True, stop=True))
                    else:
                        c = x[0]
                        k = (l, n, c)
                        ts = slice(c * P, (c + 1) * P)
                        W = HD2 if r else HD2 + 1
                        if kind == "scores":
                            eng.wait_ge(*at(("qk ready", l, n)))
                            job("V", ("s2", k), acc([(lambda o_: o_[:, 0:P], q[:, 2 + j, ts], q[:, j, ts]) for j in range(2)]))
                            if c < NCH - 1:
                                def mms(o_):
                                    for j in range(2):
                                        last = eng.transpose(o_[:, j * P:(j + 1) * P], q[:, 2 + j, ts], ident)
                                    return last
                                eng.wait_ge(*at(("qk ready", l, n)))
                                job("A", ("kT", k), mms)
                        elif kind == "values":
                            eng.wait_ge(*at(("sw", k)))
                            eng.wait_ge(*at(("v2 ready", l, n)))
                            job("A", ("intra", k), lambda o_: eng.matmul(o_[:, 0:W], SW[:, :], v[:, c, 0:W], start=True, stop=True))
                            if c > 0:
                                eng.wait_ge(*at(("C", (l, n, c - 1), 1)))
                                job("V", ("inter", k), acc([(lambda o_: o_[:, 0:W], q[:, j, ts], C2[:, j, 0:W])
                                                            for j in range(2)]))
                            if c < NCH - 1:
                                for j in range(2):
                                    eng.wait_ge(*at(("kw", k)))
                                    eng.wait_ge(*at(("v2 ready", l, n)))
                                    job("V", ("dC", k, j), lambda o_: eng.matmul(o_[:, 0:W], KW[:, j * P:(j + 1) * P], v[:, c, 0:W],
                                                                                 start=True, stop=True))
                        elif kind == "turn":
                            def mms3(o_):
                                for j in range(2):
                                    last = eng.transpose(o_[:, j * P:(j + 1) * P], HN[:, j * P:(j + 1) * P], ident)
                                return last
                            eng.wait_ge(*at(("hn", k)))
                            job("V", ("hT", k), mms3)
                pe.stage("out2")
                for j in range(KD):
                    w = weights(wv(I["w_out_2"][l], j * P, P), 16, P)
                    eng.wait_ge(*at(("ys", l)))
                    job("V", ("y", L, j, "x"), acc([(lambda o_: o_[:, 0:TX], w[:, k, :], ys[:, k, :])
                                                    for k in range(16)]))
                    used(("full", ("y", L, j, "x")))

            pe.stage("end")
            square_sum("ss", 4, ["x"])
            for u in range(4):
                for half in range(2):
                    def mms(o_, u=u, half=half):
                        for k in range(4):
                            last = eng.transpose(o_[:, k * P:(k + 1) * P],
                                                 hT[:, half * 4 + k, TC + u * P:TC + (u + 1) * P], ident)
                        return last
                    eng.wait_ge(*at(("h ready", 4, "x")))
                    job("A", ("final", u, half), mms)


        @block.scalar
        def _(eng):
            act = Lane(m, eng, "act")
            act.stage("start")

            def fn(out_, in_, func, key=None, **kw):
                act.link(eng.activation(out_, in_, func, **kw), key)

            def evac(key, out_, lo, n, func=ACT.Copy, rows_=slice(0, P), **kw):
                eng.wait_ge(*at(("full", key)))
                fn(out_, bank_of[key][rows_, lo:lo + n], func, ("free", key), **kw)

            for k in range(KD):
                for g in ("x", "c"):
                    t0, n = SEG[g]
                    evac(("xT", k, g), xT[:, k, t0:t0 + n], 0, n)
            for s in range(NSET):
                evac(("cols", s), cols[:, s, :], 0, P)
            fn(cT[:, :], cols[:, 6, 8:32], ACT.Silu, ("cT",))

            def head_of_layer(L, ncol):
                act.stage("norm")
                s = L if L < 2 else L + 2
                for g in range(12):
                    for j in range(2):
                        f = 2 * g + j
                        evac((("mod", L), g, j), modT[:, L % 2, f, 0:ncol], 0, ncol, ACT.Identity,
                             bias=col(s, B_MOD + f))
                for c_, sg in list(enumerate(("x", "c")))[:2 if L < 2 else 1]:
                    t0, n = SEG[sg]
                    evac(("ss", L, sg), rstd[:, t0:t0 + n], 0, n, ACT.Sqrt, scale=1.0 / D, bias=eps[:, :])
                for c_, sg in list(enumerate(("x", "c")))[:2 if L < 2 else 1]:
                    t0, n = SEG[sg]
                    for k in range(KD):
                        eng.wait_ge(*at(("h scaled", L, sg, k)))
                        fn(hT[:, k, t0:t0 + n], hT[:, k, t0:t0 + n], ACT.Identity,
                           ("h ready", L, sg) if k == KD - 1 else None, bias=modT[:, L % 2, k, c_:c_ + 1])

            def tiles(name, l, dst, ntile, seg, func=ACT.Identity, b0=None, off=None):
                for j in range(ntile):
                    for sg in seg:
                        t0, n = SEG[sg]
                        t1 = off[sg] + PAD if off else t0
                        kw = {"bias": col(l, b0 + j)} if b0 is not None else {}
                        evac((name, l, j, sg), dst[:, j, t1:t1 + n], 0, n, func, **kw)

            def gate_first(l, p, d):
                act.stage("gla_gate")
                prev = (l, p, d)
                i = l * 4 + p * 2 + d
                if i:
                    q = i - 1
                    eng.wait_ge(*at(("gla ks", (q // 4, q // 2 % 2, q % 2))))
                if d == 0 and i:
                    eng.wait_ge(*at(("gla out done", (i - 1) // 4, (i - 1) // 2 % 2)))
                for sg in ("x", "c"):
                    t0, n = SEG[sg]
                    evac(("z", prev, sg), bA[:, t0:t0 + n], 0, n, ACT.Identity, bias=col(l, G_B + 2 * d + p))
                fn(bE, bA, ACT.Abs)
                fn(bE, bE, ACT.Exp, scale=-1.0)
                fn(bE, bE, ACT.Ln, ("gla ln", prev), bias=1.0)

            def gate_second(l, p, d):
                act.stage("gla_gate")
                key = (l, p, d)
                eng.wait_ge(*at(("gla cum", key)))
                fn(bE, bC, ACT.Exp, ("gla e", key), scale=1.0 / 16)
                fn(bK, bC, ACT.Exp, ("gla ek", key), scale=-1.0 / 16)
                fn(bS, bS, ACT.Exp, ("gla es", key), scale=1.0 / 16)
                end = bC[:, 63:T:64] if d == 0 else bC[:, 0:T:64]
                fn(small[:, 0:12], end, ACT.Exp, ("gla dec", key), scale=1.0 / 16)

            def kstate(l, p, d):
                act.stage("gla_core")
                key = (l, p, d)
                for half in range(2):
                    evac(("kst", key, half), kst[:, half * 3:half * 3 + 3, :], 0, 384)
                    m.mark(("kst", key, half), *m.at[("free", ("kst", key, half))])

            def out_norm(l, p):
                act.stage("gla_norm")
                for hh, buf in ((0, bA), (1, bK)):
                    eng.wait_ge(*at(("gla core", (l, p, 1))))
                    for sg in segs(l):
                        t0, n = SEG[sg]
                        src = ps[:, 4 + hh, 0:512] if sg == "x" else ps[:, 6, hh * 256:hh * 256 + 256]
                        fn(buf[:, t0:t0 + n], src, ACT.Copy)
                    m.mark(("gla o", l, 2 * p + hh), act.name, act.n[act.name])
                m.mark(("gla out read", l, p), act.name, act.n[act.name])
                for hh in range(2):
                    for sg in segs(l):
                        t0, n = SEG[sg]
                        evac(("gss", l, 2 * p + hh, sg), bE[:, t0:t0 + n], 0, n, ACT.Sqrt, scale=1.0 / P, bias=eps[:, :])

            att_no = [0]

            def attend(l, sg):
                act.stage("attend")
                nq, nkt = (4, 6) if sg == "x" else (2, 2)
                q0 = SEG[sg][0]
                n_all = 8 * nq
                for n_ in range(n_all + 1):
                    if n_ < n_all:
                        i = att_no[0] + n_
                        eng.wait_ge(*at(("nmax", i)))
                        if i >= 2:
                            eng.wait_ge(*at(("pT read", i - 2)))
                        b0 = 4 + 2 * (i % 2)
                        if sg == "x":
                            src = ps[:, b0:b0 + 2, 0:384]
                            dst = pr[:, i % 2, :].rearrange("p (a b) -> p a b", b=384)
                        else:
                            src, dst = ps[:, b0, 0:256], pr[:, i % 2, 0:256]
                        fn(dst, src, ACT.Exp, ("probs", i), bias=small[:, 40 + i % 2:41 + i % 2],
                           accum_out=small[:, 44 + i % 2:45 + i % 2])
                    if n_ >= 1 and (n_ - 1) % nq == nq - 1:
                        h = (n_ - 1) // nq
                        r = slice((h % 2) * 64, (h % 2) * 64 + 64)
                        evac(("o", l, h, sg), res[r, 8 + h // 2, q0:q0 + nq * P], 0, nq * P, rows_=r)
                att_no[0] += n_all

            for l in range(DEPTH):
                head_of_layer(l, 2)
                both = ["x", "c"]
                act.stage("proj1")
                for sg in both:
                    for d in range(2):
                        t0, n = SEG[sg]
                        r = slice(32 * d, 32 * d + RANK)
                        evac(("lr", l, sg, d), lr[r, t0:t0 + n], 0, n, ACT.Identity, rows_=r, bias=cols[r, l, B_LR:B_LR + 1])
                        m.mark(("lr", l, sg, d), *m.at[("free", ("lr", l, sg, d))])
                gate_first(l, 0, 0)
                act.stage("proj1")
                tiles("gq", l, gq, 2, segs(l), b0=B_IN + C_GQ // P)
                tiles("gk", l, gk, 2, both, b0=B_IN + C_GK // P)
                gate_second(l, 0, 0)
                act.stage("proj1")
                for g in range(2):
                    for u in range(6):
                        evac(("gv", l, g, u), gv[:, u, g * 256:(g + 1) * 256], 0, 256)
                m.mark(("gla v", l), *m.at[("free", ("gv", l, 1, 5))])
                tiles("gg", l, res[:, 4:8, :], 4, segs(l), ACT.Silu, B_IN + C_GG // P)
                kstate(l, 0, 0)
                gate_first(l, 0, 1)
                act.stage("proj1")
                eng.wait_ge(*at(("up zero", l)))
                tiles("val", l, up, 4, segs(l), b0=B_IN, off=UO)
                gate_second(l, 0, 1)
                kstate(l, 0, 1)
                act.stage("proj1")
                tiles("glu", l, res[:, 0:4, :], 4, segs(l), ACT.Sigmoid, B_IN + 4)
                out_norm(l, 0)
                gate_first(l, 1, 0)
                act.stage("proj1")
                tiles("aq", l, res[:, 8:12, :], 4, segs(l), b0=B_AQ)
                gate_second(l, 1, 0)
                kstate(l, 1, 0)
                gate_first(l, 1, 1)
                gate_second(l, 1, 1)
                kstate(l, 1, 1)
                out_norm(l, 1)
                act.stage("attn_proj")
                eng.wait_ge(*at(("gla out done", l, 1)))
                for g in range(2):
                    for sg in both:
                        t0, n = SEG[sg]
                        evac(("ak", l, g, sg), ak[:, g, t0:t0 + n], 0, n, ACT.Identity, bias=col(l, B_AK + g))
                for u in range(6):
                    evac(("av", l, 0, u), av[:, u, :], 0, P)
                m.mark(("av", l), *m.at[("free", ("av", l, 0, 5))])
                for j, name in ((0, "k"), (1, "k"), (0, "q"), (1, "q"), (2, "q"), (3, "q")):
                    for sg in (both if name == "k" else segs(l)):
                        t0, n = SEG[sg]
                        evac(("hss", l, name, j, sg), rs[:, t0:t0 + n], 0, n, ACT.Sqrt, bias=eps[:, :])
                if l < DEPTH - 1:
                    attend(l, "c")
                attend(l, "x")
                act.stage("conv_ln")
                for sg in segs(l):
                    t0, n = SEG[sg]
                    evac(("csum", l, sg), sq[:, t0:t0 + n], 0, n, scale=1.0 / 512)
                for sg in segs(l):
                    t0, n = SEG[sg]
                    evac(("csq", l, sg), rs[:, t0:t0 + n], 0, n, ACT.Sqrt, scale=1.0 / 512, bias=eps[:, :])
                for j in range(4):
                    for sg in segs(l):
                        t0, n = SEG[sg]
                        eng.wait_ge(*at(("conv scaled", l, j, sg)))
                        fn(res[:, j, t0:t0 + n], res[:, j, t0:t0 + n], ACT.Silu, ("conv act", l, j, sg),
                           scale=col(l, LN_G + j), bias=col(l, LN_B + j))
                act.stage("merge")
                tiles("ag", l, mg, 4, segs(l), ACT.Silu, B_AG)
                tiles("cgate", l, cg, 4, segs(l), ACT.Silu, B_IN + C_CGATE // P)
                eng.wait_ge(*at(("branch", l, 2)))
                eng.wait_ge(*at(("branch", l, 0)))
                for a in range(4):
                    if a:
                        eng.wait_ge(*at(("merged", l, 2 * a - 1)))
                    for b_ in range(3):
                        for j in range(2):
                            for sg in segs(l):
                                t0, n = SEG[sg]
                                evac(("mgate", l, a, b_, j, sg), mg[:, 2 * b_ + j, t0:t0 + n], 0, n, ACT.Sigmoid,
                                     bias=col(l, B_M + 8 * b_ + 2 * a + j))
                    for b_ in range(3):
                        for j in range(2):
                            for sg in segs(l):
                                t0, n = SEG[sg]
                                evac(("mout", l, a, b_, j, sg), my[:, 2 * b_ + j, t0:t0 + n], 0, n)

            act.stage("rotary")
            eng.wait_ge(*at(("angles", 0)))
            fn(rope[:, 1, :], WT, ACT.Sin)
            eng.wait_ge(*at(("angles", 1)))
            fn(rope[:, 0, :], zt, ACT.Sin, ("rotary",))

            for l in range(DEPTH):
                L = 2 + l
                s = L + 2
                head_of_layer(L, 1)
                act.stage("cell_gates")
                evac(("if", l, 0), rI[0:4, :], 0, TX, ACT.Identity, rows_=slice(0, 4), bias=small[0:4, 24 + 2 * l:25 + 2 * l])
                evac(("if", l, 1), rF[0:4, :], 0, TX, ACT.Identity, rows_=slice(0, 4), bias=small[0:4, 25 + 2 * l:26 + 2 * l])
                fn(rM[0:4, :], rF[0:4, :], ACT.Abs)
                fn(rM[0:4, :], rM[0:4, :], ACT.Exp, scale=-1.0)
                fn(rM[0:4, :], rM[0:4, :], ACT.Ln, ("f ln", l), bias=1.0)
                act.stage("cell")

                def silu(n, j):
                    eng.wait_ge(*at(("conv2", l, n, j)))
                    q = qk2[n % 2]
                    last = j == 3
                    cb = col(s, 96 + (8 if j >= 2 else 0) + 2 * (n % 4) + j % 2)
                    fn(q[:, j, :], q[:, j, :], ACT.Silu, ("qk ready", l, n) if last else None, bias=cb)

                for kind, n, *x in steps2():
                    h, r, b = n % 4, n // 4, n % 2
                    if kind == "gates":
                        evac(("gcols", l), qcol[:, :, :, :], 0, 64)
                        fn(qcol[:, :, 0, :], qcol[:, :, 0, :], ACT.Exp)
                        fn(qcol[:, :, 1, :], qcol[:, :, 1, :], ACT.Exp, scale=-1.0)
                        fn(qcol[:, :, 2, :], qcol[:, :, 2, :], ACT.Exp, ("gate cols", l))
                        evac(("decay", l), decc[:, :, :], 0, 16, ACT.Exp)
                    elif kind == "qk":
                        j = x[0]
                        if n or l:
                            eng.wait_ge(*at(("pre read", l, n - 1, j) if n else ("pre read", l - 1, 7, j)))
                        if r:
                            evac(("qk", l, n, j), pre[:, j, 0:TX], 0, TX)
                        else:
                            evac(("qk", l, n, j), pre[:, j, TAPS2 - 1:TAPS2 - 1 + TX], 0, TX)
                            if j:
                                silu(n, j - 1)
                    elif kind == "v":
                        u = x[0]
                        if not r and u == 0:
                            silu(n, 3)
                        evac(("v2", l, n, u), vv[b][:, u, 0:HD2], 0, HD2)
                        if u == NCH - 1:
                            m.mark(("v2 ready", l, n), *m.at[("free", ("v2", l, n, u))])
                    elif kind == "gate":
                        b_, j = x
                        key = ("gate2", l, n, b_, j)
                        if b_ == 1:
                            if n or j:
                                eng.wait_ge(*at(("zt free", l, n, j)))
                            evac(key, zt, 0, TX, ACT.Silu)
                        else:
                            evac(key, ys[:, 2 * n + j, :], 0, TX, ACT.Silu if r else ACT.Sigmoid)
                    elif kind == "ub":
                        eng.wait_ge(*at(("wt logs", l, n)))
                        fn(WT, WT, ACT.Exp, ("wt", l, n))
                    elif kind == "scores":
                        c = x[0]
                        k = (l, n, c)
                        if c < NCH - 1:
                            scale = const[:, K_ZETA + h:K_ZETA + h + 1] if r else qcol[:, c, 2, h:h + 1]
                            if c:
                                eng.wait_ge(*at(("full", ("dC", (l, n, c - 1), 1))))
                            elif n:
                                eng.wait_ge(*at(("full", ("dC", (l, n - 1, NCH - 2), 1))))
                            if not r:
                                eng.wait_ge(*at(("gate cols scaled", l)))
                            evac(("kT", k), KW, 0, HD2, ACT.Copy, scale=scale)
                            m.mark(("kw", k), *m.at[("free", ("kT", k))])
                    elif kind == "values":
                        c = x[0]
                        k = (l, n, c)
                        if c or n:
                            eng.wait_ge(*at(("hn", (l, n, c - 1) if c else (l, n - 1, NCH - 1))))
                        W = HD2 if r else HD2 + 1
                        evac(("intra", k), NI[:, 0:W], 0, W)
                        eng.wait_ge(*at(("var", k)))
                        fn(small[:, 56:57], small[:, 55:56], ACT.Sqrt, ("sd", k), bias=eps[:, :])

            act.stage("end")
            evac(("ss", 4, "x"), rstd[:, TC:T], 0, TX, ACT.Sqrt, scale=1.0 / D, bias=eps[:, :])
            for u in range(4):
                for half in range(2):
                    evac(("final", u, half), xout[:, u, half * 512:(half + 1) * 512], 0, 512)


        @block.vector
        def _(eng):
            dve = Lane(m, eng, "dve")
            dve.stage("start")
            tt = lambda o_, a, b, op, key=None: dve.link(eng.tensor_tensor(o_, a, b, op), key)
            ts = lambda o_, a, s1, s2, op0, op1, key=None: dve.link(
                eng.tensor_scalar(o_, a, s1, s2, op0, op1) if s2 is not None else eng.tensor_scalar(o_, a, s1, None, op0), key)
            stt = lambda o_, a, s_, b, op0, op1, key=None: dve.link(
                eng.scalar_tensor_tensor(out=o_, in0=a, scalar=s_, in1=b, op0=op0, op1=op1), key)
            cp = lambda o_, a, key=None: dve.link(eng.tensor_copy(o_, a), key)
            rcp = lambda o_, a, key=None: dve.link(eng.reciprocal(o_, a), key)
            M_, A_, S_ = ALU.mult, ALU.add, ALU.subtract

            dve.link(eng.memset(eps[:, :], EPS))
            dve.link(eng.memset(rows, 0.0), "rows clear")
            eng.wait_ge(*at("vrow in"))
            eng.wait_ge(*at(("free", ("cols", NSET - 1))))
            for l in range(DEPTH):
                ts(small[:, 20 + l:21 + l], col(l, QN), 0.125, None, M_, None)

            def norm(L, xs):
                dve.stage("norm")
                s = L if L < 2 else L + 2
                sgs = list(enumerate(("x", "c")))[:xs]
                for c_, sg in sgs:
                    t0, n = SEG[sg]
                    eng.wait_ge(*at(("free", ("xT", KD - 1, "c"))))
                    tt(hT[:, :, t0:t0 + n], xT[:, :, t0:t0 + n], xT[:, :, t0:t0 + n], M_, ("squares", L, sg))
                if L < 4:
                    eng.wait_ge(*at(("free", (("mod", L), 11, 1))))
                    nc_ = 2 if L < 2 else 1
                    stt(gsT[:, :, 0:nc_], modT[:, L % 2, 8:16, 0:nc_], 1.0,
                        cols[:, s, 0:8].unsqueeze(2).broadcast_to([P, 8, nc_]), A_, M_)
                for c_, sg in sgs:
                    t0, n = SEG[sg]
                    eng.wait_ge(*at(("free", ("ss", L, sg))))
                    rcp(rstd[:, t0:t0 + n], rstd[:, t0:t0 + n])
                for c_, sg in sgs:
                    t0, n = SEG[sg]
                    for k in range(KD):
                        g = gsT[:, k, c_:c_ + 1] if L < 4 else col(6, k)
                        stt(hT[:, k, t0:t0 + n], xT[:, k, t0:t0 + n], g, rstd[:, t0:t0 + n], M_, M_,
                            ("h scaled", L, sg, k))
                if L == 4:
                    m.mark(("h ready", 4, "x"), *m.at[("h scaled", 4, "x", KD - 1)])

            def gate(l, p, d):
                dve.stage("gla_gate")
                key = (l, p, d)
                i = l * 4 + p * 2 + d
                eng.wait_ge(*at(("gla ln", key)))
                stt(bA, bA, 0.0, bE, ALU.min, S_)
                if i:
                    q = i - 1
                    eng.wait_ge(*at(("gla core", (q // 4, q // 2 % 2, q % 2))))
                if d == 0 and i:
                    q = (i - 1) // 2
                    eng.wait_ge(*at(("gla out done", q // 2, q % 2)))
                eng.wait_ge(*at("gscan in"))
                dve.link(eng.tensor_tensor_scan(bC, gscan[:, :], bA, 0.0, M_, A_))
                v3 = lambda x_: x_.rearrange("p (a b) -> p a b", b=64)
                last = bC[:, 63:T:64].unsqueeze(2).broadcast_to([P, 12, 64])
                if d == 0:
                    tt(v3(bS), last, v3(bC), S_, ("gla cum", key))
                else:
                    tt(v3(bK), last, v3(bC), S_)
                    tt(bS, bC, bA, S_)
                    tt(bC, bK, bA, A_, ("gla cum", key))
                t0 = 0 if l < DEPTH - 1 else TC
                eng.wait_ge(*at(("gla e", key)))
                eng.wait_ge(*at(("free", ("gq", l, 1, segs(l)[-1]))))
                eng.wait_ge(*at(("free", ("gk", l, 1, "c"))))
                for hh in range(2):
                    r = slice(hh * 64, hh * 64 + 64)
                    stt(bQz[hh][r, t0:T], gq[r, p, t0:T], 0.125, bE[r, t0:T], M_, M_, ("gla qi", key) if hh else None)
                eng.wait_ge(*at(("gla ek", key)))
                tt(bK, gk[:, p, :], bK, M_, ("gla ki", key))
                eng.wait_ge(*at(("gla es", key)))
                tt(bS, gk[:, p, :], bS, M_, ("gla ks", key))

            def core(l, p, d):
                dve.stage("gla_core")
                key = (l, p, d)
                order = [0, 1, 2, 3, 4, 5] if d == 0 else [1, 0, 5, 4, 3, 2]
                steps = [2 * u + c for u in order for c in ((0, 1) if d == 0 else (1, 0))]
                mask = const[:, K_CAUS:K_CAUS + P] if d == 0 else const[:, K_ANTI:K_ANTI + P]
                mask = mask.unsqueeze(1).broadcast_to([P, 2, P])

                def masked(ui):
                    u = order[ui]
                    if not ("c" if u < 2 else "x") in segs(l):
                        return
                    if ui >= 2 and ("c" if order[ui - 2] < 2 else "x") in segs(l):
                        eng.wait_ge(*at(("att used", key, order[ui - 2])))
                    k = ("att", key, u)
                    eng.wait_ge(*at(("full", k)))
                    tt(AM[:, ui % 2, :].rearrange("p (a b) -> p a b", b=P),
                       bank_of[k][:, 0:256].rearrange("p (a b) -> p a b", b=P), mask, M_, ("free", k))
                    m.mark(("att masked", key, u), *m.at[("free", k)])
                masked(0)
                for ui, u in enumerate(order):
                    if ui < 5:
                        masked(ui + 1)
                    for c in ((0, 1) if d == 0 else (1, 0)):
                        ch = 2 * u + c
                        si = steps.index(ch)
                        if si == 11:
                            continue
                        k = ("con", key, si)
                        eng.wait_ge(*at(("full", k)))
                        eng.wait_ge(*at(("gla dec", key)))
                        if si >= 1:
                            eng.wait_ge(*at(("state used", key, si - 1)))
                        if si == 0:
                            cp(ST[:, 1, :], bank_of[k][:, 0:256], ("free", k))
                        else:
                            stt(ST[:, (si + 1) % 2, :], ST[:, si % 2, :], small[:, ch:ch + 1], bank_of[k][:, 0:256],
                                M_, A_, ("free", k))
                        m.mark(("state", key, si + 1), *m.at[("free", k)])

            def out_norm(l, p):
                dve.stage("gla_norm")
                t0 = 0 if l < DEPTH - 1 else TC
                for hh, buf in ((0, bA), (1, bK)):
                    h = 2 * p + hh
                    eng.wait_ge(*at(("gla o", l, h)))
                    tt(bC[:, t0:T], buf[:, t0:T], buf[:, t0:T], M_, ("gla sq", l, h))
                    for sg in segs(l):
                        eng.wait_ge(*at(("free", ("gss", l, h, sg))))
                    rcp(bE[:, t0:T], bE[:, t0:T], ("gss read", l, h))
                    tt(buf[:, t0:T], buf[:, t0:T], bE[:, t0:T], M_)
                    stt(res[:, 4 + h, t0:T], buf[:, t0:T], col(l, G_N), res[:, 4 + h, t0:T], M_, M_,
                        ("gla out done", l, p) if hh else ("gla half done", l, p))

            att_no = [0]

            def attend(l, sg):
                dve.stage("attend")
                nq, nkt = (4, 6) if sg == "x" else (2, 2)
                n_all = 8 * nq
                for n_ in range(n_all + 1):
                    i = att_no[0] + n_
                    if n_ < n_all:
                        eng.wait_ge(*at(("scores", i)))
                        b0 = 4 + 2 * (i % 2)
                        src, ax = (ps[:, b0:b0 + 2, 0:384], AX.XY) if sg == "x" else (ps[:, b0, 0:256], AX.X)
                        if i >= 2:
                            eng.wait_ge(*at(("probs", i - 2)))
                        dve.link(eng.tensor_reduce(small[:, 40 + i % 2:41 + i % 2], src, ax, ALU.max, negate=True), ("nmax", i))
                    if n_ >= 1:
                        i -= 1
                        qb = (n_ - 1) % nq
                        h = (n_ - 1) // nq
                        eng.wait_ge(*at(("probs", i)))
                        rcp(small[:, 48 + i % 2:49 + i % 2], small[:, 44 + i % 2:45 + i % 2])
                        ts(pr[:, i % 2, 0:nkt * P], pr[:, i % 2, 0:nkt * P], small[:, 48 + i % 2:49 + i % 2], None, M_, None,
                           ("probs norm", i))
                        nb = 3 if sg == "x" else 2
                        hn = head_no[0]
                        if qb == 0 and hn >= 2:
                            eng.wait_ge(*at(("full", owners[hn - 2])))
                        for half in range(2 if sg == "x" else 1):
                            k = ("pT", i, half)
                            eng.wait_ge(*at(("full", k)))
                            cp(pt[:, hn % 2, half * nb:(half + 1) * nb, qb * P:(qb + 1) * P],
                               bank_of[k][:, 0:nb * P].rearrange("p (a b) -> p a b", b=P), ("free", k))
                        m.mark(("pT read", i), *m.at[("free", k)])
                        if qb == nq - 1:
                            m.mark(("pt", l, h, sg), *m.at[("free", k)])
                            owners.append(("o", l, h, sg))
                            head_no[0] += 1
                att_no[0] += n_all

            head_no, owners = [0], []

            for l in range(DEPTH):
                norm(l, 2)
                dve.link(eng.memset(bQz[0][64:128, :], 0.0))
                dve.link(eng.memset(bQz[1][0:64, :], 0.0))
                gate(l, 0, 0)
                core(l, 0, 0)
                gate(l, 0, 1)
                core(l, 0, 1)
                out_norm(l, 0)
                gate(l, 1, 0)
                core(l, 1, 0)
                gate(l, 1, 1)
                core(l, 1, 1)
                out_norm(l, 1)
                m.mark(("branch", l, 1), *m.at[("gla out done", l, 1)])
                dve.stage("rope")
                eng.wait_ge(*at("rope in"))
                for j, name in ((0, "k"), (1, "k"), (0, "q"), (1, "q"), (2, "q"), (3, "q")):
                    seg = ["x", "c"] if name == "k" else segs(l)
                    t0 = 0 if "c" in seg else TC
                    src = ak[:, j, :] if name == "k" else res[:, 8 + j, :]
                    g = col(l, KN) if name == "k" else small[:, 20 + l:21 + l]
                    for sg in seg:
                        eng.wait_ge(*at(("free", ("ak", l, j, sg) if name == "k" else ("aq", l, j, sg))))
                    tt(sq[:, t0:T], src[:, t0:T], src[:, t0:T], M_, ("hsq", l, name, j))
                    for sg in seg:
                        eng.wait_ge(*at(("free", ("hss", l, name, j, sg))))
                    rcp(rs[:, t0:T], rs[:, t0:T])
                    stt(src[:, t0:T], src[:, t0:T], g, rs[:, t0:T], M_, M_, ("normed", l, name, j))
                    k = ("rot", l, name, j)
                    eng.wait_ge(*at(("full", k)))
                    tt(tmp[:, 0:TX], bank_of[k][:, 0:TX], rope[:, 1, :], M_, ("free", k))
                    tt(src[:, TC:T], src[:, TC:T], rope[:, 0, :], M_)
                    tt(src[:, TC:T], src[:, TC:T], tmp[:, 0:TX], A_,
                       ("k ready", l, j) if name == "k" else ("q ready", l, j, "x"))
                    if name == "q":
                        m.mark(("q ready", l, j, "c"), *m.at[("q ready", l, j, "x")])
                if l < DEPTH - 1:
                    attend(l, "c")
                attend(l, "x")
                dve.stage("conv_ln")
                for sg in segs(l):
                    t0, n = SEG[sg]
                    eng.wait_ge(*at(("free", ("csum", l, sg))))
                    mean = sq[:, t0:t0 + n].unsqueeze(1).broadcast_to([P, 4, n])
                    tt(res[:, 0:4, t0:t0 + n], res[:, 0:4, t0:t0 + n], mean, S_)
                    tt(mg[:, 0:4, t0:t0 + n], res[:, 0:4, t0:t0 + n], res[:, 0:4, t0:t0 + n], M_, ("conv squares", l, sg))
                for sg in segs(l):
                    t0, n = SEG[sg]
                    eng.wait_ge(*at(("free", ("csq", l, sg))))
                    rcp(rs[:, t0:t0 + n], rs[:, t0:t0 + n])
                for j in range(4):
                    for sg in segs(l):
                        t0, n = SEG[sg]
                        tt(res[:, j, t0:t0 + n], res[:, j, t0:t0 + n], rs[:, t0:t0 + n], M_, ("conv scaled", l, j, sg))
                dve.stage("merge")
                t0 = 0 if l < DEPTH - 1 else TC
                last = segs(l)[-1]
                eng.wait_ge(*at(("free", ("ag", l, 3, last))))
                tt(res[:, 8:12, t0:T], res[:, 8:12, t0:T], mg[:, 0:4, t0:T], M_, ("branch", l, 2))
                eng.wait_ge(*at(("free", ("cgate", l, 3, last))))
                eng.wait_ge(*at(("conv act", l, 3, last)))
                tt(res[:, 0:4, t0:T], res[:, 0:4, t0:T], cg[:, :, t0:T], M_, ("branch", l, 0))
                for a in range(4):
                    eng.wait_ge(*at(("free", ("mgate", l, a, 2, 1, last))))
                    for b_ in range(3):
                        eng.wait_ge(*at(("free", ("mout", l, a, b_, 1, last))))
                        tt(my[:, 2 * b_:2 * b_ + 2, t0:T], my[:, 2 * b_:2 * b_ + 2, t0:T], mg[:, 2 * b_:2 * b_ + 2, t0:T], M_)
                    tt(my[:, 0:2, t0:T], my[:, 0:2, t0:T], my[:, 2:4, t0:T], A_)
                    tt(mT[:, 2 * a:2 * a + 2, t0:T], my[:, 0:2, t0:T], my[:, 4:6, t0:T], A_, ("merged", l, 2 * a))
                    m.mark(("merged", l, 2 * a + 1), *m.at[("merged", l, 2 * a)])
                for j in range(KD):
                    for sg in segs(l):
                        t0, n = SEG[sg]
                        k = ("y", l, j, sg)
                        eng.wait_ge(*at(("full", k)))
                        c_ = 0 if sg == "x" else 1
                        stt(xT[:, j, t0:t0 + n], bank_of[k][:, 0:n], modT[:, l % 2, 16 + j, c_:c_ + 1],
                            xT[:, j, t0:t0 + n], M_, A_, ("free", k))

            dve.stage("rotary")
            eng.wait_ge(*at("positions in"))
            C1, C2_, C3 = 6.28125, 0.0019350051879882812, 3.0199157663446332e-07
            PI = float(np.nextafter(np.float32(np.pi), np.float32(0)))
            cp(WT, posi[:, :])
            ts(WT, WT, const[:, K_FREQ:K_FREQ + 1], None, M_, None)
            ts(UBs, WT, float(1 / (2 * np.pi)), 12582912.0, M_, A_)
            ts(UBs, UBs, -12582912.0, None, A_, None)
            for c_ in (C1, C2_, C3):
                stt(WT, UBs, -c_, WT, M_, A_)
            ts(WT, WT, PI, -PI, ALU.min, ALU.max, ("angles", 0))
            ts(zt, WT, HALF_PI, None, A_, None)
            ts(UBs, zt, PI, -2 * float(np.pi), ALU.is_gt, M_)
            tt(zt, zt, UBs, A_)
            ts(zt, zt, PI, -PI, ALU.min, ALU.max, ("angles", 1))
            dve.link(eng.memset(gscan[0:4, 0:TX], 1.0))
            dve.link(eng.memset(gscan[0:4, 0:TX:CH], 0.0))
            for b in range(2):
                dve.link(eng.memset(vv[b][:, :, HD2:HD2 + 1], 1.0))
            dve.link(eng.memset(small[0:4, 32:33], 0.0))
            dve.link(eng.memset(pre[:, :, 0:TAPS2 - 1], 0.0), ("pre zero", 0))

            for l in range(DEPTH):
                L = 2 + l
                s = L + 2
                norm(L, 1)
                dve.stage("cell_gates")
                R = slice(0, 4)
                v3 = lambda x_: x_[R, :].rearrange("p (a b) -> p a b", b=CH)
                eng.wait_ge(*at(("f ln", l)))
                eng.wait_ge(*at(("free", ("if", l, 0))))
                stt(rF[R, :], rF[R, :], 0.0, rM[R, :], ALU.min, S_)
                dve.link(eng.tensor_tensor_scan(rM[R, :], rF[R, :], rI[R, :], 0.0, A_, ALU.max))
                dve.link(eng.tensor_tensor_scan(rB[R, :], gscan[R, 0:TX], rF[R, :], 0.0, M_, A_))
                tt(rU[R, :], rB[R, :], rM[R, :], S_)
                tt(rW[R, :], rI[R, :], rB[R, :], S_)
                cp(small[R, 33:36], rM[R, CH - 1:TX - 1:CH])
                tt(v3(rI), v3(rU), small[R, 32:36].unsqueeze(2).broadcast_to([4, NCH, CH]), A_)
                tt(v3(rF), v3(rW), rU[R, CH - 1:TX:CH].unsqueeze(2).broadcast_to([4, NCH, CH]), A_, ("gate rows", l))
                dve.stage("cell")
                if l:
                    eng.wait_ge(*at(("pre read", l - 1, 7, 3)))
                    dve.link(eng.memset(pre[:, :, 0:TAPS2 - 1], 0.0), ("pre zero", l))

                def finish(n, c):
                    h, r = n % 4, n // 4
                    k = (l, n, c)
                    W = HD2 if r else HD2 + 1
                    eng.wait_ge(*at(("free", ("intra", k))))
                    src = NI
                    if c:
                        kk = ("inter", k)
                        eng.wait_ge(*at(("full", kk)))
                        w = const[:, K_XI + h:K_XI + h + 1] if r else qcol[:, c, 0, h:h + 1]
                        stt(NM[:, 0:W], bank_of[kk][:, 0:W], w, NI[:, 0:W], M_, A_, ("free", kk))
                        src = NM
                    if c < NCH - 1:
                        for j in range(2):
                            kk = ("dC", k, j)
                            eng.wait_ge(*at(("full", kk)))
                            eng.wait_ge(*at(("free", ("decay", l))))
                            g = const[:, K_GCH + h:K_GCH + h + 1] if r else decc[:, h, c:c + 1]
                            if c == 0:
                                cp(C2[:, j, 0:W], bank_of[kk][:, 0:W], ("free", kk))
                            else:
                                stt(C2[:, j, 0:W], C2[:, j, 0:W], g, bank_of[kk][:, 0:W], M_, A_, ("free", kk))
                            m.mark(("C", k, j), *m.at[("free", kk)])
                    if n or c:
                        eng.wait_ge(*at(("full", ("hT", (l, n, c - 1) if c else (l, n - 1, NCH - 1)))))
                    if not r:
                        ts(small[:, 60:61], src[:, HD2:HD2 + 1], -1.0, qcol[:, c, 1, h:h + 1], M_, ALU.max)
                        tt(small[:, 60:61], small[:, 60:61], src[:, HD2:HD2 + 1], ALU.max)
                        rcp(small[:, 60:61], small[:, 60:61])
                        ts(HN, src[:, 0:HD2], small[:, 60:61], None, M_, None)
                        src = HN
                    dve.link(eng.bn_stats(small[:, 64:70], src[:, 0:HD2]))
                    dve.link(eng.bn_aggr(small[:, 54:56], small[:, 64:70]), ("var", k))
                    eng.wait_ge(*at(("sd", k)))
                    rcp(small[:, 57:58], small[:, 56:57])
                    ts(HN, src[:, 0:HD2], small[:, 54:55], small[:, 57:58], S_, M_, ("hn", k))

                for kind, n, *x in steps2():
                    h, r = n % 4, n // 4
                    if kind == "gates":
                        eng.wait_ge(*at(("gate cols", l)))
                        ts(qcol[:, :, 2, :], qcol[:, :, 2, :], 1.0 / 16, None, M_, None, ("gate cols scaled", l))
                    elif kind == "ub":
                        kk = ("ub", l, n)
                        eng.wait_ge(*at(("full", kk)))
                        for c in range(NCH):
                            stt(WT[:, c * P:(c + 1) * P], bank_of[kk][:, c * P:(c + 1) * P], qcol[:, c, 3, h:h + 1],
                                const[:, K_NEG:K_NEG + P], A_, A_, ("free", kk) if c == NCH - 1 else None)
                        m.mark(("wt logs", l, n), *m.at[("free", kk)])
                    elif kind == "scores":
                        c = x[0]
                        k = (l, n, c)
                        kk = ("s2", k)
                        if n or c:
                            eng.wait_ge(*at(("full", ("intra", (l, n, c - 1) if c else (l, n - 1, NCH - 1)))))
                        if not r:
                            eng.wait_ge(*at(("wt", l, n)))
                        w = const[:, K_DEC + h * P:K_DEC + (h + 1) * P] if r else WT[:, c * P:(c + 1) * P]
                        eng.wait_ge(*at(("full", kk)))
                        stt(SW, bank_of[kk][:, 0:P], 1.0 / 16, w, M_, M_, ("free", kk))
                        m.mark(("sw", k), *m.at[("free", kk)])
                    elif kind == "values":
                        finish(n, x[0])
                    elif kind == "turn":
                        c = x[0]
                        k = (l, n, c)
                        kk = ("hT", k)
                        eng.wait_ge(*at(("full", kk)))
                        eng.wait_ge(*at(("gates ready", l, n)))
                        for j in range(2):
                            y_ = ys[:, 2 * n + j, c * P:(c + 1) * P]
                            stt(y_, bank_of[kk][:, j * P:(j + 1) * P], col(s, 112 + 2 * n + j), y_, M_, M_,
                                ("free", kk) if j else None)
                        if n == 7 and c == NCH - 1:
                            m.mark(("ys", l), *m.at[("free", kk)])
                dve.stage("out2")
                for j in range(KD):
                    k = ("y", L, j, "x")
                    eng.wait_ge(*at(("full", k)))
                    stt(xT[:, j, TC:T], bank_of[k][:, 0:TX], modT[:, L % 2, 16 + j, 0:1], xT[:, j, TC:T], M_, A_, ("free", k))
            norm(4, 1)


        @block.gpsimd
        def _(eng):
            pool = Lane(m, eng, "pool")
            pool.stage("conv")

            def add_product(dst, src, w, scratch):
                pool.link(eng.tensor_scalar(scratch, src, w, 0.0, ALU.mult, ALU.add))
                pool.link(eng.tensor_tensor(dst, dst, scratch, ALU.add))

            for l in range(DEPTH):
                if l:
                    eng.wait_ge(*at(("merged", l - 1, 7)))
                for b0 in (0, TC + PAD, TC + 2 * PAD, TC + TX + 3 * PAD):
                    pool.link(eng.memset(up[:, :, b0:b0 + PAD], 0.0), ("up zero", l) if b0 > TC + TX else None)
                for j in range(4):
                    for sg in segs(l):
                        t0, n = SEG[sg]
                        u0 = UO[sg] + PAD
                        eng.wait_ge(*at(("free", ("glu", l, j, sg))))
                        pool.link(eng.tensor_tensor(up[:, j, u0:u0 + n], up[:, j, u0:u0 + n], res[:, j, t0:t0 + n], ALU.mult))
                        for t in range(TAPS):
                            src = up[:, j, UO[sg] + t:UO[sg] + t + n]
                            w = cols[:, 2 + l, 4 * t + j:4 * t + j + 1]
                            dst = res[:, j, t0:t0 + n]
                            if t == 0:
                                pool.link(eng.tensor_scalar(dst, src, w, col(l, CW_B + j), ALU.mult, ALU.add))
                            else:
                                add_product(dst, src, w, posi[:, 0:n].bitcast(F32))
                m.mark(("conv", l), pool.name, pool.n[pool.name])
            for l in range(DEPTH):
                L = 2 + l
                s = L + 2
                pool.stage("cell")
                for kind, n, *x in steps2():
                    h, r, b = n % 4, n // 4, n % 2
                    q = qk2[b]
                    if kind == "qk":
                        j = x[0]
                        eng.wait_ge(*at(("free", ("qk", l, n, j))))
                        if n >= 2:
                            eng.wait_ge(*at(("full", ("hT", (l, n - 2, NCH - 1)))))
                        if not r:
                            eng.wait_ge(*at(("pre zero", l)))
                            for t in range(TAPS2):
                                src = pre[:, j, t:t + TX]
                                w = col(s, 32 + 16 * t + (8 if j >= 2 else 0) + 2 * h + j % 2)
                                if t == 0:
                                    pool.link(eng.tensor_scalar(q[:, j, :], src, w, None, ALU.mult))
                                else:
                                    add_product(q[:, j, :], src, w, UBs)
                            m.mark(("conv2", l, n, j), pool.name, pool.n[pool.name])
                            m.mark(("pre read", l, n, j), pool.name, pool.n[pool.name])
                        elif j % 2:
                            eng.wait_ge(*at(("rotary",)))
                            a, b_ = pre[:, j - 1, 0:TX], pre[:, j, 0:TX]
                            for out_, x1, x2, op in ((q[:, j - 1, :], a, b_, ALU.subtract), (q[:, j, :], b_, a, ALU.add)):
                                pool.link(eng.tensor_tensor(out_, x1, rope[:, 0, :], ALU.mult))
                                pool.link(eng.tensor_tensor(UBs, x2, rope[:, 1, :], ALU.mult))
                                pool.link(eng.tensor_tensor(out_, out_, UBs, op))
                            for jj in (j - 1, j):
                                m.mark(("pre read", l, n, jj), pool.name, pool.n[pool.name])
                            if j == 3:
                                m.mark(("qk ready", l, n), pool.name, pool.n[pool.name])
                    elif kind == "gate" and not r:
                        b_, j = x
                        if b_ == 1:
                            eng.wait_ge(*at(("free", ("gate2", l, n, 1, j))))
                            pool.link(eng.tensor_tensor(ys[:, 2 * n + j, :], ys[:, 2 * n + j, :], zt, ALU.mult))
                            if j == 0:
                                m.mark(("zt free", l, n, 1), pool.name, pool.n[pool.name])
                            else:
                                m.mark(("gates ready", l, n), pool.name, pool.n[pool.name])
                                if n < 3:
                                    m.mark(("zt free", l, n + 1, 0), pool.name, pool.n[pool.name])
                    elif kind == "gate" and x[1] == 1:
                        eng.wait_ge(*at(("free", ("gate2", l, n, 0, 1))))
                        m.mark(("gates ready", l, n), *m.at[("free", ("gate2", l, n, 0, 1))])


        @block.sync
        def _(eng):
            def sig(name, n, key):
                m.mark(key, name, 16 * n)

            eng.dma_start(const[:, :], I["const"]).then_inc(m.sem("const_in"), 16)
            sig("const_in", 1, "const in")
            eng.dma_start(xin[:, 2:6, :], I["x"][0].rearrange("(u p) d -> p u d", p=P)).then_inc(m.sem("x_in"), 16)
            eng.dma_start(xin[:, 0:2, :], I["ctx"][0].rearrange("(u p) d -> p u d", p=P)).then_inc(m.sem("x_in"), 16)
            nrow = 0
            sets = [(s, set1(s), set1h(s)) for s in range(2)] + [(4 + s, set2(s), []) for s in range(2)]
            sets.append((6, [(I["final_g_2"], 0, 8), (I["c"][0], 8, 8), (I["c_ctx"], 16, 8), (I["c_2"][0], 24, 8)], []))
            eng.wait_ge(*at("rows clear"))
            for s in range(2):
                eng.dma_start(rows[0:4 * TAPS, 2 + s, :], I["conv_dw_w"][s].rearrange("t (j p) -> (t j) p", p=P))\
                   .then_inc(m.sem("rows_in"), 16)
                nrow += 1
            for s, whole, halves in sets:
                for v, r0, n in whole:
                    eng.dma_start(rows[r0:r0 + n, s, :], v.rearrange("(r p) -> r p", p=P)).then_inc(m.sem("rows_in"), 16)
                    nrow += 1
                for v, r0 in halves:
                    for hf in range(2):
                        eng.dma_start(rows[r0:r0 + 1, s, hf * 64:hf * 64 + 64], v.unsqueeze(0)).then_inc(m.sem("rows_in"), 16)
                        nrow += 1
                if s < 2:
                    for d in range(2):
                        eng.dma_start(rows[B_LR:B_LR + 1, s, 32 * d:32 * d + RANK],
                                      I["b_in"][s, C_LR + RANK * d:C_LR + RANK * (d + 1)].unsqueeze(0)).then_inc(m.sem("rows_in"), 16)
                        nrow += 1
            sig("rows_in", nrow, "rows in")
            eng.wait_ge(m.sem("const_in"), 16)
            nv = 0
            for l in range(DEPTH):
                eng.dma_start(const[32 * (l + 1):32 * (l + 1) + 1, K_SEL:K_SEL + 512], I["b_in"][l, C_GV:C_GV + 512].unsqueeze(0))\
                   .then_inc(m.sem("vrow_in"), 16)
                eng.dma_start(const[96:97, K_SEL + l * P:K_SEL + (l + 1) * P], I["b_in"][l, C_AV:C_AV + P].unsqueeze(0))\
                   .then_inc(m.sem("vrow_in"), 16)
                for g, nm in enumerate(("b_igate_2", "b_fgate_2")):
                    eng.dma_start(small[0:4, 24 + 2 * l + g:25 + 2 * l + g], I[nm][l].unsqueeze(1)).then_inc(m.sem("vrow_in"), 16)
                nv += 4
            sig("vrow_in", nv, "vrow in")
            eng.dma_start(gscan[:, :], I["gscan"]).then_inc(m.sem("gscan_in"), 16)
            sig("gscan_in", 1, "gscan in")
            eng.dma_start(rope[:, :, :], I["rope"]).then_inc(m.sem("rope_in"), 16)
            sig("rope_in", 1, "rope in")

            def gate_weights(l):
                if l:
                    eng.wait_ge(*at(("full", ("z", (l - 1, 1, 1), "c"))))
                for d in range(2):
                    eng.dma_start(gup[32 * d:32 * d + RANK, :], I["gla_w_gate"][l, d]).then_inc(m.sem("gup_in"), 16)
                sig("gup_in", 2 * (l + 1), ("gup", l))

            gate_weights(0)
            for n, (parts, _) in enumerate(plan):
                if n >= RING:
                    eng.wait_ge(*at(plan[n - RING][1]))
                for dst, view in parts:
                    eng.dma_start(dst, view).then_inc(m.sem(f"w_slot{n % RING}"), 16)
                if n == starts[1]:
                    gate_weights(1)
                if n == starts[2]:
                    eng.wait_ge(*at(("conv", 1)))
                    eng.dma_start(posi[:, :], I["positions_2"].broadcast_to([P, TX])).then_inc(m.sem("pos_in"), 16)
                    sig("pos_in", 1, "positions in")
            for u in range(4):
                eng.wait_ge(*at(("free", ("final", u, 1))))
                eng.dma_start(out[0, u * P:(u + 1) * P, :], xout[:, u, :]).then_inc(m.sem("out_done"), 16)
            eng.wait_ge(m.sem("out_done"), 16 * 4)

        return m.at


_INS = ['x', 'c', 'ctx', 'c_ctx', 'norm_g', 'w_mod', 'b_mod', 'w_in', 'b_in', 'conv_dw_w', 'conv_dw_b', 'conv_ln_g',
        'conv_ln_b', 'w_conv_out', 'gla_w_gate', 'gla_b_gate', 'gla_norm_g', 'w_gla_out', 'q_norm_g', 'k_norm_g',
        'w_attn_out', 'w_out', 'c_2', 'positions_2', 'w_ada_2', 'b_ada_2', 'norm_g_2', 'w_in_2', 'conv_w_2', 'conv_b_2',
        'b_igate_2', 'b_fgate_2', 'gn_m_2', 'gn_r_2', 'w_out_2', 'final_g_2']


def kernel(**inputs):
    import numpy as _np
    import concourse.bacc as _bacc
    from concourse import mybir as _mybir
    from concourse.bass_utils import run_bass_kernel_spmd as _run

    arrays = {}
    const, gscan, rope, _ = shape_constants()
    given = [(n, _np.ascontiguousarray(inputs[n])) for n in _INS] + [("const", const), ("gscan", gscan), ("rope", rope)]
    for name, a in given:
        arrays[f"in_{name}"] = a

    def program(known):
        nc = _bacc.Bacc("TRN2", target_bir_lowering=False, num_devices=1)
        args = {name: nc.dram_tensor(f"in_{name}", a.shape, _mybir.dt.from_np(a.dtype), kind="ExternalInput").ap()
                for name, a in given}
        out = nc.dram_tensor("out_0", (1, TX, D), F32, kind="ExternalOutput").ap()
        return nc, write_program(nc, args, out, known)

    nc, _ = program(program(None)[1])
    r = _run(nc, [arrays], core_ids=[0])
    return r.results[0]["out_0"]
```

```python
from contextlib import ExitStack

import numpy as np

import concourse.bass as bass
from concourse import mybir

F32 = mybir.dt.float32
I32 = mybir.dt.int32
ALU = mybir.AluOpType
ACT = mybir.ActivationFunctionType
AX = mybir.AxisListType

P = 128
D = 1024
KD = D // P
TC, TX = 256, 512
T = TC + TX
DEPTH = 2
EPS = 1e-6
HALF_PI = float(np.pi / 2)

C_VAL, C_GLU, C_CGATE, C_GQ, C_GK, C_GV, C_GG, C_LR, C_AQ, C_AK, C_AV, C_AG, C_M = (
    0, 512, 1024, 1536, 1792, 2048, 2560, 3072, 3104, 3616, 3744, 3872, 4384)
TAPS, PAD = 31, 15
GLA_CHUNK = 64
RANK = 16
C_MI, C_RQ = 5120, 5128
HEADS2, HD2, TAPS2 = 4, 256, 4
CH = 128
NCH = TX // CH

K_ID, K_HALF, K_ONE, K_PERM, K_CAUS, K_ANTI, K_NEG, K_DEC, K_XI, K_ZETA, K_GCH, K_FREQ, K_SEL, K_END = np.cumsum(
    [0, 128, 128, 128, 128, 128, 128, 128, 512, 4, 4, 4, 1, 512]).tolist()


def shape_constants():
    c = np.zeros((P, K_END), np.float32)
    i = np.arange(P)
    c[:, K_ID:K_ID + P] = np.eye(P)
    c[:, K_HALF:K_HALF + P] = (i[:, None] // 64 == i[None] // 64) / 64.0
    c[:, K_ONE:K_ONE + P] = 1.0
    for p in range(P):
        if p % 32 < 16:
            c[p + 16, K_PERM + p] = -1.0
        else:
            c[p - 16, K_PERM + p] = 1.0
    same = i[:, None] // GLA_CHUNK == i[None] // GLA_CHUNK
    c[:, K_CAUS:K_CAUS + P] = same & (i[:, None] <= i[None])
    c[:, K_ANTI:K_ANTI + P] = same & (i[:, None] >= i[None])
    c[:, K_NEG:K_NEG + P] = np.where(i[:, None] <= i[None], 0.0, -1e30)
    lg = np.log(1.0 - 2.0 ** (-5.0 - np.arange(HEADS2)))
    for h in range(HEADS2):
        d = i[None] - i[:, None]
        c[:, K_DEC + h * P:K_DEC + (h + 1) * P] = np.where(d >= 0, np.exp(lg[h] * np.maximum(d, 0)), 0.0)
        c[:, K_XI + h] = np.exp(lg[h] * (i + 1.0))
        c[:, K_ZETA + h] = np.exp(lg[h] * (CH - 1.0 - i)) / 16.0
        c[:, K_GCH + h] = np.exp(lg[h] * CH)
        c[h, K_SEL + h * P:K_SEL + (h + 1) * P] = 1.0
    c[:, K_FREQ] = (1.0 / (np.float32(10000.0) ** np.linspace(0.0, 1.0, P, dtype=np.float32))).astype(np.float32)
    m = np.ones((P, T), np.float32)
    m[:, ::GLA_CHUNK] = 0.0
    t = np.arange(TX)
    f = (np.float32(10000.0) ** (-np.arange(16, dtype=np.float32) / 16)).astype(np.float32)
    pos = np.where((i[:, None] % 64) < 32, t[None] // 64, t[None] % 64).astype(np.float32)
    ang = pos * f[i % 16][:, None]
    rope = np.stack([np.cos(ang), np.sin(ang)], 1).astype(np.float32)
    m2 = np.ones((P, TX), np.float32)
    m2[:, ::CH] = 0.0
    return c, m, rope, m2


def steps2():
    def proj(n):
        yield [("load", n, 0), ("qk", n, 0)]
        yield [("qk", n, 1)]
        yield [("load", n, 1), ("qk", n, 2)]
        yield [("qk", n, 3)]
        yield [("load", n, 2), ("v", n, 0), ("v", n, 1)]
        yield [("v", n, 2), ("v", n, 3)]
        for b in range(1 if n // 4 else 2):
            yield [("load", n, 3 + b), ("gate", n, b, 0)]
            yield [("gate", n, b, 1)]

    def core(n):
        for c in range(NCH):
            yield ([("ub", n)] if c == 0 and n < 4 else []) + [("scores", n, c)]
            yield [("values", n, c)]
            yield [("turn", n, c)]

    for s in proj(0):
        yield from s
    yield ("gates", 0)
    for n in range(1, HEADS2 * 2 + 1):
        a = list(proj(n)) if n < HEADS2 * 2 else []
        b = list(core(n - 1))
        if n == HEADS2 * 2:
            a = [[("mod", n, i)] for i in range(12)]
        for i in range(max(len(a), len(b))):
            for part in (a, b):
                if i < len(part):
                    yield from part[i]


class Counts:

    def __init__(self, nc, ctx, known):
        self.nc, self.ctx, self.known, self.at, self.sems = nc, ctx, known, {}, {}

    def sem(self, name):
        if name not in self.sems:
            self.sems[name] = self.ctx.enter_context(self.nc.semaphore(name))
        return self.sems[name]

    def mark(self, key, name, count):
        assert key not in self.at, key
        self.at[key] = (name, count)

    def reached(self, key):
        if self.known is None:
            return self.sem("draft"), 1
        name, count = self.known[key]
        return self.sem(name), count


class Lane:

    def __init__(self, counts, eng, who):
        self.m, self.eng, self.who, self.name, self.n = counts, eng, who, None, {}

    def stage(self, name):
        self.name = f"{self.who}_{name}"
        self.n.setdefault(self.name, 0)

    def tell(self, key=None):
        self.n[self.name] += 1
        if key is not None:
            self.m.mark(key, self.name, self.n[self.name])
        return self.m.sem(self.name), 1

    def link(self, ins, key=None):
        ins.then_inc(*self.tell(key))
        self.eng.wait_ge(self.m.sem(self.name), self.n[self.name])


def write_program(nc, I, out, known):
    with ExitStack() as ctx:
        def sb(name, shape, dt=F32):
            return ctx.enter_context(nc.sbuf_tensor(name, shape, dt))

        m = Counts(nc, ctx, known)
        at = m.reached

        const = sb("const", [P, K_END])
        xT = sb("xT", [P, KD, T])
        hT = sb("hT", [P, KD, T])
        RING, SLOT = 4, 2048
        wring = sb("wring", [P, RING, SLOT])
        NSET = 7
        cols = sb("cols", [P, NSET, P])
        cT = sb("cT", [P, 24])
        modT = sb("modT", [P, 2, 24, 2])
        posi = sb("posi", [P, TX], I32)
        gsT = sb("gsT", [P, KD, 2])
        rstd = sb("rstd", [P, T])
        rope = sb("rope", [P, 2, TX])
        eps = sb("eps", [P, 1])
        small = sb("small", [P, 96])
        A0, A1, A2 = 12 * T, 13312, 3328
        arena = sb("arena", [P, A0 + A1 + A2])

        def cut(at, *shape):
            n = int(np.prod(shape))
            v = arena[:, at:at + n]
            if len(shape) == 2:
                v = v.rearrange("p (a b) -> p a b", b=shape[1])
            elif len(shape) == 3:
                v = v.rearrange("p (a b c) -> p a b c", b=shape[1], c=shape[2])
            return v, at + n

        res, _ = cut(0, 12, T)
        gq, o = cut(A0, 2, T)
        gk, o = cut(o, 2, T)
        gv, o = cut(o, 6, 512)
        lr, o = cut(o, T)
        bA, o = cut(o, T)
        bC, o = cut(o, T)
        bE, o = cut(o, T)
        bQ, o = cut(o, T)
        bK, o = cut(o, T)
        bS, o = cut(o, T)
        kst, o = cut(o, 6, P)
        ST, o = cut(o, 2, 256)
        AM, o = cut(o, 2, 256)
        assert o <= A0 + A1, o
        bQz = [bQ, rstd[:, :]]
        dec = [small[:, 0:12], small[:, 72:84]]
        gup = sb("gup", [P, 256])
        gscan = sb("gscan", [P, T])
        ak, o = cut(A0, 2, T)
        av, o = cut(o, 6, P)
        pr, o = cut(o, 3, T)
        pt, o = cut(o, 2, 6, 512)
        sq, o = cut(o, T)
        rs, o = cut(o, T)
        tmp, o = cut(o, T)
        assert o <= A0 + A1, o
        UW = TC + TX + 4 * PAD
        up, o = cut(A0 + A1, 4, UW)
        UO = {"c": 0, "x": TC + 2 * PAD}
        cg, _ = cut(A0 + A1, 4, T)
        mT, o = cut(A0, KD, T)
        mg, o = cut(o, 6, T)
        my, o = cut(o, 6, T)
        assert o <= A0 + A1 + A2, o
        xin, _ = cut(A0, 6, D)
        rows, _ = cut(0, NSET, P)
        xout, _ = cut(0, 4, D)
        ys, o = cut(0, 16, TX)
        pre, o = cut(o, 4, TX + TAPS2 - 1 + 1)
        qk2, vv = [None] * 2, [None] * 2
        for b in range(2):
            qk2[b], o = cut(o, 4, TX)
            vv[b], o = cut(o, NCH, 260)
        zt, o = cut(o, TX)
        WT, o = cut(o, TX)
        SW, o = cut(o, P)
        NI, o = cut(o, 260)
        NM, o = cut(o, 260)
        HN, o = cut(o, 256)
        KW, o = cut(o, 256)
        C2, o = cut(o, 2, 260)
        UBs, o = cut(o, TX)
        rI, o = cut(o, TX)
        rF, o = cut(o, TX)
        rM, o = cut(o, TX)
        rB, o = cut(o, TX)
        rU, o = cut(o, TX)
        rW, o = cut(o, TX)
        assert o <= A0 + A1 + A2, (o, A0 + A1 + A2)
        qcol = sb("qcol", [P, NCH, 4, 4])
        decc = sb("decc", [P, 4, NCH])

        ps = ctx.enter_context(nc.psum_tensor("ps", [P, 8, 512], F32))
        bank = [ps[:, i, :] for i in range(8)]
        NARROW, WIDE = {"A": [0, 1], "V": [2, 3]}, {"A": [0, 1, 4, 5], "V": [2, 3, 6, 7]}
        GLA_RINGS = {"A": [0, 1, 7], "V": [2, 3]}
        CELL = {"A": [0, 1, 4], "V": [2, 3, 5]}
        turn_of, last_on, bank_of = {"A": 0, "V": 0}, {}, {}

        ident = const[:, K_ID:K_ID + P]
        ones = const[:, K_ONE:K_ONE + P]
        block = ctx.enter_context(nc.Block())
        landed = [0] * RING
        starts, plan = [], []
        SEG = {"x": (TC, TX), "c": (0, TC)}

        def segs(l):
            return ["x", "c"] if l < DEPTH - 1 else ["x"]

        def set1(l):
            return [(I["norm_g"][l], 0, 8), (I["b_mod"][l], 8, 24),
                    (I["b_in"][l, 0:C_LR], 32, 24), (I["b_in"][l, C_AQ:C_AK], 56, 4),
                    (I["b_in"][l, C_AG:C_M], 60, 4), (I["b_in"][l, C_M:C_M + 3 * D], 64, 24),
                    (I["conv_dw_b"][l], 88, 4), (I["conv_ln_g"][l], 92, 4), (I["conv_ln_b"][l], 96, 4),
                    (I["gla_b_gate"][l, 0], 100, 2), (I["gla_b_gate"][l, 1], 102, 2),
                    (I["gla_norm_g"][l], 104, 1)]

        def set1h(l):
            b = I["b_in"][l]
            return [(b[C_AK:C_AK + 64], 105), (b[C_AK + 64:C_AK + 128], 106),
                    (I["q_norm_g"][l], 107), (I["k_norm_g"][l], 108)]

        N_G, B_MOD, B_IN, B_AQ, B_AG, B_M, CW_B, LN_G, LN_B, G_B, G_N, B_AK, QN, KN, B_LR = (
            0, 8, 32, 56, 60, 64, 88, 92, 96, 100, 104, 105, 107, 108, 109)

        def set2(l):
            return [(I["norm_g_2"][l], 0, 8), (I["b_ada_2"][l], 8, 24),
                    (I["conv_w_2"][l].rearrange("a b -> (a b)"), 32, 64), (I["conv_b_2"][l], 96, 16),
                    (I["gn_m_2"][l], 112, 8), (I["gn_r_2"][l], 120, 8)]

        def col(s, r):
            return cols[:, s, r:r + 1]

        @block.tensor
        def _(eng):
            pe = Lane(m, eng, "pe")
            pe.stage("start")

            rings = [WIDE]

            def claim(*banks):
                for b in banks:
                    if b in last_on:
                        eng.wait_ge(*at(("free", last_on.pop(b))))

            def next_bank(ring, key):
                turn_of[ring] += 1
                b = rings[0][ring][turn_of[ring] % len(rings[0][ring])]
                if b in last_on:
                    eng.wait_ge(*at(("free", last_on[b])))
                last_on[b] = key
                bank_of[key] = bank[b]
                return b

            def job(ring, key, mms):
                mms(bank[next_bank(ring, key)]).then_inc(*pe.tell(("full", key)))

            def weights(view, K, C, parts=None):
                n = len(plan)
                slot = wring[:, n % RING, 0:K * C].rearrange("p (k c) -> p k c", c=C)
                plan.append([parts(slot) if parts else [(slot, view)], None])
                landed[n % RING] += 16 * len(plan[n][0])
                eng.wait_ge(m.sem(f"w_slot{n % RING}"), landed[n % RING])
                return wring[:, n % RING, 0:K * C].rearrange("p (k c) -> p k c", c=C)

            def used(key):
                plan[-1][1] = key

            def wv(t, c0, C):
                return t[:, c0:c0 + C].rearrange("(k p) c -> p k c", p=P)

            def acc(parts):
                def mms(out):
                    for i, (o_, a, b_) in enumerate(parts):
                        last = eng.matmul(o_(out), a, b_, start=(i == 0), stop=(i == len(parts) - 1))
                    return last
                return mms

            def project(key, w, c, src, K, sg, ring="A", M=P):
                t0, n = SEG[sg]
                job(ring, key, acc([(lambda o_: o_[0:M, 0:n], w[:, k, c:c + M], src[:, k, t0:t0 + n])
                                    for k in range(K)]))

            def tiles_by_part(name, l, wt, c0, ntile, seg, first=0):
                for j0 in range(first, first + ntile, 2):
                    w = weights(wv(wt, c0 + j0 * P, 2 * P), KD, 2 * P)
                    for j in range(2):
                        for sg in seg:
                            t0, n = SEG[sg]
                            key = (name, l, j0 + j, sg)
                            b = next_bank("A", key)
                            for k in range(KD):
                                mm = eng.matmul(bank[b][:, 0:n], w[:, k, j * P:(j + 1) * P], hT[:, k, t0:t0 + n],
                                                start=(k == 0), stop=(k == KD - 1))
                                if k == KD - 1:
                                    mm.then_inc(*pe.tell(("full", key)))
                                if k % 2:
                                    yield
                    used(("full", (name, l, j0 + 1, seg[-1])))

            def tiles(*a):
                for _ in tiles_by_part(*a):
                    pass

            eng.wait_ge(*at("const in"))
            eng.wait_ge(m.sem("x_in"), 16 * 2)
            for k in range(KD):
                for g, u0, nu in (("x", 2, 4), ("c", 0, 2)):
                    def mms(o_, k=k, u0=u0, nu=nu):
                        for u in range(nu):
                            last = eng.transpose(o_[:, u * P:(u + 1) * P], xin[:, u0 + u, k * P:(k + 1) * P], ident)
                        return last
                    job("A", ("xT", k, g), mms)
            eng.wait_ge(*at("rows in"))
            for s in range(NSET):
                job("A", ("cols", s), lambda o_: eng.transpose(o_[:, 0:P], rows[:, s, :], ident))

            def modulate(L, groups=range(12)):
                for _ in mod_by_part(L, groups):
                    pass

            def mod_by_part(L, groups):
                key = ("mod", L)
                wt, col0, ncol = (I["w_mod"][L], 0, 2) if L < 2 else (I["w_ada_2"][L - 2], 16, 1)
                eng.wait_ge(*at(("cT",)))
                for g in groups:
                    w = weights(wv(wt, g * 256, 256), KD, 256)
                    for j in range(2):
                        job("A", (key, g, j), acc([(lambda o_: o_[:, 0:ncol], w[:, k, j * P:(j + 1) * P],
                                                    cT[:, col0 + k:col0 + k + 8 * (ncol - 1) + 1:8])
                                                   for k in range(KD)]))
                    used(("full", (key, g, 1)))
                    yield

            def square_sum(L, k):
                for i, sg in enumerate(["x", "c"] if L < 2 else ["x"]):
                    t0, n = SEG[sg]
                    eng.wait_ge(*at(("squares", L, sg, k)))
                    mm = eng.matmul(bank[4 + i][:, 0:n], ones, hT[:, k, t0:t0 + n], start=(k == 0), stop=(k == KD - 1))
                    mm.then_inc(*pe.tell(("ss", L, sg, k)))

            def gla_core(l, p, d, between, rate):
                pe.stage("gla_core")
                key = (l, p, d)
                if d == 0:
                    claim(4, 5, 6)
                for half in range(2):
                    def mms(o_, half=half):
                        for u in range(3):
                            last = eng.transpose(o_[:, u * P:(u + 1) * P],
                                                 bS[:, (half * 3 + u) * P:(half * 3 + u + 1) * P], ident)
                        return last
                    eng.wait_ge(*at(("gla ks", key)))
                    job("A", ("kst", key, half), mms)
                order = [0, 1, 2, 3, 4, 5] if d == 0 else [1, 0, 5, 4, 3, 2]
                steps = [2 * u + c for u in order for c in ((0, 1) if d == 0 else (1, 0))]
                accs = {"x": [bank[4], bank[5]], "c": [bank[6], bank[6]]}
                if d == 0 and (l, p) != (0, 0):
                    eng.wait_ge(*at(("gla out read", l if p else l - 1, 1 - p)))
                if d == 0:
                    gla_gate(l, p, 1)
                    pe.stage("gla_core")
                def att(u):
                    if u is not None and ("c" if u < 2 else "x") in segs(l):
                        eng.wait_ge(*at(("gla qi", key)))
                        eng.wait_ge(*at(("gla ki", key)))
                        job("V", ("att", key, u), acc_two(key, slice(u * P, u * P + P)))
                att(order[0])
                for ui, u in enumerate(order):
                    sg = "c" if u < 2 else "x"
                    outs = sg in segs(l)
                    col0 = u * P if u < 2 else (u - 2) * P
                    att(order[ui + 1] if ui < 5 else None)
                    if outs:
                        eng.wait_ge(*at(("att masked", key, u)))
                        eng.wait_ge(*at(("gla v", l)))
                        for hh in range(2):
                            h = 2 * p + hh
                            c1 = col0 + (hh * 256 if sg == "c" else 0)
                            first = d == 0 and ((sg == "x" and u == 2) or (sg == "c" and u == 0 and hh == 0))
                            last = eng.matmul(accs[sg][hh][:, c1:c1 + P], gv[:, u, h * P:(h + 1) * P],
                                              AM[:, ui % 2, hh * P:(hh + 1) * P], start=first, stop=False,
                                              skip_group_check=True)
                        last.then_inc(*pe.tell(("att used", key, u)))
                    for c in ((0, 1) if d == 0 else (1, 0)):
                        ch = 2 * u + c
                        si = steps.index(ch)
                        if outs and si > 0:
                            eng.wait_ge(*at(("state", key, si)))
                            for hh in range(2):
                                c1 = col0 + c * 64 + (hh * 256 if sg == "c" else 0)
                                last = eng.matmul(accs[sg][hh][:, c1:c1 + 64],
                                                  ST[:, si % 2, hh * P:(hh + 1) * P],
                                                  bQz[hh][:, ch * 64:ch * 64 + 64],
                                                  start=False, skip_group_check=True,
                                                  stop=d == 1 and c == 0 and (u == 2 or (u == 0 and hh == 1)))
                        if outs:
                            if si == 0:
                                m.mark(("state used", key, si), *m.at[("att used", key, u)])
                            else:
                                last.then_inc(*pe.tell(("state used", key, si)))
                        if si < 11:
                            eng.wait_ge(*at(("kst", key, 1)))
                            eng.wait_ge(*at(("gla v", l)))
                            job("V", ("con", key, si),
                                lambda o_: eng.matmul(o_[:, 0:256], kst[c * 64:c * 64 + 64, u, :],
                                                      gv[c * 64:c * 64 + 64, u, p * 256:p * 256 + 256],
                                                      start=True, stop=True))
                            if not outs:
                                m.mark(("state used", key, si), *m.at[("full", ("con", key, si))])
                        for _ in range(rate):
                            next(between, None)
                m.mark(("gla core", key), *m.at[("state used", key, 11)])
                for _ in between:
                    pass

            def acc_two(key, tk):
                def mms(o_):
                    for hh in range(2):
                        last = eng.matmul(o_[:, hh * P:(hh + 1) * P], bK[:, tk], bQz[hh][:, tk], start=True, stop=True)
                    return last
                return mms

            def gla_gate(l, p, d):
                pe.stage("gla_gate")
                for sg in ("x", "c"):
                    t0, n = SEG[sg]
                    eng.wait_ge(*at(("gup", l)))
                    eng.wait_ge(*at(("lr", l, "c", 1)))
                    job("A", ("z", (l, p, d), sg),
                        lambda o_: eng.matmul(o_[:, 0:n], gup[32 * d:32 * d + RANK, p * P:(p + 1) * P],
                                              lr[32 * d:32 * d + RANK, t0:t0 + n], start=True, stop=True))

            def gla_out_norm(l, p):
                pe.stage("gla_norm")
                for hh in range(2):
                    for sg in segs(l):
                        t0, n = SEG[sg]
                        eng.wait_ge(*at(("gla sq", l, 2 * p + hh)))
                        job("A", ("gss", l, 2 * p + hh, sg),
                            lambda o_: eng.matmul(o_[:, 0:n], ones, bC[:, t0:t0 + n], start=True, stop=True))

            def attend(l, sg):
                pe.stage("attend")
                claim(4, 5, 6, 7)
                rings[0] = NARROW
                nq, nkt = (4, 6) if sg == "x" else (2, 2)
                q0 = SEG[sg][0]
                keys = nkt * P
                cnt = [0]

                def scores(h, qb):
                    i = att_no[0]
                    att_no[0] += 1
                    g = h // 4
                    r = slice((h % 2) * 64, (h % 2) * 64 + 64)
                    b0 = 4 + 2 * (i % 2)
                    if i >= 2:
                        eng.wait_ge(*at(("probs", i - 2)))
                    eng.wait_ge(*at(("q ready", l, h // 2, sg)))
                    eng.wait_ge(*at(("k ready", l, g)))
                    w = 384 if sg == "x" else 256
                    for half in range(keys // w):
                        last = eng.matmul(bank[b0 + half][:, 0:w], res[r, 8 + h // 2, q0 + qb * P:q0 + qb * P + P],
                                          ak[r, g, half * w:(half + 1) * w], start=True, stop=True)
                    last.then_inc(*pe.tell(("scores", i)))
                    return i

                def turn(h, qb, i):
                    for half in range(2 if sg == "x" else 1):
                        nb = 3 if sg == "x" else 2

                        def mms(o_, half=half):
                            for u in range(nb):
                                kt = half * nb + u
                                last = eng.transpose(o_[:, u * P:(u + 1) * P], pr[:, i % 3, kt * P:(kt + 1) * P], ident)
                            return last
                        eng.wait_ge(*at(("probs norm", i)))
                        job("V", ("pT", i, half), mms)

                def values(h, hn):
                    g = h // 4
                    r0 = (h % 2) * 64

                    def mms(o_):
                        for kt in range(nkt):
                            last = eng.matmul(o_[r0:r0 + 64, 0:nq * P], av[:, kt, g * 64:(g + 1) * 64],
                                              pt[:, hn % 2, kt, 0:nq * P], start=(kt == 0), stop=(kt == nkt - 1))
                        return last
                    eng.wait_ge(*at(("pt", l, h, sg)))
                    eng.wait_ge(*at(("av", l)))
                    job("A", ("o", l, h, sg), mms)

                seq = [(h, qb) for h in range(8) for qb in range(nq)]
                ids = {}

                def back(n_):
                    hp, qp = seq[n_]
                    turn(hp, qp, ids[n_])
                    if qp == nq - 1:
                        values(hp, head_no[0])
                        head_no[0] += 1
                for n_, (h, qb) in enumerate(seq):
                    ids[n_] = scores(h, qb)
                    if n_ >= 2:
                        back(n_ - 2)
                back(len(seq) - 2)
                back(len(seq) - 1)

            att_no, head_no = [0], [0]

            for l in range(DEPTH):
                if l == 0:
                    pe.stage("proj1")
                    modulate(0)
                    claim(4, 5)
                    for k in range(KD):
                        square_sum(0, k)
                starts.append(len(plan))
                pe.stage("proj1")
                rings[0] = GLA_RINGS
                both = ["x", "c"]
                wi = I["w_in"][l]
                w = weights(wv(wi, C_LR, 32), KD, 32)
                for sg in both:
                    for d in range(2):
                        t0, n = SEG[sg]
                        if d == 0:
                            eng.wait_ge(*at(("h ready", l, sg)))
                        job("A", ("lr", l, sg, d), acc([(lambda o_: o_[32 * d:32 * d + RANK, 0:n],
                                                         w[:, k, d * RANK:(d + 1) * RANK], hT[:, k, t0:t0 + n])
                                                        for k in range(KD)]))
                used(("full", ("lr", l, "c", 1)))
                gla_gate(l, 0, 0)
                pe.stage("proj1")
                tiles("val", l, wi, C_VAL, 4, segs(l))
                tiles("glu", l, wi, C_GLU, 4, segs(l))
                tiles("gq", l, wi, C_GQ, 2, segs(l))
                tiles("gk", l, wi, C_GK, 2, both)

                def value_rows(name, c0, width, row, bc):
                    eng.wait_ge(*at("vrow in"))
                    for g0 in range(0, width, 256):
                        cw = min(256, width - g0)
                        w = weights(wv(wi, c0 + g0, cw), KD, cw)
                        for u in range(6):
                            job("A", (name, l, g0 // 256, u), acc(
                                [(lambda o_: o_[:, 0:cw], hT[:, k, u * P:(u + 1) * P], w[:, k, :]) for k in range(KD)]
                                + [(lambda o_: o_[:, 0:cw], ones[row:row + 1, :], const[row:row + 1, K_SEL + bc + g0:K_SEL + bc + g0 + cw])]))
                            yield
                        used(("full", (name, l, g0 // 256, 5)))
                for _ in value_rows("gv", C_GV, 512, 32 * (l + 1), 0):
                    pass

                def keys_values():
                    def twice(slot):
                        return [(slot[:, :, g * P + hf * 64:g * P + hf * 64 + 64], wv(wi, C_AK + g * 64, 64))
                                for g in range(2) for hf in range(2)]
                    w = weights(None, KD, 256, twice)
                    for g in range(2):
                        for sg in both:
                            project(("ak", l, g, sg), w, g * P, hT, KD, sg)
                            yield
                    used(("full", ("ak", l, 1, "c")))
                    yield from value_rows("av", C_AV, 128, 96, l * P)

                gla_core(l, 0, 0, tiles_by_part("gg", l, wi, C_GG, 4, segs(l)), 2)
                gla_core(l, 0, 1, tiles_by_part("aq", l, wi, C_AQ, 2, segs(l)), 1)
                gla_out_norm(l, 0)
                gla_gate(l, 1, 0)
                pe.stage("proj1")
                tiles("aq", l, wi, C_AQ, 2, segs(l), 2)
                gla_core(l, 1, 0, mod_by_part(l + 1, range(0, 6)), 1)
                gla_core(l, 1, 1, keys_values(), 1)
                gla_out_norm(l, 1)
                modulate(l + 1, range(6, 12))
                pe.stage("attn_proj")
                for j, name in ((0, "k"), (1, "k"), (0, "q"), (1, "q"), (2, "q"), (3, "q")):
                    for sg in (both if name == "k" else segs(l)):
                        t0, n = SEG[sg]
                        eng.wait_ge(*at(("hsq", l, name, j)))
                        job("A", ("hss", l, name, j, sg),
                            lambda o_: eng.matmul(o_[:, 0:n], const[:, K_HALF:K_HALF + P], sq[:, t0:t0 + n],
                                                  start=True, stop=True))
                    src = ak[:, j, TC:T] if name == "k" else res[:, 8 + j, TC:T]
                    eng.wait_ge(*at(("normed", l, name, j)))
                    job("V", ("rot", l, name, j),
                        lambda o_: eng.matmul(o_[:, 0:TX], const[:, K_PERM:K_PERM + P], src, start=True, stop=True))
                if l < DEPTH - 1:
                    attend(l, "c")
                attend(l, "x")
                pe.stage("merge")
                rings[0] = WIDE
                tiles("ag", l, wi, C_AG, 4, segs(l))
                pe.stage("conv_ln")
                for sg in segs(l):
                    t0, n = SEG[sg]
                    eng.wait_ge(*at(("conv", l)))
                    job("A", ("csum", l, sg), acc([(lambda o_: o_[:, 0:n], ones, res[:, j, t0:t0 + n])
                                                   for j in range(4)]))
                pe.stage("merge")
                tiles("cgate", l, wi, C_CGATE, 2, segs(l))
                pe.stage("conv_ln")
                for sg in segs(l):
                    t0, n = SEG[sg]
                    eng.wait_ge(*at(("conv squares", l, sg)))
                    job("A", ("csq", l, sg), acc([(lambda o_: o_[:, 0:n], ones, mT[:, j, t0:t0 + n])
                                                  for j in range(4)]))
                pe.stage("merge")
                tiles("cgate", l, wi, C_CGATE, 2, segs(l), 2)
                for a in range(4):
                    for b_ in range(3):
                        w = weights(wv(wi, C_M + b_ * D + a * 256, 256), KD, 256)
                        for j in range(2):
                            for sg in segs(l):
                                project(("mgate", l, a, b_, j, sg), w, j * P, hT, KD, sg)
                        used(("full", ("mgate", l, a, b_, 1, segs(l)[-1])))
                    for b_, nm in enumerate(("w_conv_out", "w_gla_out", "w_attn_out")):
                        if a == 0:
                            eng.wait_ge(*at(("branch", l, b_)))
                        w = weights(wv(I[nm][l], a * 256, 256), 4, 256)
                        for j in range(2):
                            for sg in segs(l):
                                project(("mout", l, a, b_, j, sg), w, j * P, res[:, 4 * b_:4 * b_ + 4, :], 4, sg)
                        used(("full", ("mout", l, a, b_, 1, segs(l)[-1])))
                eng.wait_ge(*at(("merged", l, KD - 1)))
                claim(4, 5)
                rings[0] = {"A": [0, 1], "V": [2, 3, 6, 7]}
                for j in range(0, KD, 2):
                    w = weights(wv(I["w_out"][l], j * P, 2 * P), KD, 2 * P)
                    for i in range(2):
                        for sg in segs(l):
                            project(("y", l, j + i, sg), w, i * P, mT, KD, sg, "V")
                    used(("full", ("y", l, j + 1, segs(l)[-1])))
                    if j:
                        square_sum(l + 1, j - 2)
                        square_sum(l + 1, j - 1)
                square_sum(l + 1, KD - 2)
                square_sum(l + 1, KD - 1)

            for l in range(DEPTH):
                L = 2 + l
                starts.append(len(plan))
                wi = I["w_in_2"][l]
                pe.stage("proj2")
                rings[0] = CELL
                eng.wait_ge(*at(("h ready", L, "x")))
                w = weights(wv(wi, C_MI, 8), KD, 8)
                for g in range(2):
                    job("A", ("if", l, g), acc([(lambda o_: o_[0:4, 0:TX], w[:, k, 4 * g:4 * g + 4],
                                                 hT[:, k, TC:T]) for k in range(KD)]))
                used(("full", ("if", l, 1)))

                def gate_cols():
                    def mms(o_):
                        for c in range(NCH):
                            for q_, r_ in enumerate((rI, rM, rF, rW)):
                                o4 = (c * 4 + q_) * 4
                                last = eng.transpose(o_[:, o4:o4 + 4], r_[0:4, c * P:(c + 1) * P], ident[0:4, 0:4])
                        return last
                    eng.wait_ge(*at(("gate rows", l)))
                    job("A", ("gcols", l), mms)

                    def mms2(o_):
                        for h in range(4):
                            last = eng.matmul(o_[:, h * NCH:(h + 1) * NCH], const[0:4, K_SEL + h * P:K_SEL + (h + 1) * P],
                                              rI[0:4, P - 1:TX:P], start=True, stop=True)
                        return last
                    job("A", ("decay", l), mms2)

                w2 = None
                for kind, n, *x in steps2():
                    h, r, b = n % 4, n // 4, n % 2
                    base = C_RQ if r else 0
                    q, v = qk2[b], vv[b]
                    if kind == "mod":
                        if l < DEPTH - 1:
                            modulate(L + 1, [x[0]])
                            pe.stage("cell")
                    elif kind == "gates":
                        gate_cols()
                    elif kind == "load":
                        w2 = weights(wv(wi, base + x[0] * D + h * HD2, HD2), KD, HD2)
                    elif kind == "qk":
                        project(("qk", l, n, x[0]), w2, (x[0] % 2) * P, hT, KD, "x")
                        used(("full", ("qk", l, n, x[0])))
                    elif kind == "v":
                        u = x[0]
                        job("A", ("v2", l, n, u), acc([(lambda o_: o_[:, 0:HD2], hT[:, k, TC + u * P:TC + (u + 1) * P],
                                                        w2[:, k, :]) for k in range(KD)]))
                        used(("full", ("v2", l, n, u)))
                    elif kind == "gate":
                        project(("gate2", l, n, x[0], x[1]), w2, x[1] * P, hT, KD, "x")
                        used(("full", ("gate2", l, n, x[0], x[1])))
                    elif kind == "ub":
                        eng.wait_ge(*at(("gate rows", l)))
                        job("V", ("ub", l, n), lambda o_: eng.matmul(o_[:, 0:TX], const[0:4, K_SEL + h * P:K_SEL + (h + 1) * P],
                                                                     rU[0:4, :], start=True, stop=True))
                    else:
                        c = x[0]
                        k = (l, n, c)
                        ts = slice(c * P, (c + 1) * P)
                        W = HD2 if r else HD2 + 1
                        if kind == "scores":
                            eng.wait_ge(*at(("qk ready", l, n)))
                            job("V", ("s2", k), acc([(lambda o_: o_[:, 0:P], q[:, 2 + j, ts], q[:, j, ts]) for j in range(2)]))
                            if c < NCH - 1:
                                def mms(o_):
                                    for j in range(2):
                                        last = eng.transpose(o_[:, j * P:(j + 1) * P], q[:, 2 + j, ts], ident)
                                    return last
                                eng.wait_ge(*at(("qk ready", l, n)))
                                job("A", ("kT", k), mms)
                        elif kind == "values":
                            eng.wait_ge(*at(("sw", k)))
                            eng.wait_ge(*at(("v2 ready", l, n)))
                            job("A", ("intra", k), lambda o_: eng.matmul(o_[:, 0:W], SW[:, :], v[:, c, 0:W], start=True, stop=True))
                            if c > 0:
                                eng.wait_ge(*at(("C", (l, n, c - 1), 1)))
                                job("V", ("inter", k), acc([(lambda o_: o_[:, 0:W], q[:, j, ts], C2[:, j, 0:W])
                                                            for j in range(2)]))
                            if c < NCH - 1:
                                for j in range(2):
                                    eng.wait_ge(*at(("kw", k)))
                                    eng.wait_ge(*at(("v2 ready", l, n)))
                                    job("V", ("dC", k, j), lambda o_: eng.matmul(o_[:, 0:W], KW[:, j * P:(j + 1) * P], v[:, c, 0:W],
                                                                                 start=True, stop=True))
                        elif kind == "turn":
                            def mms3(o_):
                                for j in range(2):
                                    last = eng.transpose(o_[:, j * P:(j + 1) * P], HN[:, j * P:(j + 1) * P], ident)
                                return last
                            eng.wait_ge(*at(("hn", k)))
                            job("V", ("hT", k), mms3)
                pe.stage("out2")
                claim(4, 5)
                rings[0] = {"A": [0, 1], "V": [2, 3, 6, 7]}
                for j in range(KD):
                    w = weights(wv(I["w_out_2"][l], j * P, P), 16, P)
                    eng.wait_ge(*at(("ys", l)))
                    job("V", ("y", L, j, "x"), acc([(lambda o_: o_[:, 0:TX], w[:, k, :], ys[:, k, :])
                                                    for k in range(16)]))
                    used(("full", ("y", L, j, "x")))
                    if j > 1:
                        square_sum(L + 1, j - 2)
                square_sum(L + 1, KD - 2)
                square_sum(L + 1, KD - 1)

            pe.stage("end")
            rings[0] = NARROW
            for u in range(4):
                for half in range(2):
                    def mms(o_, u=u, half=half):
                        for k in range(4):
                            last = eng.transpose(o_[:, k * P:(k + 1) * P],
                                                 hT[:, half * 4 + k, TC + u * P:TC + (u + 1) * P], ident)
                        return last
                    eng.wait_ge(*at(("h ready", 4, "x")))
                    job("A", ("final", u, half), mms)


        @block.scalar
        def _(eng):
            act = Lane(m, eng, "act")
            act.stage("start")

            def fn(out_, in_, func, key=None, **kw):
                act.link(eng.activation(out_, in_, func, **kw), key)

            def evac(key, out_, lo, n, func=ACT.Copy, rows_=slice(0, P), **kw):
                eng.wait_ge(*at(("full", key)))
                fn(out_, bank_of[key][rows_, lo:lo + n], func, ("free", key), **kw)

            for k in range(KD):
                for g in ("x", "c"):
                    t0, n = SEG[g]
                    evac(("xT", k, g), xT[:, k, t0:t0 + n], 0, n)
            for s in range(NSET):
                evac(("cols", s), cols[:, s, :], 0, P)
            fn(cT[:, :], cols[:, 6, 8:32], ACT.Silu, ("cT",))

            def modulate(L, groups=range(12)):
                act.stage("modulation")
                s, ncol = (L, 2) if L < 2 else (L + 2, 1)
                for g in groups:
                    for j in range(2):
                        f = 2 * g + j
                        evac((("mod", L), g, j), modT[:, L % 2, f, 0:ncol], 0, ncol, ACT.Identity,
                             bias=col(s, B_MOD + f))

            def head_of_layer(L):
                act.stage("norm")
                sgs = list(enumerate(("x", "c")))[:2 if L < 2 else 1]
                for c_, sg in sgs:
                    t0, n = SEG[sg]
                    eng.wait_ge(*at(("ss", L, sg, KD - 1)))
                    fn(rstd[:, t0:t0 + n], ps[:, 4 + c_, 0:n], ACT.Sqrt, ("std", L, sg), scale=1.0 / D, bias=eps[:, :])
                for c_, sg in sgs if L < 4 else ():
                    t0, n = SEG[sg]
                    for k in range(KD):
                        eng.wait_ge(*at(("h scaled", L, sg, k)))
                        fn(hT[:, k, t0:t0 + n], hT[:, k, t0:t0 + n], ACT.Identity,
                           ("h ready", L, sg) if k == KD - 1 else None, bias=modT[:, L % 2, k, c_:c_ + 1])

            def tiles(name, l, dst, ntile, seg, func=ACT.Identity, b0=None, off=None, first=0):
                for j in range(first, first + ntile):
                    for sg in seg:
                        t0, n = SEG[sg]
                        t1 = off[sg] + PAD if off else t0
                        kw = {"bias": col(l, b0 + j)} if b0 is not None else {}
                        evac((name, l, j, sg), dst[:, j, t1:t1 + n], 0, n, func, **kw)

            def gate_first(l, p, d):
                act.stage("gla_gate")
                prev = (l, p, d)
                i = l * 4 + p * 2 + d
                if d:
                    eng.wait_ge(*at(("gla ki", (l, p, 0))))
                if d == 0 and i:
                    eng.wait_ge(*at(("gla out done", (i - 1) // 4, (i - 1) // 2 % 2)))
                for sg in ("x", "c"):
                    t0, n = SEG[sg]
                    evac(("z", prev, sg), bA[:, t0:t0 + n], 0, n, ACT.Identity, bias=col(l, G_B + 2 * d + p))
                fn(bE, bA, ACT.Abs)
                fn(bE, bE, ACT.Exp, scale=-1.0)
                fn(bE, bE, ACT.Ln, ("gla ln", prev), bias=1.0)

            def gate_second(l, p, d):
                act.stage("gla_gate")
                key = (l, p, d)
                eng.wait_ge(*at(("gla cum", key)))
                fn(bE, bC, ACT.Exp, ("gla e", key), scale=1.0 / 16)
                fn(bS, bS, ACT.Exp, ("gla es", key), scale=1.0 / 16)
                end = bC[:, 63:T:64] if d == 0 else bC[:, 0:T:64]
                fn(dec[d], end, ACT.Exp, ("gla dec", key), scale=1.0 / 16)

            def gate_third(l, p, d):
                act.stage("gla_gate")
                if d:
                    eng.wait_ge(*at(("gla core", (l, p, 0))))
                fn(bK, bC, ACT.Exp, ("gla ek", (l, p, d)), scale=-1.0 / 16)

            def kstate(l, p, d):
                act.stage("gla_core")
                key = (l, p, d)
                for half in range(2):
                    evac(("kst", key, half), kst[:, half * 3:half * 3 + 3, :], 0, 384)
                    m.mark(("kst", key, half), *m.at[("free", ("kst", key, half))])

            def out_norm(l, p):
                act.stage("gla_norm")
                for hh, buf in ((0, bA), (1, bK)):
                    eng.wait_ge(*at(("gla core", (l, p, 1))))
                    for sg in segs(l):
                        t0, n = SEG[sg]
                        src = ps[:, 4 + hh, 0:512] if sg == "x" else ps[:, 6, hh * 256:hh * 256 + 256]
                        fn(buf[:, t0:t0 + n], src, ACT.Copy)
                    m.mark(("gla o", l, 2 * p + hh), act.name, act.n[act.name])
                m.mark(("gla out read", l, p), act.name, act.n[act.name])
                for hh in range(2):
                    for sg in segs(l):
                        t0, n = SEG[sg]
                        evac(("gss", l, 2 * p + hh, sg), bE[:, t0:t0 + n], 0, n, ACT.Sqrt, scale=1.0 / P, bias=eps[:, :])

            att_no = [0]

            def attend(l, sg):
                act.stage("attend")
                nq, nkt = (4, 6) if sg == "x" else (2, 2)
                q0 = SEG[sg][0]
                n_all = 8 * nq
                for n_ in range(n_all + 2):
                    if n_ < n_all:
                        i = att_no[0] + n_
                        eng.wait_ge(*at(("nmax", i)))
                        if i >= 3:
                            eng.wait_ge(*at(("pT read", i - 3)))
                        b0 = 4 + 2 * (i % 2)
                        if sg == "x":
                            src = ps[:, b0:b0 + 2, 0:384]
                            dst = pr[:, i % 3, :].rearrange("p (a b) -> p a b", b=384)
                        else:
                            src, dst = ps[:, b0, 0:256], pr[:, i % 3, 0:256]
                        fn(dst, src, ACT.Exp, ("probs", i), bias=small[:, 40 + i % 2:41 + i % 2],
                           accum_out=small[:, 44 + i % 2:45 + i % 2])
                    if n_ >= 2 and (n_ - 2) % nq == nq - 1:
                        h = (n_ - 2) // nq
                        r = slice((h % 2) * 64, (h % 2) * 64 + 64)
                        evac(("o", l, h, sg), res[r, 8 + h // 2, q0:q0 + nq * P], 0, nq * P, rows_=r)
                att_no[0] += n_all

            for l in range(DEPTH):
                if l == 0:
                    modulate(0)
                head_of_layer(l)
                both = ["x", "c"]
                act.stage("proj1")
                for sg in both:
                    for d in range(2):
                        t0, n = SEG[sg]
                        r = slice(32 * d, 32 * d + RANK)
                        evac(("lr", l, sg, d), lr[r, t0:t0 + n], 0, n, ACT.Identity, rows_=r, bias=cols[r, l, B_LR:B_LR + 1])
                        m.mark(("lr", l, sg, d), *m.at[("free", ("lr", l, sg, d))])
                gate_first(l, 0, 0)
                act.stage("proj1")
                eng.wait_ge(*at(("up zero", l)))
                tiles("val", l, up, 4, segs(l), b0=B_IN, off=UO)
                tiles("glu", l, res[:, 0:4, :], 4, segs(l), ACT.Sigmoid, B_IN + 4)
                gate_second(l, 0, 0)
                gate_third(l, 0, 0)
                act.stage("proj1")
                tiles("gq", l, gq, 2, segs(l), b0=B_IN + C_GQ // P)
                tiles("gk", l, gk, 2, both, b0=B_IN + C_GK // P)
                for g in range(2):
                    for u in range(6):
                        evac(("gv", l, g, u), gv[:, u, g * 256:(g + 1) * 256], 0, 256)
                m.mark(("gla v", l), *m.at[("free", ("gv", l, 1, 5))])
                kstate(l, 0, 0)
                gate_first(l, 0, 1)
                act.stage("proj1")
                tiles("gg", l, res[:, 4:8, :], 1, segs(l), ACT.Silu, B_IN + C_GG // P)
                gate_second(l, 0, 1)
                act.stage("proj1")
                tiles("gg", l, res[:, 4:8, :], 3, segs(l), ACT.Silu, B_IN + C_GG // P, first=1)
                gate_third(l, 0, 1)
                kstate(l, 0, 1)
                act.stage("proj1")
                tiles("aq", l, res[:, 8:12, :], 2, segs(l), b0=B_AQ)
                out_norm(l, 0)
                gate_first(l, 1, 0)
                gate_second(l, 1, 0)
                gate_third(l, 1, 0)
                act.stage("proj1")
                tiles("aq", l, res[:, 8:12, :], 2, segs(l), b0=B_AQ, first=2)
                kstate(l, 1, 0)
                gate_first(l, 1, 1)
                modulate(l + 1, range(0, 3))
                gate_second(l, 1, 1)
                modulate(l + 1, range(3, 6))
                gate_third(l, 1, 1)
                kstate(l, 1, 1)
                act.stage("attn_proj")
                eng.wait_ge(*at(("gla ks", (l, 1, 1))))
                for g in range(2):
                    for sg in both:
                        t0, n = SEG[sg]
                        evac(("ak", l, g, sg), ak[:, g, t0:t0 + n], 0, n, ACT.Identity, bias=col(l, B_AK + g))
                for u in range(6):
                    evac(("av", l, 0, u), av[:, u, :], 0, P)
                m.mark(("av", l), *m.at[("free", ("av", l, 0, 5))])
                out_norm(l, 1)
                modulate(l + 1, range(6, 12))
                act.stage("attn_proj")
                for j, name in ((0, "k"), (1, "k"), (0, "q"), (1, "q"), (2, "q"), (3, "q")):
                    for sg in (both if name == "k" else segs(l)):
                        t0, n = SEG[sg]
                        evac(("hss", l, name, j, sg), rs[:, t0:t0 + n], 0, n, ACT.Sqrt, bias=eps[:, :])
                if l < DEPTH - 1:
                    attend(l, "c")
                attend(l, "x")
                act.stage("merge")
                tiles("ag", l, mg, 4, segs(l), ACT.Silu, B_AG)
                act.stage("conv_ln")
                for sg in segs(l):
                    t0, n = SEG[sg]
                    evac(("csum", l, sg), sq[:, t0:t0 + n], 0, n, scale=1.0 / 512)
                act.stage("merge")
                tiles("cgate", l, cg, 2, segs(l), ACT.Silu, B_IN + C_CGATE // P)
                act.stage("conv_ln")
                for sg in segs(l):
                    t0, n = SEG[sg]
                    evac(("csq", l, sg), rs[:, t0:t0 + n], 0, n, ACT.Sqrt, scale=1.0 / 512, bias=eps[:, :])
                act.stage("merge")
                tiles("cgate", l, cg, 2, segs(l), ACT.Silu, B_IN + C_CGATE // P, first=2)
                act.stage("conv_ln")
                for j in range(4):
                    for sg in segs(l):
                        t0, n = SEG[sg]
                        eng.wait_ge(*at(("conv scaled", l, j, sg)))
                        fn(res[:, j, t0:t0 + n], res[:, j, t0:t0 + n], ACT.Silu, ("conv act", l, j, sg),
                           scale=col(l, LN_G + j), bias=col(l, LN_B + j))
                act.stage("merge")
                eng.wait_ge(*at(("branch", l, 2)))
                eng.wait_ge(*at(("branch", l, 0)))
                for a in range(4):
                    if a:
                        eng.wait_ge(*at(("merged", l, 2 * a - 1)))
                    for b_ in range(3):
                        for j in range(2):
                            for sg in segs(l):
                                t0, n = SEG[sg]
                                evac(("mgate", l, a, b_, j, sg), mg[:, 2 * b_ + j, t0:t0 + n], 0, n, ACT.Sigmoid,
                                     bias=col(l, B_M + 8 * b_ + 2 * a + j))
                    for b_ in range(3):
                        for j in range(2):
                            for sg in segs(l):
                                t0, n = SEG[sg]
                                evac(("mout", l, a, b_, j, sg), my[:, 2 * b_ + j, t0:t0 + n], 0, n)

            act.stage("rotary")
            eng.wait_ge(*at(("angles", 0)))
            fn(rope[:, 1, :], WT, ACT.Sin)
            eng.wait_ge(*at(("angles", 1)))
            fn(rope[:, 0, :], zt, ACT.Sin, ("rotary",))

            for l in range(DEPTH):
                L = 2 + l
                s = L + 2
                head_of_layer(L)
                act.stage("cell_gates")
                evac(("if", l, 0), rI[0:4, :], 0, TX, ACT.Identity, rows_=slice(0, 4), bias=small[0:4, 24 + 2 * l:25 + 2 * l])
                evac(("if", l, 1), rF[0:4, :], 0, TX, ACT.Identity, rows_=slice(0, 4), bias=small[0:4, 25 + 2 * l:26 + 2 * l])
                fn(rM[0:4, :], rF[0:4, :], ACT.Abs)
                fn(rM[0:4, :], rM[0:4, :], ACT.Exp, scale=-1.0)
                fn(rM[0:4, :], rM[0:4, :], ACT.Ln, ("f ln", l), bias=1.0)
                act.stage("cell")

                def silu(n, j):
                    eng.wait_ge(*at(("conv2", l, n, j)))
                    q = qk2[n % 2]
                    last = j == 3
                    cb = col(s, 96 + (8 if j >= 2 else 0) + 2 * (n % 4) + j % 2)
                    fn(q[:, j, :], q[:, j, :], ACT.Silu, ("qk ready", l, n) if last else None, bias=cb)

                for kind, n, *x in steps2():
                    h, r, b = n % 4, n // 4, n % 2
                    if kind == "mod":
                        if l < DEPTH - 1:
                            modulate(L + 1, [x[0]])
                            act.stage("cell")
                    elif kind == "gates":
                        evac(("gcols", l), qcol[:, :, :, :], 0, 64)
                        fn(qcol[:, :, 0, :], qcol[:, :, 0, :], ACT.Exp)
                        fn(qcol[:, :, 1, :], qcol[:, :, 1, :], ACT.Exp, scale=-1.0)
                        fn(qcol[:, :, 2, :], qcol[:, :, 2, :], ACT.Exp, ("gate cols", l))
                        evac(("decay", l), decc[:, :, :], 0, 16, ACT.Exp)
                    elif kind == "qk":
                        j = x[0]
                        if n or l:
                            eng.wait_ge(*at(("pre read", l, n - 1, j) if n else ("pre read", l - 1, 7, j)))
                        if r:
                            evac(("qk", l, n, j), pre[:, j, 0:TX], 0, TX)
                        else:
                            evac(("qk", l, n, j), pre[:, j, TAPS2 - 1:TAPS2 - 1 + TX], 0, TX)
                            if j:
                                silu(n, j - 1)
                    elif kind == "v":
                        u = x[0]
                        if not r and u == 0:
                            silu(n, 3)
                        evac(("v2", l, n, u), vv[b][:, u, 0:HD2], 0, HD2)
                        if u == NCH - 1:
                            m.mark(("v2 ready", l, n), *m.at[("free", ("v2", l, n, u))])
                    elif kind == "gate":
                        b_, j = x
                        key = ("gate2", l, n, b_, j)
                        if b_ == 1:
                            if n or j:
                                eng.wait_ge(*at(("zt free", l, n, j)))
                            evac(key, zt, 0, TX, ACT.Silu)
                        else:
                            evac(key, ys[:, 2 * n + j, :], 0, TX, ACT.Silu if r else ACT.Sigmoid)
                    elif kind == "ub":
                        eng.wait_ge(*at(("wt logs", l, n)))
                        fn(WT, WT, ACT.Exp, ("wt", l, n))
                    elif kind == "scores":
                        c = x[0]
                        k = (l, n, c)
                        if c < NCH - 1:
                            scale = const[:, K_ZETA + h:K_ZETA + h + 1] if r else qcol[:, c, 2, h:h + 1]
                            if c:
                                eng.wait_ge(*at(("full", ("dC", (l, n, c - 1), 1))))
                            elif n:
                                eng.wait_ge(*at(("full", ("dC", (l, n - 1, NCH - 2), 1))))
                            if not r:
                                eng.wait_ge(*at(("gate cols scaled", l)))
                            evac(("kT", k), KW, 0, HD2, ACT.Copy, scale=scale)
                            m.mark(("kw", k), *m.at[("free", ("kT", k))])
                    elif kind == "values":
                        c = x[0]
                        k = (l, n, c)
                        if c or n:
                            eng.wait_ge(*at(("hn", (l, n, c - 1) if c else (l, n - 1, NCH - 1))))
                        W = HD2 if r else HD2 + 1
                        evac(("intra", k), NI[:, 0:W], 0, W)
                        eng.wait_ge(*at(("var", k)))
                        fn(small[:, 56:57], small[:, 55:56], ACT.Sqrt, ("sd", k), bias=eps[:, :])

            act.stage("end")
            head_of_layer(4)
            for u in range(4):
                for half in range(2):
                    evac(("final", u, half), xout[:, u, half * 512:(half + 1) * 512], 0, 512)


        @block.vector
        def _(eng):
            dve = Lane(m, eng, "dve")
            dve.stage("start")
            tt = lambda o_, a, b, op, key=None: dve.link(eng.tensor_tensor(o_, a, b, op), key)
            ts = lambda o_, a, s1, s2, op0, op1, key=None: dve.link(
                eng.tensor_scalar(o_, a, s1, s2, op0, op1) if s2 is not None else eng.tensor_scalar(o_, a, s1, None, op0), key)
            stt = lambda o_, a, s_, b, op0, op1, key=None: dve.link(
                eng.scalar_tensor_tensor(out=o_, in0=a, scalar=s_, in1=b, op0=op0, op1=op1), key)
            cp = lambda o_, a, key=None: dve.link(eng.tensor_copy(o_, a), key)
            rcp = lambda o_, a, key=None: dve.link(eng.reciprocal(o_, a), key)
            M_, A_, S_ = ALU.mult, ALU.add, ALU.subtract

            dve.link(eng.memset(eps[:, :], EPS))
            dve.link(eng.memset(rows, 0.0), "rows clear")
            eng.wait_ge(*at("vrow in"))
            eng.wait_ge(*at(("free", ("cols", NSET - 1))))
            for l in range(DEPTH):
                ts(small[:, 20 + l:21 + l], col(l, QN), 0.125, None, M_, None)

            def squares(L, k):
                for sg in ["x", "c"] if L < 2 else ["x"]:
                    t0, n = SEG[sg]
                    tt(hT[:, k, t0:t0 + n], xT[:, k, t0:t0 + n], xT[:, k, t0:t0 + n], M_, ("squares", L, sg, k))

            def norm(L):
                dve.stage("norm")
                s = L if L < 2 else L + 2
                sgs = list(enumerate(("x", "c")))[:2 if L < 2 else 1]
                if L < 4:
                    eng.wait_ge(*at(("free", (("mod", L), 11, 1))))
                    nc_ = 2 if L < 2 else 1
                    stt(gsT[:, :, 0:nc_], modT[:, L % 2, 8:16, 0:nc_], 1.0,
                        cols[:, s, 0:8].unsqueeze(2).broadcast_to([P, 8, nc_]), A_, M_)
                for c_, sg in sgs:
                    t0, n = SEG[sg]
                    eng.wait_ge(*at(("std", L, sg)))
                    rcp(rstd[:, t0:t0 + n], rstd[:, t0:t0 + n])
                    for k in range(KD):
                        g = gsT[:, k, c_:c_ + 1] if L < 4 else col(6, k)
                        stt(hT[:, k, t0:t0 + n], xT[:, k, t0:t0 + n], g, rstd[:, t0:t0 + n], M_, M_,
                            ("h scaled", L, sg, k))
                if L == 4:
                    m.mark(("h ready", 4, "x"), *m.at[("h scaled", 4, "x", KD - 1)])

            def gate_first(l, p, d):
                dve.stage("gla_gate")
                key = (l, p, d)
                eng.wait_ge(*at(("gla ln", key)))
                stt(bA, bA, 0.0, bE, ALU.min, S_)
                eng.wait_ge(*at("gscan in"))
                dve.link(eng.tensor_tensor_scan(bC, gscan[:, :], bA, 0.0, M_, A_))
                v3 = lambda x_: x_.rearrange("p (a b) -> p a b", b=64)
                last = bC[:, 63:T:64].unsqueeze(2).broadcast_to([P, 12, 64])
                if d == 0:
                    tt(v3(bS), last, v3(bC), S_, ("gla cum", key))
                else:
                    tt(v3(bE), last, v3(bC), S_)
                    eng.wait_ge(*at(("full", ("kst", (l, p, 0), 1))))
                    tt(bS, bC, bA, S_)
                    tt(bC, bE, bA, A_, ("gla cum", key))

            def gate_second(l, p, d):
                dve.stage("gla_gate")
                key = (l, p, d)
                t0 = 0 if l < DEPTH - 1 else TC
                eng.wait_ge(*at(("gla es", key)))
                eng.wait_ge(*at(("free", ("gk", l, 1, "c"))))
                tt(bS, gk[:, p, :], bS, M_, ("gla ks", key))
                if d:
                    eng.wait_ge(*at(("gla core", (l, p, 0))))
                for hh in range(2):
                    r = slice(hh * 64, hh * 64 + 64)
                    stt(bQz[hh][r, t0:T], gq[r, p, t0:T], 0.125, bE[r, t0:T], M_, M_, ("gla qi", key) if hh else None)
                eng.wait_ge(*at(("gla ek", key)))
                tt(bK, gk[:, p, :], bK, M_, ("gla ki", key))

            def core(l, p, d):
                dve.stage("gla_core")
                key = (l, p, d)
                order = [0, 1, 2, 3, 4, 5] if d == 0 else [1, 0, 5, 4, 3, 2]
                steps = [2 * u + c for u in order for c in ((0, 1) if d == 0 else (1, 0))]
                mask = const[:, K_CAUS:K_CAUS + P] if d == 0 else const[:, K_ANTI:K_ANTI + P]
                mask = mask.unsqueeze(1).broadcast_to([P, 2, P])
                gate_at = 1 if d == 0 else None

                def masked(ui):
                    u = order[ui]
                    if not ("c" if u < 2 else "x") in segs(l):
                        return
                    if ui >= 2 and ("c" if order[ui - 2] < 2 else "x") in segs(l):
                        eng.wait_ge(*at(("att used", key, order[ui - 2])))
                    k = ("att", key, u)
                    eng.wait_ge(*at(("full", k)))
                    tt(AM[:, ui % 2, :].rearrange("p (a b) -> p a b", b=P),
                       bank_of[k][:, 0:256].rearrange("p (a b) -> p a b", b=P), mask, M_, ("free", k))
                    m.mark(("att masked", key, u), *m.at[("free", k)])
                masked(0)
                for ui, u in enumerate(order):
                    if ui < 5:
                        masked(ui + 1)
                    if ui == gate_at:
                        gate_first(l, p, 1)
                        dve.stage("gla_core")
                    for c in ((0, 1) if d == 0 else (1, 0)):
                        ch = 2 * u + c
                        si = steps.index(ch)
                        if si == 11:
                            continue
                        k = ("con", key, si)
                        eng.wait_ge(*at(("full", k)))
                        eng.wait_ge(*at(("gla dec", key)))
                        if si >= 1:
                            eng.wait_ge(*at(("state used", key, si - 1)))
                        if si == 0:
                            cp(ST[:, 1, :], bank_of[k][:, 0:256], ("free", k))
                        else:
                            stt(ST[:, (si + 1) % 2, :], ST[:, si % 2, :], dec[d][:, ch:ch + 1], bank_of[k][:, 0:256],
                                M_, A_, ("free", k))
                        m.mark(("state", key, si + 1), *m.at[("free", k)])

            def out_norm(l, p):
                dve.stage("gla_norm")
                t0 = 0 if l < DEPTH - 1 else TC
                for hh, buf in ((0, bA), (1, bK)):
                    h = 2 * p + hh
                    eng.wait_ge(*at(("gla o", l, h)))
                    tt(bC[:, t0:T], buf[:, t0:T], buf[:, t0:T], M_, ("gla sq", l, h))
                    for sg in segs(l):
                        eng.wait_ge(*at(("free", ("gss", l, h, sg))))
                    rcp(bE[:, t0:T], bE[:, t0:T], ("gss read", l, h))
                    tt(buf[:, t0:T], buf[:, t0:T], bE[:, t0:T], M_)
                    stt(res[:, 4 + h, t0:T], buf[:, t0:T], col(l, G_N), res[:, 4 + h, t0:T], M_, M_,
                        ("gla out done", l, p) if hh else ("gla half done", l, p))

            att_no = [0]

            def attend(l, sg):
                dve.stage("attend")
                nq, nkt = (4, 6) if sg == "x" else (2, 2)
                n_all = 8 * nq
                for n_ in range(n_all + 2):
                    i = att_no[0] + n_
                    if n_ < n_all:
                        eng.wait_ge(*at(("scores", i)))
                        b0 = 4 + 2 * (i % 2)
                        src, ax = (ps[:, b0:b0 + 2, 0:384], AX.XY) if sg == "x" else (ps[:, b0, 0:256], AX.X)
                        if i >= 2:
                            eng.wait_ge(*at(("probs", i - 2)))
                        dve.link(eng.tensor_reduce(small[:, 40 + i % 2:41 + i % 2], src, ax, ALU.max, negate=True), ("nmax", i))
                    if 1 <= n_ <= n_all:
                        i = att_no[0] + n_ - 1
                        eng.wait_ge(*at(("probs", i)))
                        rcp(small[:, 48 + i % 2:49 + i % 2], small[:, 44 + i % 2:45 + i % 2])
                        ts(pr[:, i % 3, 0:nkt * P], pr[:, i % 3, 0:nkt * P], small[:, 48 + i % 2:49 + i % 2], None, M_, None,
                           ("probs norm", i))
                    if n_ >= 2:
                        i = att_no[0] + n_ - 2
                        qb = (n_ - 2) % nq
                        h = (n_ - 2) // nq
                        nb = 3 if sg == "x" else 2
                        hn = head_no[0]
                        if qb == 0 and hn >= 2:
                            eng.wait_ge(*at(("full", owners[hn - 2])))
                        for half in range(2 if sg == "x" else 1):
                            k = ("pT", i, half)
                            eng.wait_ge(*at(("full", k)))
                            cp(pt[:, hn % 2, half * nb:(half + 1) * nb, qb * P:(qb + 1) * P],
                               bank_of[k][:, 0:nb * P].rearrange("p (a b) -> p a b", b=P), ("free", k))
                        m.mark(("pT read", i), *m.at[("free", k)])
                        if qb == nq - 1:
                            m.mark(("pt", l, h, sg), *m.at[("free", k)])
                            owners.append(("o", l, h, sg))
                            head_no[0] += 1
                att_no[0] += n_all

            head_no, owners = [0], []

            for l in range(DEPTH):
                if l == 0:
                    dve.stage("squares")
                    eng.wait_ge(*at(("free", ("xT", KD - 1, "c"))))
                    for k in range(KD):
                        squares(0, k)
                norm(l)
                dve.link(eng.memset(bQz[0][64:128, :], 0.0))
                dve.link(eng.memset(bQz[1][0:64, :], 0.0))
                for p in range(2):
                    gate_first(l, p, 0)
                    gate_second(l, p, 0)
                    core(l, p, 0)
                    gate_second(l, p, 1)
                    core(l, p, 1)
                    out_norm(l, p)
                m.mark(("branch", l, 1), *m.at[("gla out done", l, 1)])
                dve.stage("rope")
                eng.wait_ge(*at("rope in"))
                for j, name in ((0, "k"), (1, "k"), (0, "q"), (1, "q"), (2, "q"), (3, "q")):
                    seg = ["x", "c"] if name == "k" else segs(l)
                    t0 = 0 if "c" in seg else TC
                    src = ak[:, j, :] if name == "k" else res[:, 8 + j, :]
                    g = col(l, KN) if name == "k" else small[:, 20 + l:21 + l]
                    for sg in seg:
                        eng.wait_ge(*at(("free", ("ak", l, j, sg) if name == "k" else ("aq", l, j, sg))))
                    tt(sq[:, t0:T], src[:, t0:T], src[:, t0:T], M_, ("hsq", l, name, j))
                    for sg in seg:
                        eng.wait_ge(*at(("free", ("hss", l, name, j, sg))))
                    rcp(rs[:, t0:T], rs[:, t0:T])
                    stt(src[:, t0:T], src[:, t0:T], g, rs[:, t0:T], M_, M_, ("normed", l, name, j))
                    k = ("rot", l, name, j)
                    eng.wait_ge(*at(("full", k)))
                    tt(tmp[:, 0:TX], bank_of[k][:, 0:TX], rope[:, 1, :], M_, ("free", k))
                    tt(src[:, TC:T], src[:, TC:T], rope[:, 0, :], M_)
                    tt(src[:, TC:T], src[:, TC:T], tmp[:, 0:TX], A_,
                       ("k ready", l, j) if name == "k" else ("q ready", l, j, "x"))
                    if name == "q":
                        m.mark(("q ready", l, j, "c"), *m.at[("q ready", l, j, "x")])
                if l < DEPTH - 1:
                    attend(l, "c")
                attend(l, "x")
                dve.stage("merge")
                t0 = 0 if l < DEPTH - 1 else TC
                last = segs(l)[-1]
                eng.wait_ge(*at(("free", ("ag", l, 3, last))))
                tt(res[:, 8:12, t0:T], res[:, 8:12, t0:T], mg[:, 0:4, t0:T], M_, ("branch", l, 2))
                dve.stage("conv_ln")
                for sg in segs(l):
                    t0, n = SEG[sg]
                    eng.wait_ge(*at(("free", ("csum", l, sg))))
                    mean = sq[:, t0:t0 + n].unsqueeze(1).broadcast_to([P, 4, n])
                    tt(res[:, 0:4, t0:t0 + n], res[:, 0:4, t0:t0 + n], mean, S_)
                    tt(mT[:, 0:4, t0:t0 + n], res[:, 0:4, t0:t0 + n], res[:, 0:4, t0:t0 + n], M_, ("conv squares", l, sg))
                for sg in segs(l):
                    t0, n = SEG[sg]
                    eng.wait_ge(*at(("free", ("csq", l, sg))))
                    rcp(rs[:, t0:t0 + n], rs[:, t0:t0 + n])
                for j in range(4):
                    for sg in segs(l):
                        t0, n = SEG[sg]
                        tt(res[:, j, t0:t0 + n], res[:, j, t0:t0 + n], rs[:, t0:t0 + n], M_, ("conv scaled", l, j, sg))
                dve.stage("merge")
                t0 = 0 if l < DEPTH - 1 else TC
                eng.wait_ge(*at(("free", ("cgate", l, 3, last))))
                eng.wait_ge(*at(("conv act", l, 3, last)))
                tt(res[:, 0:4, t0:T], res[:, 0:4, t0:T], cg[:, :, t0:T], M_, ("branch", l, 0))
                for a in range(4):
                    eng.wait_ge(*at(("free", ("mgate", l, a, 2, 1, last))))
                    for b_ in range(3):
                        eng.wait_ge(*at(("free", ("mout", l, a, b_, 1, last))))
                        tt(my[:, 2 * b_:2 * b_ + 2, t0:T], my[:, 2 * b_:2 * b_ + 2, t0:T], mg[:, 2 * b_:2 * b_ + 2, t0:T], M_)
                    tt(my[:, 0:2, t0:T], my[:, 0:2, t0:T], my[:, 2:4, t0:T], A_)
                    tt(mT[:, 2 * a:2 * a + 2, t0:T], my[:, 0:2, t0:T], my[:, 4:6, t0:T], A_, ("merged", l, 2 * a))
                    m.mark(("merged", l, 2 * a + 1), *m.at[("merged", l, 2 * a)])
                for j in range(KD):
                    for sg in segs(l):
                        t0, n = SEG[sg]
                        k = ("y", l, j, sg)
                        eng.wait_ge(*at(("full", k)))
                        c_ = 0 if sg == "x" else 1
                        stt(xT[:, j, t0:t0 + n], bank_of[k][:, 0:n], modT[:, l % 2, 16 + j, c_:c_ + 1],
                            xT[:, j, t0:t0 + n], M_, A_, ("free", k))
                    squares(l + 1, j)

            dve.stage("rotary")
            eng.wait_ge(*at("positions in"))
            C1, C2_, C3 = 6.28125, 0.0019350051879882812, 3.0199157663446332e-07
            PI = float(np.nextafter(np.float32(np.pi), np.float32(0)))
            cp(WT, posi[:, :])
            ts(WT, WT, const[:, K_FREQ:K_FREQ + 1], None, M_, None)
            ts(UBs, WT, float(1 / (2 * np.pi)), 12582912.0, M_, A_)
            ts(UBs, UBs, -12582912.0, None, A_, None)
            for c_ in (C1, C2_, C3):
                stt(WT, UBs, -c_, WT, M_, A_)
            ts(WT, WT, PI, -PI, ALU.min, ALU.max, ("angles", 0))
            ts(zt, WT, HALF_PI, None, A_, None)
            ts(UBs, zt, PI, -2 * float(np.pi), ALU.is_gt, M_)
            tt(zt, zt, UBs, A_)
            ts(zt, zt, PI, -PI, ALU.min, ALU.max, ("angles", 1))
            dve.link(eng.memset(gscan[0:4, 0:TX], 1.0))
            dve.link(eng.memset(gscan[0:4, 0:TX:CH], 0.0))
            for b in range(2):
                dve.link(eng.memset(vv[b][:, :, HD2:HD2 + 1], 1.0))
            dve.link(eng.memset(small[0:4, 32:33], 0.0))
            dve.link(eng.memset(pre[:, :, 0:TAPS2 - 1], 0.0), ("pre zero", 0))

            for l in range(DEPTH):
                L = 2 + l
                s = L + 2
                norm(L)
                dve.stage("cell_gates")
                R = slice(0, 4)
                v3 = lambda x_: x_[R, :].rearrange("p (a b) -> p a b", b=CH)
                eng.wait_ge(*at(("f ln", l)))
                eng.wait_ge(*at(("free", ("if", l, 0))))
                stt(rF[R, :], rF[R, :], 0.0, rM[R, :], ALU.min, S_)
                dve.link(eng.tensor_tensor_scan(rM[R, :], rF[R, :], rI[R, :], 0.0, A_, ALU.max))
                dve.link(eng.tensor_tensor_scan(rB[R, :], gscan[R, 0:TX], rF[R, :], 0.0, M_, A_))
                tt(rU[R, :], rB[R, :], rM[R, :], S_)
                tt(rW[R, :], rI[R, :], rB[R, :], S_)
                cp(small[R, 33:36], rM[R, CH - 1:TX - 1:CH])
                tt(v3(rI), v3(rU), small[R, 32:36].unsqueeze(2).broadcast_to([4, NCH, CH]), A_)
                tt(v3(rF), v3(rW), rU[R, CH - 1:TX:CH].unsqueeze(2).broadcast_to([4, NCH, CH]), A_, ("gate rows", l))
                dve.stage("cell")
                if l:
                    eng.wait_ge(*at(("pre read", l - 1, 7, 3)))
                    dve.link(eng.memset(pre[:, :, 0:TAPS2 - 1], 0.0), ("pre zero", l))

                def finish(n, c):
                    h, r = n % 4, n // 4
                    k = (l, n, c)
                    W = HD2 if r else HD2 + 1
                    eng.wait_ge(*at(("free", ("intra", k))))
                    src = NI
                    if c:
                        kk = ("inter", k)
                        eng.wait_ge(*at(("full", kk)))
                        w = const[:, K_XI + h:K_XI + h + 1] if r else qcol[:, c, 0, h:h + 1]
                        stt(NM[:, 0:W], bank_of[kk][:, 0:W], w, NI[:, 0:W], M_, A_, ("free", kk))
                        src = NM
                    if c < NCH - 1:
                        for j in range(2):
                            kk = ("dC", k, j)
                            eng.wait_ge(*at(("full", kk)))
                            eng.wait_ge(*at(("free", ("decay", l))))
                            g = const[:, K_GCH + h:K_GCH + h + 1] if r else decc[:, h, c:c + 1]
                            if c == 0:
                                cp(C2[:, j, 0:W], bank_of[kk][:, 0:W], ("free", kk))
                            else:
                                stt(C2[:, j, 0:W], C2[:, j, 0:W], g, bank_of[kk][:, 0:W], M_, A_, ("free", kk))
                            m.mark(("C", k, j), *m.at[("free", kk)])
                    if n or c:
                        eng.wait_ge(*at(("full", ("hT", (l, n, c - 1) if c else (l, n - 1, NCH - 1)))))
                    if not r:
                        ts(small[:, 60:61], src[:, HD2:HD2 + 1], -1.0, qcol[:, c, 1, h:h + 1], M_, ALU.max)
                        tt(small[:, 60:61], small[:, 60:61], src[:, HD2:HD2 + 1], ALU.max)
                        rcp(small[:, 60:61], small[:, 60:61])
                        ts(HN, src[:, 0:HD2], small[:, 60:61], None, M_, None)
                        src = HN
                    dve.link(eng.bn_stats(small[:, 64:70], src[:, 0:HD2]))
                    dve.link(eng.bn_aggr(small[:, 54:56], small[:, 64:70]), ("var", k))
                    eng.wait_ge(*at(("sd", k)))
                    rcp(small[:, 57:58], small[:, 56:57])
                    ts(HN, src[:, 0:HD2], small[:, 54:55], small[:, 57:58], S_, M_, ("hn", k))

                for kind, n, *x in steps2():
                    h, r = n % 4, n // 4
                    if kind == "gates":
                        eng.wait_ge(*at(("gate cols", l)))
                        ts(qcol[:, :, 2, :], qcol[:, :, 2, :], 1.0 / 16, None, M_, None, ("gate cols scaled", l))
                    elif kind == "ub":
                        kk = ("ub", l, n)
                        eng.wait_ge(*at(("full", kk)))
                        for c in range(NCH):
                            stt(WT[:, c * P:(c + 1) * P], bank_of[kk][:, c * P:(c + 1) * P], qcol[:, c, 3, h:h + 1],
                                const[:, K_NEG:K_NEG + P], A_, A_, ("free", kk) if c == NCH - 1 else None)
                        m.mark(("wt logs", l, n), *m.at[("free", kk)])
                    elif kind == "scores":
                        c = x[0]
                        k = (l, n, c)
                        kk = ("s2", k)
                        if n or c:
                            eng.wait_ge(*at(("full", ("intra", (l, n, c - 1) if c else (l, n - 1, NCH - 1)))))
                        if not r:
                            eng.wait_ge(*at(("wt", l, n)))
                        w = const[:, K_DEC + h * P:K_DEC + (h + 1) * P] if r else WT[:, c * P:(c + 1) * P]
                        eng.wait_ge(*at(("full", kk)))
                        stt(SW, bank_of[kk][:, 0:P], 1.0 / 16, w, M_, M_, ("free", kk))
                        m.mark(("sw", k), *m.at[("free", kk)])
                    elif kind == "values":
                        finish(n, x[0])
                    elif kind == "turn":
                        c = x[0]
                        k = (l, n, c)
                        kk = ("hT", k)
                        eng.wait_ge(*at(("full", kk)))
                        eng.wait_ge(*at(("gates ready", l, n)))
                        for j in range(2):
                            y_ = ys[:, 2 * n + j, c * P:(c + 1) * P]
                            stt(y_, bank_of[kk][:, j * P:(j + 1) * P], col(s, 112 + 2 * n + j), y_, M_, M_,
                                ("free", kk) if j else None)
                        if n == 7 and c == NCH - 1:
                            m.mark(("ys", l), *m.at[("free", kk)])
                dve.stage("out2")
                for j in range(KD):
                    k = ("y", L, j, "x")
                    eng.wait_ge(*at(("full", k)))
                    stt(xT[:, j, TC:T], bank_of[k][:, 0:TX], modT[:, L % 2, 16 + j, 0:1], xT[:, j, TC:T], M_, A_, ("free", k))
                    squares(L + 1, j)
            norm(4)


        @block.gpsimd
        def _(eng):
            pool = Lane(m, eng, "pool")
            pool.stage("conv")

            def add_product(dst, src, w, scratch):
                pool.link(eng.tensor_scalar(scratch, src, w, 0.0, ALU.mult, ALU.add))
                pool.link(eng.tensor_tensor(dst, dst, scratch, ALU.add))

            for l in range(DEPTH):
                if l:
                    eng.wait_ge(*at(("merged", l - 1, 7)))
                for b0 in (0, TC + PAD, TC + 2 * PAD, TC + TX + 3 * PAD):
                    pool.link(eng.memset(up[:, :, b0:b0 + PAD], 0.0), ("up zero", l) if b0 > TC + TX else None)
                for j in range(4):
                    for sg in segs(l):
                        t0, n = SEG[sg]
                        u0 = UO[sg] + PAD
                        eng.wait_ge(*at(("free", ("glu", l, j, sg))))
                        pool.link(eng.tensor_tensor(up[:, j, u0:u0 + n], up[:, j, u0:u0 + n], res[:, j, t0:t0 + n], ALU.mult))
                        for t in range(TAPS):
                            src = up[:, j, UO[sg] + t:UO[sg] + t + n]
                            w = cols[:, 2 + l, 4 * t + j:4 * t + j + 1]
                            dst = res[:, j, t0:t0 + n]
                            if t == 0:
                                pool.link(eng.tensor_scalar(dst, src, w, col(l, CW_B + j), ALU.mult, ALU.add))
                            else:
                                add_product(dst, src, w, posi[:, 0:n].bitcast(F32))
                m.mark(("conv", l), pool.name, pool.n[pool.name])
            for l in range(DEPTH):
                L = 2 + l
                s = L + 2
                pool.stage("cell")
                for kind, n, *x in steps2():
                    h, r, b = n % 4, n // 4, n % 2
                    q = qk2[b]
                    if kind == "qk":
                        j = x[0]
                        eng.wait_ge(*at(("free", ("qk", l, n, j))))
                        if n >= 2:
                            eng.wait_ge(*at(("full", ("hT", (l, n - 2, NCH - 1)))))
                        if not r:
                            eng.wait_ge(*at(("pre zero", l)))
                            for t in range(TAPS2):
                                src = pre[:, j, t:t + TX]
                                w = col(s, 32 + 16 * t + (8 if j >= 2 else 0) + 2 * h + j % 2)
                                if t == 0:
                                    pool.link(eng.tensor_scalar(q[:, j, :], src, w, None, ALU.mult))
                                else:
                                    add_product(q[:, j, :], src, w, UBs)
                            m.mark(("conv2", l, n, j), pool.name, pool.n[pool.name])
                            m.mark(("pre read", l, n, j), pool.name, pool.n[pool.name])
                        elif j % 2:
                            eng.wait_ge(*at(("rotary",)))
                            a, b_ = pre[:, j - 1, 0:TX], pre[:, j, 0:TX]
                            for out_, x1, x2, op in ((q[:, j - 1, :], a, b_, ALU.subtract), (q[:, j, :], b_, a, ALU.add)):
                                pool.link(eng.tensor_tensor(out_, x1, rope[:, 0, :], ALU.mult))
                                pool.link(eng.tensor_tensor(UBs, x2, rope[:, 1, :], ALU.mult))
                                pool.link(eng.tensor_tensor(out_, out_, UBs, op))
                            for jj in (j - 1, j):
                                m.mark(("pre read", l, n, jj), pool.name, pool.n[pool.name])
                            if j == 3:
                                m.mark(("qk ready", l, n), pool.name, pool.n[pool.name])
                    elif kind == "gate" and not r:
                        b_, j = x
                        if b_ == 1:
                            eng.wait_ge(*at(("free", ("gate2", l, n, 1, j))))
                            pool.link(eng.tensor_tensor(ys[:, 2 * n + j, :], ys[:, 2 * n + j, :], zt, ALU.mult))
                            if j == 0:
                                m.mark(("zt free", l, n, 1), pool.name, pool.n[pool.name])
                            else:
                                m.mark(("gates ready", l, n), pool.name, pool.n[pool.name])
                                if n < 3:
                                    m.mark(("zt free", l, n + 1, 0), pool.name, pool.n[pool.name])
                    elif kind == "gate" and x[1] == 1:
                        eng.wait_ge(*at(("free", ("gate2", l, n, 0, 1))))
                        m.mark(("gates ready", l, n), *m.at[("free", ("gate2", l, n, 0, 1))])


        @block.sync
        def _(eng):
            def sig(name, n, key):
                m.mark(key, name, 16 * n)

            eng.dma_start(const[:, :], I["const"]).then_inc(m.sem("const_in"), 16)
            sig("const_in", 1, "const in")
            eng.dma_start(xin[:, 2:6, :], I["x"][0].rearrange("(u p) d -> p u d", p=P)).then_inc(m.sem("x_in"), 16)
            eng.dma_start(xin[:, 0:2, :], I["ctx"][0].rearrange("(u p) d -> p u d", p=P)).then_inc(m.sem("x_in"), 16)
            nrow = 0
            sets = [(s, set1(s), set1h(s)) for s in range(2)] + [(4 + s, set2(s), []) for s in range(2)]
            sets.append((6, [(I["final_g_2"], 0, 8), (I["c"][0], 8, 8), (I["c_ctx"], 16, 8), (I["c_2"][0], 24, 8)], []))
            eng.wait_ge(*at("rows clear"))
            for s in range(2):
                eng.dma_start(rows[0:4 * TAPS, 2 + s, :], I["conv_dw_w"][s].rearrange("t (j p) -> (t j) p", p=P))\
                   .then_inc(m.sem("rows_in"), 16)
                nrow += 1
            for s, whole, halves in sets:
                for v, r0, n in whole:
                    eng.dma_start(rows[r0:r0 + n, s, :], v.rearrange("(r p) -> r p", p=P)).then_inc(m.sem("rows_in"), 16)
                    nrow += 1
                for v, r0 in halves:
                    for hf in range(2):
                        eng.dma_start(rows[r0:r0 + 1, s, hf * 64:hf * 64 + 64], v.unsqueeze(0)).then_inc(m.sem("rows_in"), 16)
                        nrow += 1
                if s < 2:
                    for d in range(2):
                        eng.dma_start(rows[B_LR:B_LR + 1, s, 32 * d:32 * d + RANK],
                                      I["b_in"][s, C_LR + RANK * d:C_LR + RANK * (d + 1)].unsqueeze(0)).then_inc(m.sem("rows_in"), 16)
                        nrow += 1
            sig("rows_in", nrow, "rows in")
            eng.wait_ge(m.sem("const_in"), 16)
            nv = 0
            for l in range(DEPTH):
                eng.dma_start(const[32 * (l + 1):32 * (l + 1) + 1, K_SEL:K_SEL + 512], I["b_in"][l, C_GV:C_GV + 512].unsqueeze(0))\
                   .then_inc(m.sem("vrow_in"), 16)
                eng.dma_start(const[96:97, K_SEL + l * P:K_SEL + (l + 1) * P], I["b_in"][l, C_AV:C_AV + P].unsqueeze(0))\
                   .then_inc(m.sem("vrow_in"), 16)
                for g, nm in enumerate(("b_igate_2", "b_fgate_2")):
                    eng.dma_start(small[0:4, 24 + 2 * l + g:25 + 2 * l + g], I[nm][l].unsqueeze(1)).then_inc(m.sem("vrow_in"), 16)
                nv += 4
            sig("vrow_in", nv, "vrow in")
            eng.dma_start(gscan[:, :], I["gscan"]).then_inc(m.sem("gscan_in"), 16)
            sig("gscan_in", 1, "gscan in")
            eng.dma_start(rope[:, :, :], I["rope"]).then_inc(m.sem("rope_in"), 16)
            sig("rope_in", 1, "rope in")

            def gate_weights(l):
                if l:
                    eng.wait_ge(*at(("full", ("z", (l - 1, 1, 1), "c"))))
                for d in range(2):
                    eng.dma_start(gup[32 * d:32 * d + RANK, :], I["gla_w_gate"][l, d]).then_inc(m.sem("gup_in"), 16)
                sig("gup_in", 2 * (l + 1), ("gup", l))

            gate_weights(0)
            for n, (parts, _) in enumerate(plan):
                if n >= RING:
                    eng.wait_ge(*at(plan[n - RING][1]))
                for dst, view in parts:
                    eng.dma_start(dst, view).then_inc(m.sem(f"w_slot{n % RING}"), 16)
                if n == starts[1]:
                    gate_weights(1)
                if n == starts[2]:
                    eng.wait_ge(*at(("conv", 1)))
                    eng.dma_start(posi[:, :], I["positions_2"].broadcast_to([P, TX])).then_inc(m.sem("pos_in"), 16)
                    sig("pos_in", 1, "positions in")
            for u in range(4):
                eng.wait_ge(*at(("free", ("final", u, 1))))
                eng.dma_start(out[0, u * P:(u + 1) * P, :], xout[:, u, :]).then_inc(m.sem("out_done"), 16)
            eng.wait_ge(m.sem("out_done"), 16 * 4)

        return m.at


_INS = ['x', 'c', 'ctx', 'c_ctx', 'norm_g', 'w_mod', 'b_mod', 'w_in', 'b_in', 'conv_dw_w', 'conv_dw_b', 'conv_ln_g',
        'conv_ln_b', 'w_conv_out', 'gla_w_gate', 'gla_b_gate', 'gla_norm_g', 'w_gla_out', 'q_norm_g', 'k_norm_g',
        'w_attn_out', 'w_out', 'c_2', 'positions_2', 'w_ada_2', 'b_ada_2', 'norm_g_2', 'w_in_2', 'conv_w_2', 'conv_b_2',
        'b_igate_2', 'b_fgate_2', 'gn_m_2', 'gn_r_2', 'w_out_2', 'final_g_2']


def kernel(**inputs):
    import numpy as _np
    import concourse.bacc as _bacc
    from concourse import mybir as _mybir
    from concourse.bass_utils import run_bass_kernel_spmd as _run

    arrays = {}
    const, gscan, rope, _ = shape_constants()
    given = [(n, _np.ascontiguousarray(inputs[n])) for n in _INS] + [("const", const), ("gscan", gscan), ("rope", rope)]
    for name, a in given:
        arrays[f"in_{name}"] = a

    def program(known):
        nc = _bacc.Bacc("TRN2", target_bir_lowering=False, num_devices=1)
        args = {name: nc.dram_tensor(f"in_{name}", a.shape, _mybir.dt.from_np(a.dtype), kind="ExternalInput").ap()
                for name, a in given}
        out = nc.dram_tensor("out_0", (1, TX, D), F32, kind="ExternalOutput").ap()
        return nc, write_program(nc, args, out, known)

    nc, _ = program(program(None)[1])
    r = _run(nc, [arrays], core_ids=[0])
    return r.results[0]["out_0"]
```

```python
from contextlib import ExitStack
from itertools import chain

import numpy as np

import concourse.bass as bass
from concourse import mybir

F32 = mybir.dt.float32
I32 = mybir.dt.int32
ALU = mybir.AluOpType
ACT = mybir.ActivationFunctionType
AX = mybir.AxisListType

P = 128
D = 1024
KD = D // P
TC, TX = 256, 512
T = TC + TX
DEPTH = 2
EPS = 1e-6
HALF_PI = float(np.pi / 2)

C_VAL, C_GLU, C_CGATE, C_GQ, C_GK, C_GV, C_GG, C_LR, C_AQ, C_AK, C_AV, C_AG, C_M = (
    0, 512, 1024, 1536, 1792, 2048, 2560, 3072, 3104, 3616, 3744, 3872, 4384)
TAPS, PAD = 31, 15
GLA_CHUNK = 64
RANK = 16
C_MI, C_RQ = 5120, 5128
HEADS2, HD2, TAPS2 = 4, 256, 4
CH = 128
NCH = TX // CH
HEAD_TILES = [("k", 0), ("k", 1), ("q", 0), ("q", 1), ("q", 2), ("q", 3)]
OUT_EARLY = 3

K_ID, K_HALF, K_ONE, K_PERM, K_CAUS, K_ANTI, K_NEG, K_DEC, K_XI, K_ZETA, K_GCH, K_FREQ, K_SEL, K_END = np.cumsum(
    [0, 128, 128, 128, 128, 128, 128, 128, 512, 4, 4, 4, 1, 512]).tolist()


def shape_constants():
    c = np.zeros((P, K_END), np.float32)
    i = np.arange(P)
    c[:, K_ID:K_ID + P] = np.eye(P)
    c[:, K_HALF:K_HALF + P] = (i[:, None] // 64 == i[None] // 64) / 64.0
    c[:, K_ONE:K_ONE + P] = 1.0
    for p in range(P):
        if p % 32 < 16:
            c[p + 16, K_PERM + p] = -1.0
        else:
            c[p - 16, K_PERM + p] = 1.0
    same = i[:, None] // GLA_CHUNK == i[None] // GLA_CHUNK
    c[:, K_CAUS:K_CAUS + P] = same & (i[:, None] <= i[None])
    c[:, K_ANTI:K_ANTI + P] = same & (i[:, None] >= i[None])
    c[:, K_NEG:K_NEG + P] = np.where(i[:, None] <= i[None], 0.0, -1e30)
    lg = np.log(1.0 - 2.0 ** (-5.0 - np.arange(HEADS2)))
    for h in range(HEADS2):
        d = i[None] - i[:, None]
        c[:, K_DEC + h * P:K_DEC + (h + 1) * P] = np.where(d >= 0, np.exp(lg[h] * np.maximum(d, 0)), 0.0)
        c[:, K_XI + h] = np.exp(lg[h] * (i + 1.0))
        c[:, K_ZETA + h] = np.exp(lg[h] * (CH - 1.0 - i)) / 16.0
        c[:, K_GCH + h] = np.exp(lg[h] * CH)
        c[h, K_SEL + h * P:K_SEL + (h + 1) * P] = 1.0
    c[:, K_FREQ] = (1.0 / (np.float32(10000.0) ** np.linspace(0.0, 1.0, P, dtype=np.float32))).astype(np.float32)
    m = np.ones((P, T), np.float32)
    m[:, ::GLA_CHUNK] = 0.0
    t = np.arange(TX)
    f = (np.float32(10000.0) ** (-np.arange(16, dtype=np.float32) / 16)).astype(np.float32)
    pos = np.where((i[:, None] % 64) < 32, t[None] // 64, t[None] % 64).astype(np.float32)
    ang = pos * f[i % 16][:, None]
    rope = np.stack([np.cos(ang), np.sin(ang)], 1).astype(np.float32)
    return c, m, rope


def mod_groups(l, a):
    todo = ([(0, g) for g in range(8, 12)] if l == 0 else []) + [(l + 1, g) for g in range(12)]
    n = len(todo) // 4
    return todo[a * n:(a + 1) * n]


def steps2():
    def proj(n):
        yield [("load", n, 0), ("qk", n, 0)]
        yield [("qk", n, 1)] + [("mod", n, 2 * n - 3)] * (2 <= n < 8)
        yield [("load", n, 1), ("qk", n, 2)]
        yield [("qk", n, 3)]
        yield [("load", n, 2), ("v", n, 0), ("v", n, 1)]
        yield [("v", n, 2), ("v", n, 3)] + [("mod load", n, 2 * n - 2)] * (1 <= n < 7)
        for b in range(1 if n // 4 else 2):
            yield [("load", n, 3 + b), ("gate", n, b, 0)]
            yield [("gate", n, b, 1)] + [("mod", n, 2 * n - 2), ("mod load", n, 2 * n - 1)] * (b == 0 and 1 <= n < 7)

    def core(n):
        for c in range(NCH):
            yield ([("ub", n)] if c == 0 and n < 4 else []) + [("scores", n, c)] + ([("turn", n, c - 1)] if c else [])
            yield [("values", n, c)]
        yield [("turn", n, NCH - 1)]

    for s in proj(0):
        yield from s
    yield ("gates", 0)
    for n in range(1, HEADS2 * 2 + 1):
        a = list(proj(n)) if n < HEADS2 * 2 else []
        b = list(core(n - 1))
        if n == HEADS2 * 2:
            a = [[("out", n, j)] for j in range(OUT_EARLY)]
        for i in range(max(len(a), len(b))):
            for part in (b, a):
                if i < len(part):
                    yield from part[i]


class Counts:

    def __init__(self, nc, ctx, known):
        self.nc, self.ctx, self.known, self.at, self.sems = nc, ctx, known, {}, {}

    def sem(self, name):
        if name not in self.sems:
            self.sems[name] = self.ctx.enter_context(self.nc.semaphore(name))
        return self.sems[name]

    def mark(self, key, name, count):
        assert key not in self.at, key
        self.at[key] = (name, count)

    def reached(self, key):
        if self.known is None:
            return self.sem("draft"), 1
        name, count = self.known[key]
        return self.sem(name), count


class Lane:

    def __init__(self, counts, eng, who):
        self.m, self.eng, self.who, self.name, self.n = counts, eng, who, None, {}

    def stage(self, name):
        self.name = f"{self.who}_{name}"
        self.n.setdefault(self.name, 0)

    def tell(self, key=None):
        self.n[self.name] += 1
        if key is not None:
            self.m.mark(key, self.name, self.n[self.name])
        return self.m.sem(self.name), 1

    def link(self, ins, key=None):
        ins.then_inc(*self.tell(key))
        self.eng.wait_ge(self.m.sem(self.name), self.n[self.name])


def write_program(nc, I, out, known):
    with ExitStack() as ctx:
        def sb(name, shape, dt=F32):
            return ctx.enter_context(nc.sbuf_tensor(name, shape, dt))

        m = Counts(nc, ctx, known)
        at = m.reached

        const = sb("const", [P, K_END])
        xT = sb("xT", [P, KD, T])
        hT = sb("hT", [P, KD, T])
        RING, SLOT = 4, 2048
        wring = sb("wring", [P, RING, SLOT])
        NSET = 7
        FIRST_SETS, LATER_SETS = [6, 0], [1, 2, 3, 4, 5]
        cols = sb("cols", [P, NSET, P])
        cT = sb("cT", [P, 24])
        modT = sb("modT", [P, 2, 24, 2])
        posi = sb("posi", [P, TX], I32)
        gsT = sb("gsT", [P, KD, 2])
        rstd = sb("rstd", [P, T])
        rope = sb("rope", [P, 2, TX])
        eps = sb("eps", [P, 1])
        small = sb("small", [P, 96])
        A0, A1, A2 = 12 * T, 13312, 3328
        arena = sb("arena", [P, A0 + A1 + A2])

        def cut(at, *shape):
            n = int(np.prod(shape))
            v = arena[:, at:at + n]
            if len(shape) == 2:
                v = v.rearrange("p (a b) -> p a b", b=shape[1])
            elif len(shape) == 3:
                v = v.rearrange("p (a b c) -> p a b c", b=shape[1], c=shape[2])
            return v, at + n

        res, _ = cut(0, 12, T)
        gq, o = cut(A0, 2, T)
        gk, o = cut(o, 2, T)
        gv, o = cut(o, 6, 512)
        lr, o = cut(o, T)
        bA, o = cut(o, T)
        bC, o = cut(o, T)
        bE, o = cut(o, T)
        bQ, o = cut(o, T)
        bK, o = cut(o, T)
        bS, o = cut(o, T)
        kst, o = cut(o, 6, P)
        ST, o = cut(o, 2, 256)
        AM, o = cut(o, 2, 256)
        assert o <= A0 + A1, o
        bQz = [bQ, rstd[:, :]]
        dec = [small[:, 0:12], small[:, 72:84]]
        gup = sb("gup", [P, 256])
        gscan = sb("gscan", [P, T])
        ak, o = cut(A0, 2, T)
        av, o = cut(o, 6, P)
        ag, o = cut(o, 4, T)
        pr, o = cut(o, 3, T)
        pt, o = cut(o, 3, 6, P)
        sq, rs = [None] * 2, [None] * 2
        sq[0], o = cut(o, T)
        rs[0], o = cut(o, T)
        tmp, o = cut(o, T)
        assert o <= A0 + A1, o
        sq[1], rs[1] = pr[:, 0, :], pr[:, 1, :]
        UW = TC + TX + 4 * PAD
        up, o = cut(A0 + A1, 4, UW)
        UO = {"c": 0, "x": TC + 2 * PAD}
        cg, _ = cut(A0 + A1, 4, T)
        mT, o = cut(A0, KD, T)
        mg, o = cut(o, 6, T)
        my, o = cut(o, 6, T)
        assert o <= A0 + A1 + A2, o
        md, o = cut(A0 + 20 * T, 2, 512)
        assert o <= A0 + A1 + A2, o
        md_first, _ = cut(A0 + 15 * T, 2, 512)
        xin, _ = cut(A0, 6, D)
        rows, _ = cut(0, NSET, P)
        xout, _ = cut(0, 4, D)
        ys, o = cut(0, 16, TX)
        pre, o = cut(o, 4, TX + TAPS2 - 1 + 1)
        qk2, vv = [None] * 2, [None] * 2
        for b in range(2):
            qk2[b], o = cut(o, 4, TX)
            vv[b], o = cut(o, NCH, 260)
        zt, o = cut(o, TX)
        WT, o = cut(o, TX)
        SW, o = cut(o, P)
        NI, o = cut(o, 260)
        NM, o = cut(o, 260)
        HN, o = cut(o, 256)
        KW, o = cut(o, 256)
        C2, o = cut(o, 2, 260)
        UBs, o = cut(o, TX)
        rI, o = cut(o, TX)
        rF, o = cut(o, TX)
        rM, o = cut(o, TX)
        rB, o = cut(o, TX)
        rU, o = cut(o, TX)
        rW, o = cut(o, TX)
        assert o <= A0 + A1 + A2, (o, A0 + A1 + A2)
        qcol = sb("qcol", [P, NCH, 4, 4])
        decc = sb("decc", [P, 4, NCH])

        ps = ctx.enter_context(nc.psum_tensor("ps", [P, 8, 512], F32))
        bank = [ps[:, i, :] for i in range(8)]
        NARROW, WIDE = {"A": [0, 1], "V": [2, 3]}, {"A": [0, 1, 4, 5], "V": [2, 3, 6, 7]}
        GLA_RINGS = {"A": [0, 1, 7], "V": [2, 3]}
        CELL = {"A": [0, 1, 4, 6, 7], "V": [2, 3, 5]}
        LAST_HEAD = {"A": [0, 1, 4], "V": [2, 3]}
        turn_of, last_on, bank_of = {"A": 0, "V": 0}, {}, {}

        ident = const[:, K_ID:K_ID + P]
        ones = const[:, K_ONE:K_ONE + P]
        block = ctx.enter_context(nc.Block())
        landed = [0] * RING
        starts, plan = [], []
        mod_slot = {}
        SEG = {"x": (TC, TX), "c": (0, TC)}

        def segs(l):
            return ["x", "c"] if l < DEPTH - 1 else ["x"]

        def set1(l):
            return [(I["norm_g"][l], 0, 8), (I["b_mod"][l], 8, 24),
                    (I["b_in"][l, 0:C_LR], 32, 24), (I["b_in"][l, C_AQ:C_AK], 56, 4),
                    (I["b_in"][l, C_AG:C_M], 60, 4), (I["b_in"][l, C_M:C_M + 3 * D], 64, 24),
                    (I["conv_dw_b"][l], 88, 4), (I["conv_ln_g"][l], 92, 4), (I["conv_ln_b"][l], 96, 4),
                    (I["gla_b_gate"][l, 0], 100, 2), (I["gla_b_gate"][l, 1], 102, 2),
                    (I["gla_norm_g"][l], 104, 1)]

        def set1h(l):
            b = I["b_in"][l]
            return [(b[C_AK:C_AK + 64], 105), (b[C_AK + 64:C_AK + 128], 106),
                    (I["q_norm_g"][l], 107), (I["k_norm_g"][l], 108)]

        N_G, B_MOD, B_IN, B_AQ, B_AG, B_M, CW_B, LN_G, LN_B, G_B, G_N, B_AK, QN, KN, B_LR = (
            0, 8, 32, 56, 60, 64, 88, 92, 96, 100, 104, 105, 107, 108, 109)

        def set2(l):
            return [(I["norm_g_2"][l], 0, 8), (I["b_ada_2"][l], 8, 24),
                    (I["conv_w_2"][l].rearrange("a b -> (a b)"), 32, 64), (I["conv_b_2"][l], 96, 16),
                    (I["gn_m_2"][l], 112, 8), (I["gn_r_2"][l], 120, 8)]

        def col(s, r):
            return cols[:, s, r:r + 1]

        @block.tensor
        def _(eng):
            pe = Lane(m, eng, "pe")
            pe.stage("start")

            rings = [WIDE]

            def claim(*banks):
                for b in banks:
                    if b in last_on:
                        eng.wait_ge(*at(("free", last_on.pop(b))))

            def next_bank(ring, key):
                turn_of[ring] += 1
                b = rings[0][ring][turn_of[ring] % len(rings[0][ring])]
                if b in last_on:
                    eng.wait_ge(*at(("free", last_on[b])))
                last_on[b] = key
                bank_of[key] = bank[b]
                return b

            def job(ring, key, mms):
                mms(bank[next_bank(ring, key)]).then_inc(*pe.tell(("full", key)))

            def weights(view, K, C, parts=None):
                n = len(plan)
                slot = wring[:, n % RING, 0:K * C].rearrange("p (k c) -> p k c", c=C)
                plan.append([parts(slot) if parts else [(slot, view)], None])
                landed[n % RING] += 16 * len(plan[n][0])
                eng.wait_ge(m.sem(f"w_slot{n % RING}"), landed[n % RING])
                return wring[:, n % RING, 0:K * C].rearrange("p (k c) -> p k c", c=C)

            def used(key):
                plan[-1][1] = key

            def wv(t, c0, C):
                return t[:, c0:c0 + C].rearrange("(k p) c -> p k c", p=P)

            def acc(parts):
                def mms(out):
                    for i, (o_, a, b_) in enumerate(parts):
                        last = eng.matmul(o_(out), a, b_, start=(i == 0), stop=(i == len(parts) - 1))
                    return last
                return mms

            def project(key, w, c, src, K, sg, ring="A", M=P):
                t0, n = SEG[sg]
                job(ring, key, acc([(lambda o_: o_[0:M, 0:n], w[:, k, c:c + M], src[:, k, t0:t0 + n])
                                    for k in range(K)]))

            def first_product(key, w, L, sg, M):
                t0, n = SEG[sg]
                b = next_bank("A", key)
                for k in range(KD):
                    eng.wait_ge(*at(("h ready", L, sg, k)))
                    mm = eng.matmul(bank[b][0:M, 0:n], w[:, k, 0:M], hT[:, k, t0:t0 + n], start=(k == 0), stop=(k == KD - 1))
                mm.then_inc(*pe.tell(("full", key)))

            def tiles_by_part(name, l, wt, c0, ntile, seg, first=0):
                for j0 in range(first, first + ntile, 2):
                    w = weights(wv(wt, c0 + j0 * P, 2 * P), KD, 2 * P)
                    for j in range(2):
                        for sg in seg:
                            t0, n = SEG[sg]
                            key = (name, l, j0 + j, sg)
                            b = next_bank("A", key)
                            for k in range(KD):
                                mm = eng.matmul(bank[b][:, 0:n], w[:, k, j * P:(j + 1) * P], hT[:, k, t0:t0 + n],
                                                start=(k == 0), stop=(k == KD - 1))
                                if k == KD - 1:
                                    mm.then_inc(*pe.tell(("full", key)))
                                if k % 2:
                                    yield
                    used(("full", (name, l, j0 + 1, seg[-1])))

            def tiles(*a):
                for _ in tiles_by_part(*a):
                    pass

            eng.wait_ge(*at("const in"))
            eng.wait_ge(m.sem("x_in"), 16 * 2)
            for k in range(KD):
                for g, u0, nu in (("x", 2, 4), ("c", 0, 2)):
                    def mms(o_, k=k, u0=u0, nu=nu):
                        for u in range(nu):
                            last = eng.transpose(o_[:, u * P:(u + 1) * P], xin[:, u0 + u, k * P:(k + 1) * P], ident)
                        return last
                    job("A", ("xT", k, g), mms)

            def turn_rows(sets):
                for s in sets:
                    job("A", ("cols", s), lambda o_: eng.transpose(o_[:, 0:P], rows[:, s, :], ident))

            eng.wait_ge(*at("first rows in"))
            turn_rows(FIRST_SETS)

            def modulate(L, groups=range(12)):
                for _ in mod_by_part(L, groups):
                    pass

            def mod_by_part(L, groups):
                key = ("mod", L)
                wt, col0, ncol = (I["w_mod"][L], 0, 2) if L < 2 else (I["w_ada_2"][L - 2], 16, 1)
                eng.wait_ge(*at(("cT",)))
                for g in groups:
                    w = weights(wv(wt, g * 256, 256), KD, 256)
                    for j in range(2):
                        job("A", (key, g, j), acc([(lambda o_: o_[:, 0:ncol], w[:, k, j * P:(j + 1) * P],
                                                    cT[:, col0 + k:col0 + k + 8 * (ncol - 1) + 1:8])
                                                   for k in range(KD)]))
                    used(("full", (key, g, 1)))
                    yield

            def mod_load(L, g):
                wt = I["w_mod"][L] if L < 2 else I["w_ada_2"][L - 2]
                n = len(plan)
                plan.append([[(wring[:, n % RING, :].rearrange("p (k c) -> p k c", c=256),
                               wv(wt, g * 256, 256))], ("mod summed", L, g)])
                landed[n % RING] += 16
                mod_slot[L, g] = (n % RING, landed[n % RING])

            def mod_finish(L, g):
                ncol = 2 if L < 2 else 1
                eng.wait_ge(*at(("mod summed", L, g)))
                i = mod_no[0] % 2
                mod_no[0] += 1
                for j in range(2):
                    def mms(o_):
                        for c in range(ncol):
                            last = eng.matmul(o_[:, c:c + 1], (md_first if (L, g) < (0, 8) else md)[:, i, c * 256 + j * P:c * 256 + (j + 1) * P], ones[:, 0:1],
                                              start=True, stop=True)
                        return last
                    job("A", (("mod", L), g, j), mms)

            mod_no = [0]

            def square_sum(L, k):
                for i, sg in enumerate(["x", "c"] if L < 2 else ["x"]):
                    t0, n = SEG[sg]
                    eng.wait_ge(*at(("squares", L, sg, k)))
                    mm = eng.matmul(bank[4 + i][:, 0:n], ones, hT[:, k, t0:t0 + n], start=(k == 0), stop=(k == KD - 1))
                    mm.then_inc(*pe.tell(("ss", L, sg, k)))

            def gla_core(l, p, d, between, rate):
                pe.stage("gla_core")
                key = (l, p, d)
                if d == 0:
                    claim(4, 5, 6)
                for half in range(2):
                    def mms(o_, half=half):
                        for u in range(3):
                            last = eng.transpose(o_[:, u * P:(u + 1) * P],
                                                 bS[:, (half * 3 + u) * P:(half * 3 + u + 1) * P], ident)
                        return last
                    eng.wait_ge(*at(("gla ks", key)))
                    job("A", ("kst", key, half), mms)
                order = [0, 1, 2, 3, 4, 5] if d == 0 else [1, 0, 5, 4, 3, 2]
                steps = [2 * u + c for u in order for c in ((0, 1) if d == 0 else (1, 0))]
                accs = {"x": [bank[4], bank[5]], "c": [bank[6], bank[6]]}
                if d == 0 and (l, p) != (0, 0):
                    eng.wait_ge(*at(("gla out read", l if p else l - 1, 1 - p)))
                if d == 0:
                    gla_gate(l, p, 1)
                    pe.stage("gla_core")
                def att(u):
                    if u is not None and ("c" if u < 2 else "x") in segs(l):
                        eng.wait_ge(*at(("gla qi", key)))
                        eng.wait_ge(*at(("gla ki", key)))
                        job("V", ("att", key, u), acc_two(key, slice(u * P, u * P + P)))
                att(order[0])
                for ui, u in enumerate(order):
                    sg = "c" if u < 2 else "x"
                    outs = sg in segs(l)
                    col0 = u * P if u < 2 else (u - 2) * P
                    att(order[ui + 1] if ui < 5 else None)
                    if outs:
                        eng.wait_ge(*at(("att masked", key, u)))
                        eng.wait_ge(*at(("gla v", l)))
                        for hh in range(2):
                            h = 2 * p + hh
                            c1 = col0 + (hh * 256 if sg == "c" else 0)
                            first = d == 0 and ((sg == "x" and u == 2) or (sg == "c" and u == 0 and hh == 0))
                            last = eng.matmul(accs[sg][hh][:, c1:c1 + P], gv[:, u, h * P:(h + 1) * P],
                                              AM[:, ui % 2, hh * P:(hh + 1) * P], start=first, stop=False,
                                              skip_group_check=True)
                        last.then_inc(*pe.tell(("att used", key, u)))
                    for c in ((0, 1) if d == 0 else (1, 0)):
                        ch = 2 * u + c
                        si = steps.index(ch)
                        if outs and si > 0:
                            eng.wait_ge(*at(("state", key, si)))
                            for hh in range(2):
                                c1 = col0 + c * 64 + (hh * 256 if sg == "c" else 0)
                                last = eng.matmul(accs[sg][hh][:, c1:c1 + 64],
                                                  ST[:, si % 2, hh * P:(hh + 1) * P],
                                                  bQz[hh][:, ch * 64:ch * 64 + 64],
                                                  start=False, skip_group_check=True,
                                                  stop=d == 1 and c == 0 and (u == 2 or (u == 0 and hh == 1)))
                        if outs:
                            if si == 0:
                                m.mark(("state used", key, si), *m.at[("att used", key, u)])
                            else:
                                last.then_inc(*pe.tell(("state used", key, si)))
                        if si < 11:
                            eng.wait_ge(*at(("kst", key, 1)))
                            eng.wait_ge(*at(("gla v", l)))
                            job("V", ("con", key, si),
                                lambda o_: eng.matmul(o_[:, 0:256], kst[c * 64:c * 64 + 64, u, :],
                                                      gv[c * 64:c * 64 + 64, u, p * 256:p * 256 + 256],
                                                      start=True, stop=True))
                            if not outs:
                                m.mark(("state used", key, si), *m.at[("full", ("con", key, si))])
                        for _ in range(rate):
                            next(between, None)
                m.mark(("gla core", key), *m.at[("state used", key, 11)])
                for _ in between:
                    pass

            def acc_two(key, tk):
                def mms(o_):
                    for hh in range(2):
                        last = eng.matmul(o_[:, hh * P:(hh + 1) * P], bK[:, tk], bQz[hh][:, tk], start=True, stop=True)
                    return last
                return mms

            def gla_gate(l, p, d):
                pe.stage("gla_gate")
                for sg in ("x", "c"):
                    t0, n = SEG[sg]
                    eng.wait_ge(*at(("gup", l)))
                    eng.wait_ge(*at(("free", ("lr", l, "c"))))
                    job("A", ("z", (l, p, d), sg),
                        lambda o_: eng.matmul(o_[:, 0:n], gup[32 * d:32 * d + RANK, p * P:(p + 1) * P],
                                              lr[32 * d:32 * d + RANK, t0:t0 + n], start=True, stop=True))

            def gla_out_norm(l, p, between=iter(())):
                pe.stage("gla_norm")
                for hh in range(2):
                    next(between, None)
                    for sg in segs(l):
                        t0, n = SEG[sg]
                        eng.wait_ge(*at(("gla sq", l, 2 * p + hh)))
                        job("A", ("gss", l, 2 * p + hh, sg),
                            lambda o_: eng.matmul(o_[:, 0:n], ones, bC[:, t0:t0 + n], start=True, stop=True))

            def attend(l, sg):
                pe.stage("attend")
                claim(4, 5, 6, 7)
                rings[0] = NARROW
                nq, nkt = (4, 6) if sg == "x" else (2, 2)
                q0 = SEG[sg][0]
                keys = nkt * P
                cnt = [0]

                def scores(h, qb):
                    i = att_no[0]
                    att_no[0] += 1
                    g = h // 4
                    r = slice((h % 2) * 64, (h % 2) * 64 + 64)
                    b0 = 4 + 2 * (i % 2)
                    if i >= 2:
                        eng.wait_ge(*at(("probs", i - 2)))
                    eng.wait_ge(*at(("q ready", l, h // 2, sg)))
                    eng.wait_ge(*at(("k ready", l, g)))
                    w = 384 if sg == "x" else 256
                    for half in range(keys // w):
                        last = eng.matmul(bank[b0 + half][:, 0:w], res[r, 8 + h // 2, q0 + qb * P:q0 + qb * P + P],
                                          ak[r, g, half * w:(half + 1) * w], start=True, stop=True)
                    last.then_inc(*pe.tell(("scores", i)))
                    return i

                def turn(h, qb, i):
                    for half in range(2 if sg == "x" else 1):
                        nb = 3 if sg == "x" else 2

                        def mms(o_, half=half):
                            for u in range(nb):
                                kt = half * nb + u
                                last = eng.transpose(o_[:, u * P:(u + 1) * P], pr[:, i % 3, kt * P:(kt + 1) * P], ident)
                            return last
                        eng.wait_ge(*at(("probs norm", i)))
                        job("V", ("pT", i, half), mms)

                def values(h, qb, i):
                    g = h // 4
                    r0 = (h % 2) * 64
                    key = ("o", l, h, sg)
                    if qb == 0:
                        next_bank("A", key)
                    eng.wait_ge(*at(("pT read", i)))
                    eng.wait_ge(*at(("av", l)))
                    for kt in range(nkt):
                        last = eng.matmul(bank_of[key][r0:r0 + 64, qb * P:(qb + 1) * P], av[:, kt, g * 64:(g + 1) * 64],
                                          pt[:, i % 3, kt, :], start=(kt == 0), stop=(kt == nkt - 1))
                    last.then_inc(*pe.tell(("values", i)))
                    if qb == nq - 1:
                        m.mark(("full", key), *m.at[("values", i)])

                seq = [(h, qb) for h in range(8) for qb in range(nq)]
                ids = {}
                for n_ in range(len(seq) + 3):
                    if n_ < len(seq):
                        ids[n_] = scores(*seq[n_])
                    if 0 <= n_ - 2 < len(seq):
                        turn(*seq[n_ - 2], ids[n_ - 2])
                    if n_ >= 3:
                        values(*seq[n_ - 3], ids[n_ - 3])

            att_no = [0]

            for l in range(DEPTH):
                if l == 0:
                    pe.stage("proj1")
                    for g in range(0, 8, 2):
                        mod_load(0, g + 1)
                        modulate(0, [g])
                        mod_finish(0, g + 1)
                    eng.wait_ge(*at("rows in"))
                    turn_rows(LATER_SETS)
                    claim(4, 5)
                    for k in range(KD):
                        square_sum(0, k)
                starts.append(len(plan))
                pe.stage("proj1")
                rings[0] = GLA_RINGS
                both = ["x", "c"]
                wi = I["w_in"][l]
                w = weights(None, KD, 32 + RANK, lambda slot: [(slot[:, :, 0:32], wv(wi, C_LR, 32)),
                                                               (slot[:, :, 32:], wv(wi, C_LR + RANK, RANK))])
                for sg in both:
                    first_product(("lr", l, sg), w, l, sg, 32 + RANK)
                used(("full", ("lr", l, "c")))
                gla_gate(l, 0, 0)
                pe.stage("proj1")
                tiles("gq", l, wi, C_GQ, 2, segs(l))
                tiles("gk", l, wi, C_GK, 2, both)

                def value_rows(name, c0, width, row, bc):
                    eng.wait_ge(*at("vrow in"))
                    for g0 in range(0, width, 256):
                        cw = min(256, width - g0)
                        w = weights(wv(wi, c0 + g0, cw), KD, cw)
                        for u in range(6):
                            job("A", (name, l, g0 // 256, u), acc(
                                [(lambda o_: o_[:, 0:cw], hT[:, k, u * P:(u + 1) * P], w[:, k, :]) for k in range(KD)]
                                + [(lambda o_: o_[:, 0:cw], ones[row:row + 1, :], const[row:row + 1, K_SEL + bc + g0:K_SEL + bc + g0 + cw])]))
                            yield
                        used(("full", (name, l, g0 // 256, 5)))
                for _ in value_rows("gv", C_GV, 512, 32 * (l + 1), 0):
                    pass

                def keys_values():
                    def twice(slot):
                        return [(slot[:, :, g * P + hf * 64:g * P + hf * 64 + 64], wv(wi, C_AK + g * 64, 64))
                                for g in range(2) for hf in range(2)]
                    w = weights(None, KD, 256, twice)
                    for g in range(2):
                        for sg in both:
                            project(("ak", l, g, sg), w, g * P, hT, KD, sg)
                            yield
                    used(("full", ("ak", l, 1, "c")))
                    yield from value_rows("av", C_AV, 128, 96, l * P)

                by_part = lambda name, c0, first, n: tiles_by_part(name, l, wi, c0, n, segs(l), first)

                def by_job(name, c0, first):
                    for j0 in range(first, 4, 2):
                        w = weights(wv(wi, c0 + j0 * P, 2 * P), KD, 2 * P)
                        for j in range(2):
                            for sg in segs(l):
                                project((name, l, j0 + j, sg), w, j * P, hT, KD, sg)
                                yield
                        used(("full", (name, l, j0 + 1, segs(l)[-1])))

                gla_core(l, 0, 0, by_part("val", C_VAL, 0, 4), 2)
                gla_core(l, 0, 1, chain(by_part("glu", C_GLU, 0, 4), by_part("gg", C_GG, 0, 2)), 2)
                between = by_job("gg", C_GG, 2)
                gla_out_norm(l, 0, between)
                gla_gate(l, 1, 0)
                pe.stage("proj1")
                for _ in between:
                    pass
                tiles("aq", l, wi, C_AQ, 2, segs(l))
                gla_core(l, 1, 0, by_part("aq", C_AQ, 2, 2), 1)
                gla_core(l, 1, 1, keys_values(), 1)
                between = by_job("ag", C_AG, 0)
                gla_out_norm(l, 1, between)
                pe.stage("attn_proj")
                for t in range(len(HEAD_TILES) + 1):
                    if t < len(HEAD_TILES):
                        name, j = HEAD_TILES[t]
                        for sg in (both if name == "k" else segs(l)):
                            t0, n = SEG[sg]
                            eng.wait_ge(*at(("hsq", l, name, j)))
                            job("A", ("hss", l, name, j, sg),
                                lambda o_: eng.matmul(o_[:, 0:n], const[:, K_HALF:K_HALF + P], sq[t % 2][:, t0:t0 + n],
                                                      start=True, stop=True))
                    next(between, None)
                    if t:
                        name, j = HEAD_TILES[t - 1]
                        src = ak[:, j, TC:T] if name == "k" else res[:, 8 + j, TC:T]
                        eng.wait_ge(*at(("normed", l, name, j)))
                        job("V", ("rot", l, name, j),
                            lambda o_: eng.matmul(o_[:, 0:TX], const[:, K_PERM:K_PERM + P], src, start=True, stop=True))
                for _ in between:
                    pass
                if l < DEPTH - 1:
                    attend(l, "c")
                attend(l, "x")
                rings[0] = WIDE
                pe.stage("conv_ln")
                for sg in segs(l):
                    t0, n = SEG[sg]
                    eng.wait_ge(*at(("conv", l)))
                    job("A", ("csum", l, sg), acc([(lambda o_: o_[:, 0:n], ones, res[:, j, t0:t0 + n])
                                                   for j in range(4)]))
                pe.stage("merge")
                tiles("cgate", l, wi, C_CGATE, 2, segs(l))
                pe.stage("conv_ln")
                for sg in segs(l):
                    t0, n = SEG[sg]
                    eng.wait_ge(*at(("conv squares", l, sg)))
                    job("A", ("csq", l, sg), acc([(lambda o_: o_[:, 0:n], ones, mT[:, j, t0:t0 + n])
                                                  for j in range(4)]))
                pe.stage("merge")
                tiles("cgate", l, wi, C_CGATE, 2, segs(l), 2)
                for a in range(4):
                    mods = mod_groups(l, a)
                    for b_ in range(3):
                        w = weights(wv(wi, C_M + b_ * D + a * 256, 256), KD, 256)
                        for j in range(2):
                            for sg in segs(l):
                                project(("mgate", l, a, b_, j, sg), w, j * P, hT, KD, sg)
                        used(("full", ("mgate", l, a, b_, 1, segs(l)[-1])))
                        if b_:
                            mod_finish(*mods[b_ - 1])
                        mod_load(*mods[b_])
                    for b_, nm in enumerate(("w_conv_out", "w_gla_out", "w_attn_out")):
                        if a == 0:
                            eng.wait_ge(*at(("branch", l, b_)))
                        w = weights(wv(I[nm][l], a * 256, 256), 4, 256)
                        for j in range(2):
                            for sg in segs(l):
                                project(("mout", l, a, b_, j, sg), w, j * P, res[:, 4 * b_:4 * b_ + 4, :], 4, sg)
                        used(("full", ("mout", l, a, b_, 1, segs(l)[-1])))
                        if b_ < len(mods) - 2:
                            mod_finish(*mods[2 + b_])
                        if b_ < len(mods) - 3:
                            mod_load(*mods[3 + b_])
                eng.wait_ge(*at(("merged", l, KD - 1)))
                claim(4, 5)
                rings[0] = {"A": [0, 1], "V": [2, 3, 6, 7]}
                for j in range(0, KD, 2):
                    w = weights(wv(I["w_out"][l], j * P, 2 * P), KD, 2 * P)
                    for i in range(2):
                        for sg in segs(l):
                            project(("y", l, j + i, sg), w, i * P, mT, KD, sg, "V")
                    used(("full", ("y", l, j + 1, segs(l)[-1])))
                    if j:
                        square_sum(l + 1, j - 2)
                        square_sum(l + 1, j - 1)
                square_sum(l + 1, KD - 2)
                square_sum(l + 1, KD - 1)

            for l in range(DEPTH):
                L = 2 + l
                starts.append(len(plan))
                wi = I["w_in_2"][l]
                pe.stage("proj2")
                rings[0] = CELL
                w = weights(None, KD, 36, lambda slot: [(slot[:, :, 0:4], wv(wi, C_MI, 4)),
                                                        (slot[:, :, 4:36], wv(wi, C_MI - 24, 32))])
                first_product(("if", l), w, L, "x", 36)
                used(("full", ("if", l)))

                def gate_cols():
                    def mms(o_):
                        for c in range(NCH):
                            for q_, r_ in enumerate((rI, rM, rF, rW)):
                                o4 = (c * 4 + q_) * 4
                                last = eng.transpose(o_[:, o4:o4 + 4], r_[0:4, c * P:(c + 1) * P], ident[0:4, 0:4])
                        return last
                    eng.wait_ge(*at(("gate rows", l)))
                    job("A", ("gcols", l), mms)

                    def mms2(o_):
                        for h in range(4):
                            last = eng.matmul(o_[:, h * NCH:(h + 1) * NCH], const[0:4, K_SEL + h * P:K_SEL + (h + 1) * P],
                                              rI[0:4, P - 1:TX:P], start=True, stop=True)
                        return last
                    job("A", ("decay", l), mms2)

                w2 = None
                w_out, out_plan = [], []
                for kind, n, *x in steps2():
                    h, r, b = n % 4, n // 4, n % 2
                    base = C_RQ if r else 0
                    q, v = qk2[b], vv[b]
                    if kind == "mod load":
                        if l < DEPTH - 1:
                            mod_load(L + 1, x[0])
                    elif kind == "mod":
                        if l < DEPTH - 1:
                            mod_finish(L + 1, x[0])
                    elif kind == "out":
                        j = x[0]
                        if j == 0:
                            rings[0] = LAST_HEAD
                        claim(7 - j)
                        w_out.append(weights(wv(I["w_out_2"][l], j * P, P), 16, P))
                        out_plan.append(len(plan) - 1)
                        eng.wait_ge(*at(("ys", l, 6)))
                        for k in range(14):
                            eng.matmul(bank[7 - j][:, 0:TX], w_out[j][:, k, :], ys[:, k, :], start=(k == 0), stop=False)
                    elif kind == "gates":
                        gate_cols()
                    elif kind == "load":
                        w2 = weights(wv(wi, base + x[0] * D + h * HD2, HD2), KD, HD2)
                    elif kind == "qk":
                        project(("qk", l, n, x[0]), w2, (x[0] % 2) * P, hT, KD, "x")
                        used(("full", ("qk", l, n, x[0])))
                    elif kind == "v":
                        u = x[0]
                        job("A", ("v2", l, n, u), acc([(lambda o_: o_[:, 0:HD2], hT[:, k, TC + u * P:TC + (u + 1) * P],
                                                        w2[:, k, :]) for k in range(KD)]))
                        used(("full", ("v2", l, n, u)))
                    elif kind == "gate":
                        project(("gate2", l, n, x[0], x[1]), w2, x[1] * P, hT, KD, "x")
                        used(("full", ("gate2", l, n, x[0], x[1])))
                    elif kind == "ub":
                        eng.wait_ge(*at(("gate rows", l)))
                        job("V", ("ub", l, n), lambda o_: eng.matmul(o_[:, 0:TX], const[0:4, K_SEL + h * P:K_SEL + (h + 1) * P],
                                                                     rU[0:4, :], start=True, stop=True))
                    else:
                        c = x[0]
                        k = (l, n, c)
                        ts = slice(c * P, (c + 1) * P)
                        W = HD2 if r else HD2 + 1
                        if kind == "scores":
                            eng.wait_ge(*at(("qk ready", l, n)))
                            job("V", ("s2", k), acc([(lambda o_: o_[:, 0:P], q[:, 2 + j, ts], q[:, j, ts]) for j in range(2)]))
                            if c < NCH - 1:
                                def mms(o_):
                                    for j in range(2):
                                        last = eng.transpose(o_[:, j * P:(j + 1) * P], q[:, 2 + j, ts], ident)
                                    return last
                                eng.wait_ge(*at(("qk ready", l, n)))
                                job("A", ("kT", k), mms)
                        elif kind == "values":
                            eng.wait_ge(*at(("sw", k)))
                            eng.wait_ge(*at(("v2 ready", l, n)))
                            job("A", ("intra", k), lambda o_: eng.matmul(o_[:, 0:W], SW[:, :], v[:, c, 0:W], start=True, stop=True))
                            if c > 0:
                                eng.wait_ge(*at(("C", (l, n, c - 1), 1)))
                                job("V", ("inter", k), acc([(lambda o_: o_[:, 0:W], q[:, j, ts], C2[:, j, 0:W])
                                                            for j in range(2)]))
                            if c < NCH - 1:
                                for j in range(2):
                                    eng.wait_ge(*at(("kw", k)))
                                    eng.wait_ge(*at(("v2 ready", l, n)))
                                    job("V", ("dC", k, j), lambda o_: eng.matmul(o_[:, 0:W], KW[:, j * P:(j + 1) * P], v[:, c, 0:W],
                                                                                 start=True, stop=True))
                        elif kind == "turn":
                            def mms3(o_):
                                for j in range(2):
                                    last = eng.transpose(o_[:, j * P:(j + 1) * P], HN[:, j * P:(j + 1) * P], ident)
                                return last
                            eng.wait_ge(*at(("hn", k)))
                            job("V", ("hT", k), mms3)
                pe.stage("out2")
                for j in range(OUT_EARLY):
                    key = ("y", L, j, "x")
                    eng.wait_ge(*at(("ys", l, 7)))
                    for k in range(14, 16):
                        mm = eng.matmul(bank[7 - j][:, 0:TX], w_out[j][:, k, :], ys[:, k, :], start=False, stop=(k == 15))
                    mm.then_inc(*pe.tell(("full", key)))
                    last_on[7 - j], bank_of[key] = key, bank[7 - j]
                    plan[out_plan[j]][1] = ("full", key)
                claim(4)
                rings[0] = {"A": [0, 1], "V": [2, 3, 6, 7]}
                turn_of["V"] = -1
                for j in range(OUT_EARLY, KD):
                    w = weights(wv(I["w_out_2"][l], j * P, P), 16, P)
                    job("V", ("y", L, j, "x"), acc([(lambda o_: o_[:, 0:TX], w[:, k, :], ys[:, k, :])
                                                    for k in range(16)]))
                    used(("full", ("y", L, j, "x")))
                    for k in range(j - 1) if j == OUT_EARLY else [j - 2]:
                        square_sum(L + 1, k)
                square_sum(L + 1, KD - 2)
                square_sum(L + 1, KD - 1)

            pe.stage("end")
            rings[0] = NARROW
            for u in range(4):
                for half in range(2):
                    def mms(o_, u=u, half=half):
                        for k in range(4):
                            last = eng.transpose(o_[:, k * P:(k + 1) * P],
                                                 hT[:, half * 4 + k, TC + u * P:TC + (u + 1) * P], ident)
                        return last
                    eng.wait_ge(*at(("h ready", 4, "x", KD - 1)))
                    job("A", ("final", u, half), mms)


        @block.scalar
        def _(eng):
            act = Lane(m, eng, "act")
            act.stage("start")

            def fn(out_, in_, func, key=None, **kw):
                act.link(eng.activation(out_, in_, func, **kw), key)

            def evac(key, out_, lo, n, func=ACT.Copy, rows_=slice(0, P), **kw):
                eng.wait_ge(*at(("full", key)))
                fn(out_, bank_of[key][rows_, lo:lo + n], func, ("free", key), **kw)

            for k in range(KD):
                for g in ("x", "c"):
                    t0, n = SEG[g]
                    evac(("xT", k, g), xT[:, k, t0:t0 + n], 0, n)
            evac(("cols", 6), cols[:, 6, :], 0, P)
            fn(cT[:, :], cols[:, 6, 8:32], ACT.Silu, ("cT",))
            evac(("cols", 0), cols[:, 0, :], 0, P)

            def modulate(L, groups=range(12)):
                act.stage("modulation")
                s, ncol = (L, 2) if L < 2 else (L + 2, 1)
                for g in groups:
                    for j in range(2):
                        f = 2 * g + j
                        evac((("mod", L), g, j), modT[:, L % 2, f, 0:ncol], 0, ncol, ACT.Identity,
                             bias=col(s, B_MOD + f))

            def head_of_layer(L):
                act.stage("norm")
                sgs = list(enumerate(("x", "c")))[:2 if L < 2 else 1]
                for c_, sg in sgs:
                    t0, n = SEG[sg]
                    eng.wait_ge(*at(("ss", L, sg, KD - 1)))
                    fn(rstd[:, t0:t0 + n], ps[:, 4 + c_, 0:n], ACT.Sqrt, ("std", L, sg), scale=1.0 / D, bias=eps[:, :])
                for c_, sg in sgs if L < 4 else ():
                    t0, n = SEG[sg]
                    for k in range(KD):
                        eng.wait_ge(*at(("h scaled", L, sg, k)))
                        fn(hT[:, k, t0:t0 + n], hT[:, k, t0:t0 + n], ACT.Identity,
                           ("h ready", L, sg, k), bias=modT[:, L % 2, k, c_:c_ + 1])

            def tiles(name, l, dst, ntile, seg, func=ACT.Identity, b0=None, off=None, first=0):
                for j in range(first, first + ntile):
                    for sg in seg:
                        t0, n = SEG[sg]
                        t1 = off[sg] + PAD if off else t0
                        kw = {"bias": col(l, b0 + j)} if b0 is not None else {}
                        evac((name, l, j, sg), dst[:, j, t1:t1 + n], 0, n, func, **kw)

            def gate_first(l, p, d):
                act.stage("gla_gate")
                key = (l, p, d)
                i = l * 4 + p * 2 + d
                if d:
                    eng.wait_ge(*at(("gla ki", (l, p, 0))))
                if d == 0 and i:
                    eng.wait_ge(*at(("gla out done", (i - 1) // 4, (i - 1) // 2 % 2)))
                for sg in ("x", "c"):
                    t0, n = SEG[sg]
                    evac(("z", key, sg), bA[:, t0:t0 + n], 0, n, ACT.Identity, bias=col(l, G_B + 2 * d + p))
                fn(bE, bA, ACT.Abs)
                fn(bE, bE, ACT.Exp, scale=-1.0)
                fn(bE, bE, ACT.Ln, ("gla ln", key), bias=1.0)

            def gate_second(l, p, d):
                act.stage("gla_gate")
                key = (l, p, d)
                eng.wait_ge(*at(("gla cum", key)))
                fn(bE, bC, ACT.Exp, ("gla e", key), scale=1.0 / 16)
                fn(bS, bS, ACT.Exp, ("gla es", key), scale=1.0 / 16)
                end = bC[:, 63:T:64] if d == 0 else bC[:, 0:T:64]
                fn(dec[d], end, ACT.Exp, ("gla dec", key), scale=1.0 / 16)

            def gate_third(l, p, d):
                act.stage("gla_gate")
                if d:
                    eng.wait_ge(*at(("gla core", (l, p, 0))))
                fn(bK, bC, ACT.Exp, ("gla ek", (l, p, d)), scale=-1.0 / 16)

            def kstate(l, p, d):
                act.stage("gla_core")
                key = (l, p, d)
                for half in range(2):
                    evac(("kst", key, half), kst[:, half * 3:half * 3 + 3, :], 0, 384)
                    m.mark(("kst", key, half), *m.at[("free", ("kst", key, half))])

            def out_norm(l, p, between=iter(())):
                act.stage("gla_norm")
                for hh, buf in ((0, bA), (1, bK)):
                    eng.wait_ge(*at(("gla core", (l, p, 1))))
                    for sg in segs(l):
                        t0, n = SEG[sg]
                        src = ps[:, 4 + hh, 0:512] if sg == "x" else ps[:, 6, hh * 256:hh * 256 + 256]
                        fn(buf[:, t0:t0 + n], src, ACT.Copy)
                    m.mark(("gla o", l, 2 * p + hh), act.name, act.n[act.name])
                m.mark(("gla out read", l, p), act.name, act.n[act.name])
                for hh in range(2):
                    next(between, None)
                    act.stage("gla_norm")
                    for sg in segs(l):
                        t0, n = SEG[sg]
                        evac(("gss", l, 2 * p + hh, sg), bE[:, t0:t0 + n], 0, n, ACT.Sqrt, scale=1.0 / P, bias=eps[:, :])

            att_no = [0]

            def attend(l, sg):
                act.stage("attend")
                nq, nkt = (4, 6) if sg == "x" else (2, 2)
                q0 = SEG[sg][0]
                n_all = 8 * nq
                for n_ in range(n_all + 3):
                    if n_ < n_all:
                        i = att_no[0] + n_
                        eng.wait_ge(*at(("nmax", i)))
                        if i >= 3:
                            eng.wait_ge(*at(("pT read", i - 3)))
                        b0 = 4 + 2 * (i % 2)
                        if sg == "x":
                            src = ps[:, b0:b0 + 2, 0:384]
                            dst = pr[:, i % 3, :].rearrange("p (a b) -> p a b", b=384)
                        else:
                            src, dst = ps[:, b0, 0:256], pr[:, i % 3, 0:256]
                        fn(dst, src, ACT.Exp, ("probs", i), bias=small[:, 40 + i % 2:41 + i % 2],
                           accum_out=small[:, 44 + i % 2:45 + i % 2])
                    if n_ >= 3 and (n_ - 3) % nq == nq - 1:
                        h = (n_ - 3) // nq
                        r = slice((h % 2) * 64, (h % 2) * 64 + 64)
                        evac(("o", l, h, sg), res[r, 8 + h // 2, q0:q0 + nq * P], 0, nq * P, rows_=r)
                att_no[0] += n_all

            for l in range(DEPTH):
                if l == 0:
                    modulate(0, range(8))
                    for s in LATER_SETS:
                        evac(("cols", s), cols[:, s, :], 0, P)
                head_of_layer(l)
                both = ["x", "c"]
                act.stage("proj1")
                for sg in both:
                    t0, n = SEG[sg]
                    evac(("lr", l, sg), lr[0:32 + RANK, t0:t0 + n], 0, n, ACT.Identity, rows_=slice(0, 32 + RANK),
                         bias=cols[0:32 + RANK, l, B_LR:B_LR + 1])
                gate_first(l, 0, 0)
                act.stage("proj1")
                tiles("gq", l, gq, 2, segs(l), b0=B_IN + C_GQ // P)
                tiles("gk", l, gk, 2, both, b0=B_IN + C_GK // P)
                gate_second(l, 0, 0)
                gate_third(l, 0, 0)
                act.stage("proj1")
                for g in range(2):
                    for u in range(6):
                        evac(("gv", l, g, u), gv[:, u, g * 256:(g + 1) * 256], 0, 256)
                m.mark(("gla v", l), *m.at[("free", ("gv", l, 1, 5))])
                kstate(l, 0, 0)
                gate_first(l, 0, 1)
                act.stage("proj1")
                eng.wait_ge(*at(("up zero", l)))
                tiles("val", l, up, 1, segs(l), b0=B_IN, off=UO)
                gate_second(l, 0, 1)
                act.stage("proj1")
                tiles("val", l, up, 3, segs(l), b0=B_IN, off=UO, first=1)
                gate_third(l, 0, 1)
                kstate(l, 0, 1)
                act.stage("proj1")
                tiles("glu", l, res[:, 0:4, :], 4, segs(l), ACT.Sigmoid, B_IN + 4)
                tiles("gg", l, res[:, 4:8, :], 2, segs(l), ACT.Silu, B_IN + C_GG // P)

                def by_job(name, dst, b0, first):
                    for j in range(first, 4):
                        for sg in segs(l):
                            t0, n = SEG[sg]
                            act.stage("proj1")
                            evac((name, l, j, sg), dst[:, j, t0:t0 + n], 0, n, ACT.Silu, bias=col(l, b0 + j))
                            yield

                between = by_job("gg", res[:, 4:8, :], B_IN + C_GG // P, 2)
                out_norm(l, 0, between)
                gate_first(l, 1, 0)
                for _ in between:
                    pass
                act.stage("proj1")
                tiles("aq", l, res[:, 8:12, :], 1, segs(l), b0=B_AQ)
                gate_second(l, 1, 0)
                gate_third(l, 1, 0)
                act.stage("proj1")
                tiles("aq", l, res[:, 8:12, :], 1, segs(l), b0=B_AQ, first=1)
                kstate(l, 1, 0)
                gate_first(l, 1, 1)
                act.stage("proj1")
                tiles("aq", l, res[:, 8:12, :], 1, segs(l), b0=B_AQ, first=2)
                gate_second(l, 1, 1)
                act.stage("proj1")
                tiles("aq", l, res[:, 8:12, :], 1, segs(l), b0=B_AQ, first=3)
                gate_third(l, 1, 1)
                kstate(l, 1, 1)
                act.stage("attn_proj")
                eng.wait_ge(*at(("gla ks", (l, 1, 1))))
                for g in range(2):
                    for sg in both:
                        t0, n = SEG[sg]
                        evac(("ak", l, g, sg), ak[:, g, t0:t0 + n], 0, n, ACT.Identity, bias=col(l, B_AK + g))
                for u in range(6):
                    evac(("av", l, 0, u), av[:, u, :], 0, P)
                m.mark(("av", l), *m.at[("free", ("av", l, 0, 5))])
                between = by_job("ag", ag, B_AG, 0)
                out_norm(l, 1, between)
                for t, (name, j) in enumerate(HEAD_TILES):
                    act.stage("attn_proj")
                    for sg in (both if name == "k" else segs(l)):
                        t0, n = SEG[sg]
                        if t > 1:
                            eng.wait_ge(*at(("normed", l, *HEAD_TILES[t - 2])))
                        if t == 1:
                            eng.wait_ge(*at(("gla out done", l, 1)))
                        evac(("hss", l, name, j, sg), rs[t % 2][:, t0:t0 + n], 0, n, ACT.Sqrt, bias=eps[:, :])
                    next(between, None)
                for _ in between:
                    pass
                if l < DEPTH - 1:
                    attend(l, "c")
                attend(l, "x")
                act.stage("conv_ln")
                for sg in segs(l):
                    t0, n = SEG[sg]
                    evac(("csum", l, sg), sq[0][:, t0:t0 + n], 0, n, scale=1.0 / 512)
                act.stage("merge")
                tiles("cgate", l, cg, 2, segs(l), ACT.Silu, B_IN + C_CGATE // P)
                act.stage("conv_ln")
                for sg in segs(l):
                    t0, n = SEG[sg]
                    evac(("csq", l, sg), rs[0][:, t0:t0 + n], 0, n, ACT.Sqrt, scale=1.0 / 512, bias=eps[:, :])
                act.stage("merge")
                tiles("cgate", l, cg, 2, segs(l), ACT.Silu, B_IN + C_CGATE // P, first=2)
                act.stage("conv_ln")
                for j in range(4):
                    for sg in segs(l):
                        t0, n = SEG[sg]
                        eng.wait_ge(*at(("conv scaled", l, j, sg)))
                        fn(res[:, j, t0:t0 + n], res[:, j, t0:t0 + n], ACT.Silu, ("conv act", l, j, sg),
                           scale=col(l, LN_G + j), bias=col(l, LN_B + j))
                act.stage("merge")
                eng.wait_ge(*at(("branch", l, 2)))
                eng.wait_ge(*at(("branch", l, 0)))
                for a in range(4):
                    mods = mod_groups(l, a)
                    if a:
                        eng.wait_ge(*at(("merged", l, 2 * a - 1)))
                    for b_ in range(3):
                        for j in range(2):
                            for sg in segs(l):
                                t0, n = SEG[sg]
                                evac(("mgate", l, a, b_, j, sg), mg[:, 2 * b_ + j, t0:t0 + n], 0, n, ACT.Sigmoid,
                                     bias=col(l, B_M + 8 * b_ + 2 * a + j))
                        if b_:
                            modulate(mods[b_ - 1][0], [mods[b_ - 1][1]])
                            act.stage("merge")
                    for b_ in range(3):
                        for j in range(2):
                            for sg in segs(l):
                                t0, n = SEG[sg]
                                evac(("mout", l, a, b_, j, sg), my[:, 2 * b_ + j, t0:t0 + n], 0, n)
                        if b_ < len(mods) - 2:
                            modulate(mods[2 + b_][0], [mods[2 + b_][1]])
                            act.stage("merge")

            act.stage("rotary")
            eng.wait_ge(*at(("angles", 0)))
            fn(rope[:, 1, :], WT, ACT.Sin)
            eng.wait_ge(*at(("angles", 1)))
            fn(rope[:, 0, :], zt, ACT.Sin, ("rotary",))

            for l in range(DEPTH):
                L = 2 + l
                s = L + 2
                head_of_layer(L)
                act.stage("cell_gates")
                eng.wait_ge(*at(("full", ("if", l))))
                fn(rI[0:4, :], bank_of["if", l][0:4, 0:TX], ACT.Identity, bias=small[0:4, 24 + 2 * l:25 + 2 * l])
                evac(("if", l), rF[0:4, :], 0, TX, ACT.Identity, rows_=slice(32, 36), bias=small[0:4, 25 + 2 * l:26 + 2 * l])
                fn(rM[0:4, :], rF[0:4, :], ACT.Abs)
                fn(rM[0:4, :], rM[0:4, :], ACT.Exp, scale=-1.0)
                fn(rM[0:4, :], rM[0:4, :], ACT.Ln, ("f ln", l), bias=1.0)
                act.stage("cell")

                def silu(n, j):
                    eng.wait_ge(*at(("conv2", l, n, j)))
                    q = qk2[n % 2]
                    last = j == 3
                    cb = col(s, 96 + (8 if j >= 2 else 0) + 2 * (n % 4) + j % 2)
                    fn(q[:, j, :], q[:, j, :], ACT.Silu, ("qk ready", l, n) if last else None, bias=cb)

                for kind, n, *x in steps2():
                    h, r, b = n % 4, n // 4, n % 2
                    if kind == "mod":
                        if l < DEPTH - 1:
                            modulate(L + 1, [x[0]])
                            act.stage("cell")
                    elif kind == "gates":
                        evac(("gcols", l), qcol[:, :, :, :], 0, 64)
                        fn(qcol[:, :, 0, :], qcol[:, :, 0, :], ACT.Exp)
                        fn(qcol[:, :, 1, :], qcol[:, :, 1, :], ACT.Exp, scale=-1.0)
                        fn(qcol[:, :, 2, :], qcol[:, :, 2, :], ACT.Exp, ("gate cols", l))
                        evac(("decay", l), decc[:, :, :], 0, 16, ACT.Exp)
                    elif kind == "qk":
                        j = x[0]
                        if n or l:
                            eng.wait_ge(*at(("pre read", l, n - 1, j) if n else ("pre read", l - 1, 7, j)))
                        if r:
                            evac(("qk", l, n, j), pre[:, j, 0:TX], 0, TX)
                        else:
                            evac(("qk", l, n, j), pre[:, j, TAPS2 - 1:TAPS2 - 1 + TX], 0, TX)
                            if j:
                                silu(n, j - 1)
                    elif kind == "v":
                        u = x[0]
                        if not r and u == 0:
                            silu(n, 3)
                        evac(("v2", l, n, u), vv[b][:, u, 0:HD2], 0, HD2)
                        if u == NCH - 1:
                            m.mark(("v2 ready", l, n), *m.at[("free", ("v2", l, n, u))])
                    elif kind == "gate":
                        b_, j = x
                        key = ("gate2", l, n, b_, j)
                        if b_ == 1:
                            if n or j:
                                eng.wait_ge(*at(("zt free", l, n, j)))
                            evac(key, zt, 0, TX, ACT.Silu)
                        else:
                            evac(key, ys[:, 2 * n + j, :], 0, TX, ACT.Silu if r else ACT.Sigmoid)
                    elif kind == "ub":
                        eng.wait_ge(*at(("wt logs", l, n)))
                        fn(WT, WT, ACT.Exp, ("wt", l, n))
                    elif kind == "scores":
                        c = x[0]
                        k = (l, n, c)
                        if c < NCH - 1:
                            scale = const[:, K_ZETA + h:K_ZETA + h + 1] if r else qcol[:, c, 2, h:h + 1]
                            if c:
                                eng.wait_ge(*at(("full", ("dC", (l, n, c - 1), 1))))
                            elif n:
                                eng.wait_ge(*at(("full", ("dC", (l, n - 1, NCH - 2), 1))))
                            if not r:
                                eng.wait_ge(*at(("gate cols scaled", l)))
                            evac(("kT", k), KW, 0, HD2, ACT.Copy, scale=scale)
                            m.mark(("kw", k), *m.at[("free", ("kT", k))])
                    elif kind == "values":
                        c = x[0]
                        k = (l, n, c)
                        if c or n:
                            eng.wait_ge(*at(("hn", (l, n, c - 1) if c else (l, n - 1, NCH - 1))))
                        W = HD2 if r else HD2 + 1
                        evac(("intra", k), NI[:, 0:W], 0, W)
                        eng.wait_ge(*at(("var", k)))
                        fn(small[:, 56:57], small[:, 55:56], ACT.Sqrt, ("sd", k), bias=eps[:, :])

            act.stage("end")
            head_of_layer(4)
            for u in range(4):
                for half in range(2):
                    evac(("final", u, half), xout[:, u, half * 512:(half + 1) * 512], 0, 512)


        @block.vector
        def _(eng):
            dve = Lane(m, eng, "dve")
            dve.stage("start")
            tt = lambda o_, a, b, op, key=None: dve.link(eng.tensor_tensor(o_, a, b, op), key)
            ts = lambda o_, a, s1, s2, op0, op1, key=None: dve.link(
                eng.tensor_scalar(o_, a, s1, s2, op0, op1) if s2 is not None else eng.tensor_scalar(o_, a, s1, None, op0), key)
            stt = lambda o_, a, s_, b, op0, op1, key=None: dve.link(
                eng.scalar_tensor_tensor(out=o_, in0=a, scalar=s_, in1=b, op0=op0, op1=op1), key)
            cp = lambda o_, a, key=None: dve.link(eng.tensor_copy(o_, a), key)
            rcp = lambda o_, a, key=None: dve.link(eng.reciprocal(o_, a), key)
            M_, A_, S_ = ALU.mult, ALU.add, ALU.subtract

            dve.link(eng.memset(eps[:, :], EPS))
            dve.link(eng.memset(rows, 0.0), "rows clear")
            def squares(L, k):
                for sg in ["x", "c"] if L < 2 else ["x"]:
                    t0, n = SEG[sg]
                    tt(hT[:, k, t0:t0 + n], xT[:, k, t0:t0 + n], xT[:, k, t0:t0 + n], M_, ("squares", L, sg, k))

            mods_done = []

            def modulate(L, g):
                i = len(mods_done) % 2
                slot, count = mod_slot[L, g]
                w = wring[:, slot, :].rearrange("p (k c) -> p k c", c=256)
                eng.wait_ge(m.sem(f"w_slot{slot}"), count)
                if len(mods_done) > 1:
                    eng.wait_ge(*at(("full", (("mod", mods_done[-2][0]), mods_done[-2][1], 1))))
                ncol, col0 = (2, 0) if L < 2 else (1, 16)
                for c in range(ncol):
                    sums = (md_first if (L, g) < (0, 8) else md)[:, i, c * 256:(c + 1) * 256]
                    ts(sums, w[:, 0, :], cT[:, col0 + 8 * c:col0 + 8 * c + 1], None, M_, None)
                    for k in range(1, KD):
                        stt(sums, w[:, k, :], cT[:, col0 + 8 * c + k:col0 + 8 * c + k + 1], sums, M_, A_,
                            ("mod summed", L, g) if (c, k) == (ncol - 1, KD - 1) else None)
                mods_done.append((L, g))

            def norm(L):
                dve.stage("norm")
                s = L if L < 2 else L + 2
                sgs = list(enumerate(("x", "c")))[:2 if L < 2 else 1]
                if L < 4:
                    eng.wait_ge(*at(("free", (("mod", L), 7, 1))))
                    nc_ = 2 if L < 2 else 1
                    stt(gsT[:, :, 0:nc_], modT[:, L % 2, 8:16, 0:nc_], 1.0,
                        cols[:, s, 0:8].unsqueeze(2).broadcast_to([P, 8, nc_]), A_, M_)
                for c_, sg in sgs:
                    t0, n = SEG[sg]
                    eng.wait_ge(*at(("std", L, sg)))
                    rcp(rstd[:, t0:t0 + n], rstd[:, t0:t0 + n])
                    for k in range(KD):
                        g = gsT[:, k, c_:c_ + 1] if L < 4 else col(6, k)
                        stt(hT[:, k, t0:t0 + n], xT[:, k, t0:t0 + n], g, rstd[:, t0:t0 + n], M_, M_,
                            ("h scaled", L, sg, k))
                if L == 4:
                    m.mark(("h ready", 4, "x", KD - 1), *m.at[("h scaled", 4, "x", KD - 1)])

            def gate_first(l, p, d):
                dve.stage("gla_gate")
                key = (l, p, d)
                eng.wait_ge(*at(("gla ln", key)))
                stt(bA, bA, 0.0, bE, ALU.min, S_)
                eng.wait_ge(*at("gscan in"))
                dve.link(eng.tensor_tensor_scan(bC, gscan[:, :], bA, 0.0, M_, A_))
                v3 = lambda x_: x_.rearrange("p (a b) -> p a b", b=64)
                last = bC[:, 63:T:64].unsqueeze(2).broadcast_to([P, 12, 64])
                if d == 0:
                    tt(v3(bS), last, v3(bC), S_, ("gla cum", key))
                else:
                    tt(v3(bE), last, v3(bC), S_)
                    eng.wait_ge(*at(("full", ("kst", (l, p, 0), 1))))
                    tt(bS, bC, bA, S_)
                    tt(bC, bE, bA, A_, ("gla cum", key))

            def gate_second(l, p, d):
                dve.stage("gla_gate")
                key = (l, p, d)
                t0 = 0 if l < DEPTH - 1 else TC
                eng.wait_ge(*at(("gla es", key)))
                eng.wait_ge(*at(("free", ("gk", l, 1, "c"))))
                tt(bS, gk[:, p, :], bS, M_, ("gla ks", key))
                if d:
                    eng.wait_ge(*at(("gla core", (l, p, 0))))
                for hh in range(2):
                    r = slice(hh * 64, hh * 64 + 64)
                    stt(bQz[hh][r, t0:T], gq[r, p, t0:T], 0.125, bE[r, t0:T], M_, M_, ("gla qi", key) if hh else None)
                eng.wait_ge(*at(("gla ek", key)))
                tt(bK, gk[:, p, :], bK, M_, ("gla ki", key))

            def core(l, p, d):
                dve.stage("gla_core")
                key = (l, p, d)
                order = [0, 1, 2, 3, 4, 5] if d == 0 else [1, 0, 5, 4, 3, 2]
                steps = [2 * u + c for u in order for c in ((0, 1) if d == 0 else (1, 0))]
                mask = const[:, K_CAUS:K_CAUS + P] if d == 0 else const[:, K_ANTI:K_ANTI + P]
                mask = mask.unsqueeze(1).broadcast_to([P, 2, P])
                gate_at = 1 if d == 0 else None

                def masked(ui):
                    u = order[ui]
                    if not ("c" if u < 2 else "x") in segs(l):
                        return
                    if ui >= 2 and ("c" if order[ui - 2] < 2 else "x") in segs(l):
                        eng.wait_ge(*at(("att used", key, order[ui - 2])))
                    k = ("att", key, u)
                    eng.wait_ge(*at(("full", k)))
                    tt(AM[:, ui % 2, :].rearrange("p (a b) -> p a b", b=P),
                       bank_of[k][:, 0:256].rearrange("p (a b) -> p a b", b=P), mask, M_, ("free", k))
                    m.mark(("att masked", key, u), *m.at[("free", k)])
                masked(0)
                for ui, u in enumerate(order):
                    if ui < 5:
                        masked(ui + 1)
                    if ui == gate_at:
                        gate_first(l, p, 1)
                        dve.stage("gla_core")
                    for c in ((0, 1) if d == 0 else (1, 0)):
                        ch = 2 * u + c
                        si = steps.index(ch)
                        if si == 11:
                            continue
                        k = ("con", key, si)
                        eng.wait_ge(*at(("full", k)))
                        eng.wait_ge(*at(("gla dec", key)))
                        if si >= 1:
                            eng.wait_ge(*at(("state used", key, si - 1)))
                        if si == 0:
                            cp(ST[:, 1, :], bank_of[k][:, 0:256], ("free", k))
                        else:
                            stt(ST[:, (si + 1) % 2, :], ST[:, si % 2, :], dec[d][:, ch:ch + 1], bank_of[k][:, 0:256],
                                M_, A_, ("free", k))
                        m.mark(("state", key, si + 1), *m.at[("free", k)])

            def out_norm(l, p):
                dve.stage("gla_norm")
                t0 = 0 if l < DEPTH - 1 else TC
                for hh, buf in ((0, bA), (1, bK)):
                    h = 2 * p + hh
                    eng.wait_ge(*at(("gla o", l, h)))
                    tt(bC[:, t0:T], buf[:, t0:T], buf[:, t0:T], M_, ("gla sq", l, h))
                    for sg in segs(l):
                        eng.wait_ge(*at(("free", ("gss", l, h, sg))))
                    rcp(bE[:, t0:T], bE[:, t0:T], ("gss read", l, h))
                    tt(buf[:, t0:T], buf[:, t0:T], bE[:, t0:T], M_)
                    stt(res[:, 4 + h, t0:T], buf[:, t0:T], col(l, G_N), res[:, 4 + h, t0:T], M_, M_,
                        ("gla out done", l, p) if hh else ("gla half done", l, p))

            att_no = [0]

            def attend(l, sg):
                dve.stage("attend")
                nq, nkt = (4, 6) if sg == "x" else (2, 2)
                n_all = 8 * nq
                for n_ in range(n_all + 2):
                    i = att_no[0] + n_
                    if n_ < n_all:
                        eng.wait_ge(*at(("scores", i)))
                        b0 = 4 + 2 * (i % 2)
                        src, ax = (ps[:, b0:b0 + 2, 0:384], AX.XY) if sg == "x" else (ps[:, b0, 0:256], AX.X)
                        if i >= 2:
                            eng.wait_ge(*at(("probs", i - 2)))
                        dve.link(eng.tensor_reduce(small[:, 40 + i % 2:41 + i % 2], src, ax, ALU.max, negate=True), ("nmax", i))
                    if 1 <= n_ <= n_all:
                        i = att_no[0] + n_ - 1
                        eng.wait_ge(*at(("probs", i)))
                        rcp(small[:, 48 + i % 2:49 + i % 2], small[:, 44 + i % 2:45 + i % 2])
                        ts(pr[:, i % 3, 0:nkt * P], pr[:, i % 3, 0:nkt * P], small[:, 48 + i % 2:49 + i % 2], None, M_, None,
                           ("probs norm", i))
                    if n_ >= 2:
                        i = att_no[0] + n_ - 2
                        nb = 3 if sg == "x" else 2
                        if i >= 3:
                            eng.wait_ge(*at(("values", i - 3)))
                        for half in range(2 if sg == "x" else 1):
                            k = ("pT", i, half)
                            eng.wait_ge(*at(("full", k)))
                            cp(pt[:, i % 3, half * nb:(half + 1) * nb, :],
                               bank_of[k][:, 0:nb * P].rearrange("p (a b) -> p a b", b=P), ("free", k))
                        m.mark(("pT read", i), *m.at[("free", k)])
                att_no[0] += n_all


            for l in range(DEPTH):
                if l == 0:
                    dve.stage("squares")
                    eng.wait_ge(*at(("free", ("xT", KD - 1, "c"))))
                    for k in range(KD):
                        squares(0, k)
                    dve.stage("modulation")
                    eng.wait_ge(*at(("cT",)))
                    for g in range(1, 8, 2):
                        modulate(0, g)
                    for i in range(DEPTH):
                        eng.wait_ge(*at(("free", ("cols", i))))
                        ts(small[:, 20 + i:21 + i], col(i, QN), 0.125, None, M_, None)
                norm(l)
                dve.link(eng.memset(bQz[0][64:128, :], 0.0))
                dve.link(eng.memset(bQz[1][0:64, :], 0.0))
                for p in range(2):
                    gate_first(l, p, 0)
                    gate_second(l, p, 0)
                    core(l, p, 0)
                    gate_second(l, p, 1)
                    core(l, p, 1)
                    out_norm(l, p)
                m.mark(("branch", l, 1), *m.at[("gla out done", l, 1)])
                dve.stage("rope")
                eng.wait_ge(*at("rope in"))
                def tile_of(t):
                    name, j = HEAD_TILES[t]
                    seg = ["x", "c"] if name == "k" else segs(l)
                    return name, j, seg, 0 if "c" in seg else TC, ak[:, j, :] if name == "k" else res[:, 8 + j, :]

                for t in range(len(HEAD_TILES) + 2):
                    if t < len(HEAD_TILES):
                        name, j, seg, t0, src = tile_of(t)
                        for sg in seg:
                            eng.wait_ge(*at(("free", ("ak", l, j, sg) if name == "k" else ("aq", l, j, sg))))
                            if t > 1:
                                eng.wait_ge(*at(("full", ("hss", l, *HEAD_TILES[t - 2], "x"))))
                        tt(sq[t % 2][:, t0:T], src[:, t0:T], src[:, t0:T], M_, ("hsq", l, name, j))
                    if 1 <= t <= len(HEAD_TILES):
                        name, j, seg, t0, src = tile_of(t - 1)
                        g = col(l, KN) if name == "k" else small[:, 20 + l:21 + l]
                        r_ = rs[(t - 1) % 2]
                        for sg in seg:
                            eng.wait_ge(*at(("free", ("hss", l, name, j, sg))))
                        rcp(r_[:, t0:T], r_[:, t0:T])
                        stt(src[:, t0:T], src[:, t0:T], g, r_[:, t0:T], M_, M_, ("normed", l, name, j))
                    if t >= 2:
                        name, j, seg, t0, src = tile_of(t - 2)
                        k = ("rot", l, name, j)
                        eng.wait_ge(*at(("full", k)))
                        tt(tmp[:, 0:TX], bank_of[k][:, 0:TX], rope[:, 1, :], M_, ("free", k))
                        tt(src[:, TC:T], src[:, TC:T], rope[:, 0, :], M_)
                        tt(src[:, TC:T], src[:, TC:T], tmp[:, 0:TX], A_,
                           ("k ready", l, j) if name == "k" else ("q ready", l, j, "x"))
                        if name == "q":
                            m.mark(("q ready", l, j, "c"), *m.at[("q ready", l, j, "x")])
                if l < DEPTH - 1:
                    attend(l, "c")
                attend(l, "x")
                dve.stage("merge")
                t0 = 0 if l < DEPTH - 1 else TC
                last = segs(l)[-1]
                eng.wait_ge(*at(("free", ("ag", l, 3, last))))
                for sg in segs(l):
                    eng.wait_ge(*at(("free", ("o", l, 7, sg))))
                tt(res[:, 8:12, t0:T], res[:, 8:12, t0:T], ag[:, :, t0:T], M_, ("branch", l, 2))
                dve.stage("conv_ln")
                for sg in segs(l):
                    t0, n = SEG[sg]
                    eng.wait_ge(*at(("free", ("csum", l, sg))))
                    mean = sq[0][:, t0:t0 + n].unsqueeze(1).broadcast_to([P, 4, n])
                    tt(res[:, 0:4, t0:t0 + n], res[:, 0:4, t0:t0 + n], mean, S_)
                    tt(mT[:, 0:4, t0:t0 + n], res[:, 0:4, t0:t0 + n], res[:, 0:4, t0:t0 + n], M_, ("conv squares", l, sg))
                for sg in segs(l):
                    t0, n = SEG[sg]
                    eng.wait_ge(*at(("free", ("csq", l, sg))))
                    rcp(rs[0][:, t0:t0 + n], rs[0][:, t0:t0 + n])
                for j in range(4):
                    for sg in segs(l):
                        t0, n = SEG[sg]
                        tt(res[:, j, t0:t0 + n], res[:, j, t0:t0 + n], rs[0][:, t0:t0 + n], M_, ("conv scaled", l, j, sg))
                dve.stage("merge")
                t0 = 0 if l < DEPTH - 1 else TC
                eng.wait_ge(*at(("free", ("cgate", l, 3, last))))
                eng.wait_ge(*at(("conv act", l, 3, last)))
                tt(res[:, 0:4, t0:T], res[:, 0:4, t0:T], cg[:, :, t0:T], M_, ("branch", l, 0))
                for a in range(4):
                    dve.stage("modulation")
                    for L, g in mod_groups(l, a):
                        modulate(L, g)
                    dve.stage("merge")
                    eng.wait_ge(*at(("free", ("mgate", l, a, 2, 1, last))))
                    for b_ in range(3):
                        eng.wait_ge(*at(("free", ("mout", l, a, b_, 1, last))))
                        tt(my[:, 2 * b_:2 * b_ + 2, t0:T], my[:, 2 * b_:2 * b_ + 2, t0:T], mg[:, 2 * b_:2 * b_ + 2, t0:T], M_)
                    tt(my[:, 0:2, t0:T], my[:, 0:2, t0:T], my[:, 2:4, t0:T], A_)
                    tt(mT[:, 2 * a:2 * a + 2, t0:T], my[:, 0:2, t0:T], my[:, 4:6, t0:T], A_, ("merged", l, 2 * a))
                    m.mark(("merged", l, 2 * a + 1), *m.at[("merged", l, 2 * a)])
                eng.wait_ge(*at(("free", (("mod", l), 11, 1))))
                for j in range(KD):
                    for sg in segs(l):
                        t0, n = SEG[sg]
                        k = ("y", l, j, sg)
                        eng.wait_ge(*at(("full", k)))
                        c_ = 0 if sg == "x" else 1
                        stt(xT[:, j, t0:t0 + n], bank_of[k][:, 0:n], modT[:, l % 2, 16 + j, c_:c_ + 1],
                            xT[:, j, t0:t0 + n], M_, A_, ("free", k))
                    squares(l + 1, j)

            dve.stage("rotary")
            eng.wait_ge(*at("positions in"))
            C1, C2_, C3 = 6.28125, 0.0019350051879882812, 3.0199157663446332e-07
            PI = float(np.nextafter(np.float32(np.pi), np.float32(0)))
            cp(WT, posi[:, :])
            ts(WT, WT, const[:, K_FREQ:K_FREQ + 1], None, M_, None)
            ts(UBs, WT, float(1 / (2 * np.pi)), 12582912.0, M_, A_)
            ts(UBs, UBs, -12582912.0, None, A_, None)
            for c_ in (C1, C2_, C3):
                stt(WT, UBs, -c_, WT, M_, A_)
            ts(WT, WT, PI, -PI, ALU.min, ALU.max, ("angles", 0))
            ts(zt, WT, HALF_PI, None, A_, None)
            ts(UBs, zt, PI, -2 * float(np.pi), ALU.is_gt, M_)
            tt(zt, zt, UBs, A_)
            ts(zt, zt, PI, -PI, ALU.min, ALU.max, ("angles", 1))
            dve.link(eng.memset(gscan[0:4, 0:TX], 1.0))
            dve.link(eng.memset(gscan[0:4, 0:TX:CH], 0.0))
            for b in range(2):
                dve.link(eng.memset(vv[b][:, :, HD2:HD2 + 1], 1.0))
            dve.link(eng.memset(small[0:4, 32:33], 0.0))
            dve.link(eng.memset(pre[:, :, 0:TAPS2 - 1], 0.0), ("pre zero", 0))

            for l in range(DEPTH):
                L = 2 + l
                s = L + 2
                norm(L)
                dve.stage("cell_gates")
                R = slice(0, 4)
                v3 = lambda x_: x_[R, :].rearrange("p (a b) -> p a b", b=CH)
                eng.wait_ge(*at(("f ln", l)))
                eng.wait_ge(*at(("free", ("if", l))))
                stt(rF[R, :], rF[R, :], 0.0, rM[R, :], ALU.min, S_)
                dve.link(eng.tensor_tensor_scan(rM[R, :], rF[R, :], rI[R, :], 0.0, A_, ALU.max))
                dve.link(eng.tensor_tensor_scan(rB[R, :], gscan[R, 0:TX], rF[R, :], 0.0, M_, A_))
                tt(rU[R, :], rB[R, :], rM[R, :], S_)
                tt(rW[R, :], rI[R, :], rB[R, :], S_)
                cp(small[R, 33:36], rM[R, CH - 1:TX - 1:CH])
                tt(v3(rI), v3(rU), small[R, 32:36].unsqueeze(2).broadcast_to([4, NCH, CH]), A_)
                tt(v3(rF), v3(rW), rU[R, CH - 1:TX:CH].unsqueeze(2).broadcast_to([4, NCH, CH]), A_, ("gate rows", l))
                dve.stage("cell")
                if l:
                    eng.wait_ge(*at(("pre read", l - 1, 7, 3)))
                    dve.link(eng.memset(pre[:, :, 0:TAPS2 - 1], 0.0), ("pre zero", l))

                def finish(n, c):
                    h, r = n % 4, n // 4
                    k = (l, n, c)
                    W = HD2 if r else HD2 + 1
                    eng.wait_ge(*at(("free", ("intra", k))))
                    src = NI
                    if c:
                        kk = ("inter", k)
                        eng.wait_ge(*at(("full", kk)))
                        w = const[:, K_XI + h:K_XI + h + 1] if r else qcol[:, c, 0, h:h + 1]
                        stt(NM[:, 0:W], bank_of[kk][:, 0:W], w, NI[:, 0:W], M_, A_, ("free", kk))
                        src = NM
                    if c < NCH - 1:
                        for j in range(2):
                            kk = ("dC", k, j)
                            eng.wait_ge(*at(("full", kk)))
                            eng.wait_ge(*at(("free", ("decay", l))))
                            g = const[:, K_GCH + h:K_GCH + h + 1] if r else decc[:, h, c:c + 1]
                            if c == 0:
                                cp(C2[:, j, 0:W], bank_of[kk][:, 0:W], ("free", kk))
                            else:
                                stt(C2[:, j, 0:W], C2[:, j, 0:W], g, bank_of[kk][:, 0:W], M_, A_, ("free", kk))
                            m.mark(("C", k, j), *m.at[("free", kk)])
                    if n or c:
                        eng.wait_ge(*at(("full", ("hT", (l, n, c - 1) if c else (l, n - 1, NCH - 1)))))
                    if not r:
                        ts(small[:, 60:61], src[:, HD2:HD2 + 1], -1.0, qcol[:, c, 1, h:h + 1], M_, ALU.max)
                        tt(small[:, 60:61], small[:, 60:61], src[:, HD2:HD2 + 1], ALU.max)
                        rcp(small[:, 60:61], small[:, 60:61])
                        ts(HN, src[:, 0:HD2], small[:, 60:61], None, M_, None)
                        src = HN
                    dve.link(eng.bn_stats(small[:, 64:70], src[:, 0:HD2]))
                    dve.link(eng.bn_aggr(small[:, 54:56], small[:, 64:70]), ("var", k))
                    eng.wait_ge(*at(("sd", k)))
                    rcp(small[:, 57:58], small[:, 56:57])
                    ts(HN, src[:, 0:HD2], small[:, 54:55], small[:, 57:58], S_, M_, ("hn", k))

                for kind, n, *x in steps2():
                    h, r = n % 4, n // 4
                    if kind == "mod load":
                        if l < DEPTH - 1:
                            dve.stage("modulation")
                            modulate(L + 1, x[0])
                            dve.stage("cell")
                    elif kind == "gates":
                        eng.wait_ge(*at(("gate cols", l)))
                        ts(qcol[:, :, 2, :], qcol[:, :, 2, :], 1.0 / 16, None, M_, None, ("gate cols scaled", l))
                    elif kind == "ub":
                        kk = ("ub", l, n)
                        eng.wait_ge(*at(("full", kk)))
                        for c in range(NCH):
                            stt(WT[:, c * P:(c + 1) * P], bank_of[kk][:, c * P:(c + 1) * P], qcol[:, c, 3, h:h + 1],
                                const[:, K_NEG:K_NEG + P], A_, A_, ("free", kk) if c == NCH - 1 else None)
                        m.mark(("wt logs", l, n), *m.at[("free", kk)])
                    elif kind == "scores":
                        c = x[0]
                        k = (l, n, c)
                        kk = ("s2", k)
                        if n or c:
                            eng.wait_ge(*at(("full", ("intra", (l, n, c - 1) if c else (l, n - 1, NCH - 1)))))
                        if not r:
                            eng.wait_ge(*at(("wt", l, n)))
                        w = const[:, K_DEC + h * P:K_DEC + (h + 1) * P] if r else WT[:, c * P:(c + 1) * P]
                        eng.wait_ge(*at(("full", kk)))
                        stt(SW, bank_of[kk][:, 0:P], 1.0 / 16, w, M_, M_, ("free", kk))
                        m.mark(("sw", k), *m.at[("free", kk)])
                    elif kind == "values":
                        finish(n, x[0])
                    elif kind == "turn":
                        c = x[0]
                        k = (l, n, c)
                        kk = ("hT", k)
                        eng.wait_ge(*at(("full", kk)))
                        eng.wait_ge(*at(("gates ready", l, n)))
                        for j in range(2):
                            y_ = ys[:, 2 * n + j, c * P:(c + 1) * P]
                            stt(y_, bank_of[kk][:, j * P:(j + 1) * P], col(s, 112 + 2 * n + j), y_, M_, M_,
                                ("free", kk) if j else None)
                        if c == NCH - 1:
                            m.mark(("ys", l, n), *m.at[("free", kk)])
                dve.stage("out2")
                for j in range(KD):
                    k = ("y", L, j, "x")
                    eng.wait_ge(*at(("full", k)))
                    stt(xT[:, j, TC:T], bank_of[k][:, 0:TX], modT[:, L % 2, 16 + j, 0:1], xT[:, j, TC:T], M_, A_, ("free", k))
                    squares(L + 1, j)
            norm(4)


        @block.gpsimd
        def _(eng):
            pool = Lane(m, eng, "pool")
            pool.stage("conv")

            def add_product(dst, src, w, scratch):
                pool.link(eng.tensor_scalar(scratch, src, w, 0.0, ALU.mult, ALU.add))
                pool.link(eng.tensor_tensor(dst, dst, scratch, ALU.add))

            for l in range(DEPTH):
                if l:
                    eng.wait_ge(*at(("merged", l - 1, 7)))
                for b0 in (0, TC + PAD, TC + 2 * PAD, TC + TX + 3 * PAD):
                    pool.link(eng.memset(up[:, :, b0:b0 + PAD], 0.0), ("up zero", l) if b0 > TC + TX else None)
                for j in range(4):
                    for sg in segs(l):
                        t0, n = SEG[sg]
                        u0 = UO[sg] + PAD
                        eng.wait_ge(*at(("free", ("glu", l, j, sg))))
                        pool.link(eng.tensor_tensor(up[:, j, u0:u0 + n], up[:, j, u0:u0 + n], res[:, j, t0:t0 + n], ALU.mult))
                        for t in range(TAPS):
                            src = up[:, j, UO[sg] + t:UO[sg] + t + n]
                            w = cols[:, 2 + l, 4 * t + j:4 * t + j + 1]
                            dst = res[:, j, t0:t0 + n]
                            if t == 0:
                                pool.link(eng.tensor_scalar(dst, src, w, col(l, CW_B + j), ALU.mult, ALU.add))
                            else:
                                add_product(dst, src, w, posi[:, 0:n].bitcast(F32))
                m.mark(("conv", l), pool.name, pool.n[pool.name])
            for l in range(DEPTH):
                L = 2 + l
                s = L + 2
                pool.stage("cell")
                for kind, n, *x in steps2():
                    h, r, b = n % 4, n // 4, n % 2
                    q = qk2[b]
                    if kind == "qk":
                        j = x[0]
                        eng.wait_ge(*at(("free", ("qk", l, n, j))))
                        if n >= 2:
                            eng.wait_ge(*at(("full", ("hT", (l, n - 2, NCH - 1)))))
                        if not r:
                            eng.wait_ge(*at(("pre zero", l)))
                            for t in range(TAPS2):
                                src = pre[:, j, t:t + TX]
                                w = col(s, 32 + 16 * t + (8 if j >= 2 else 0) + 2 * h + j % 2)
                                if t == 0:
                                    pool.link(eng.tensor_scalar(q[:, j, :], src, w, None, ALU.mult))
                                else:
                                    add_product(q[:, j, :], src, w, UBs)
                            m.mark(("conv2", l, n, j), pool.name, pool.n[pool.name])
                            m.mark(("pre read", l, n, j), pool.name, pool.n[pool.name])
                        elif j % 2:
                            eng.wait_ge(*at(("rotary",)))
                            a, b_ = pre[:, j - 1, 0:TX], pre[:, j, 0:TX]
                            for out_, x1, x2, op in ((q[:, j - 1, :], a, b_, ALU.subtract), (q[:, j, :], b_, a, ALU.add)):
                                pool.link(eng.tensor_tensor(out_, x1, rope[:, 0, :], ALU.mult))
                                pool.link(eng.tensor_tensor(UBs, x2, rope[:, 1, :], ALU.mult))
                                pool.link(eng.tensor_tensor(out_, out_, UBs, op))
                            for jj in (j - 1, j):
                                m.mark(("pre read", l, n, jj), pool.name, pool.n[pool.name])
                            if j == 3:
                                m.mark(("qk ready", l, n), pool.name, pool.n[pool.name])
                    elif kind == "gate" and not r:
                        b_, j = x
                        if b_ == 1:
                            eng.wait_ge(*at(("free", ("gate2", l, n, 1, j))))
                            pool.link(eng.tensor_tensor(ys[:, 2 * n + j, :], ys[:, 2 * n + j, :], zt, ALU.mult))
                            if j == 0:
                                m.mark(("zt free", l, n, 1), pool.name, pool.n[pool.name])
                            else:
                                m.mark(("gates ready", l, n), pool.name, pool.n[pool.name])
                                if n < 3:
                                    m.mark(("zt free", l, n + 1, 0), pool.name, pool.n[pool.name])
                    elif kind == "gate" and x[1] == 1:
                        eng.wait_ge(*at(("free", ("gate2", l, n, 0, 1))))
                        m.mark(("gates ready", l, n), *m.at[("free", ("gate2", l, n, 0, 1))])


        @block.sync
        def _(eng):
            def sig(name, n, key):
                m.mark(key, name, 16 * n)

            eng.dma_start(const[:, :], I["const"]).then_inc(m.sem("const_in"), 16)
            sig("const_in", 1, "const in")
            eng.dma_start(xin[:, 2:6, :], I["x"][0].rearrange("(u p) d -> p u d", p=P)).then_inc(m.sem("x_in"), 16)
            eng.dma_start(xin[:, 0:2, :], I["ctx"][0].rearrange("(u p) d -> p u d", p=P)).then_inc(m.sem("x_in"), 16)
            parameters = {s: (set1(s), set1h(s)) for s in range(2)}
            parameters.update({4 + s: (set2(s), []) for s in range(2)})
            parameters[6] = [(I["final_g_2"], 0, 8), (I["c"][0], 8, 8), (I["c_ctx"], 16, 8), (I["c_2"][0], 24, 8)], []

            def load_rows(sets, sem):
                n_ = 0
                for s in sets:
                    if s in (2, 3):
                        eng.dma_start(rows[0:4 * TAPS, s, :], I["conv_dw_w"][s - 2].rearrange("t (j p) -> (t j) p", p=P))\
                           .then_inc(m.sem(sem), 16)
                        n_ += 1
                        continue
                    whole, halves = parameters[s]
                    for v, r0, n in whole:
                        eng.dma_start(rows[r0:r0 + n, s, :], v.rearrange("(r p) -> r p", p=P)).then_inc(m.sem(sem), 16)
                        n_ += 1
                    for v, r0 in halves:
                        for hf in range(2):
                            eng.dma_start(rows[r0:r0 + 1, s, hf * 64:hf * 64 + 64], v.unsqueeze(0)).then_inc(m.sem(sem), 16)
                            n_ += 1
                    if s < 2:
                        for d in range(2):
                            eng.dma_start(rows[B_LR:B_LR + 1, s, 32 * d:32 * d + RANK],
                                          I["b_in"][s, C_LR + RANK * d:C_LR + RANK * (d + 1)].unsqueeze(0)).then_inc(m.sem(sem), 16)
                            n_ += 1
                return n_

            eng.wait_ge(*at("rows clear"))
            sig("first_rows_in", load_rows(FIRST_SETS, "first_rows_in"), "first rows in")
            for n, (parts, _) in enumerate(plan[:RING]):
                for dst, view in parts:
                    eng.dma_start(dst, view).then_inc(m.sem(f"w_slot{n % RING}"), 16)
            sig("rows_in", load_rows(LATER_SETS, "rows_in"), "rows in")
            eng.wait_ge(m.sem("const_in"), 16)
            nv = 0
            for l in range(DEPTH):
                eng.dma_start(const[32 * (l + 1):32 * (l + 1) + 1, K_SEL:K_SEL + 512], I["b_in"][l, C_GV:C_GV + 512].unsqueeze(0))\
                   .then_inc(m.sem("vrow_in"), 16)
                eng.dma_start(const[96:97, K_SEL + l * P:K_SEL + (l + 1) * P], I["b_in"][l, C_AV:C_AV + P].unsqueeze(0))\
                   .then_inc(m.sem("vrow_in"), 16)
                for g, nm in enumerate(("b_igate_2", "b_fgate_2")):
                    eng.dma_start(small[0:4, 24 + 2 * l + g:25 + 2 * l + g], I[nm][l].unsqueeze(1)).then_inc(m.sem("vrow_in"), 16)
                nv += 4
            sig("vrow_in", nv, "vrow in")
            eng.dma_start(gscan[:, :], I["gscan"]).then_inc(m.sem("gscan_in"), 16)
            sig("gscan_in", 1, "gscan in")
            eng.dma_start(rope[:, :, :], I["rope"]).then_inc(m.sem("rope_in"), 16)
            sig("rope_in", 1, "rope in")

            def gate_weights(l):
                if l:
                    eng.wait_ge(*at(("full", ("z", (l - 1, 1, 1), "c"))))
                for d in range(2):
                    eng.dma_start(gup[32 * d:32 * d + RANK, :], I["gla_w_gate"][l, d]).then_inc(m.sem("gup_in"), 16)
                sig("gup_in", 2 * (l + 1), ("gup", l))

            gate_weights(0)
            for n, (parts, _) in enumerate(plan):
                if n >= RING:
                    eng.wait_ge(*at(plan[n - RING][1]))
                    for dst, view in parts:
                        eng.dma_start(dst, view).then_inc(m.sem(f"w_slot{n % RING}"), 16)
                if n == starts[1]:
                    gate_weights(1)
                if n == starts[2]:
                    eng.wait_ge(*at(("conv", 1)))
                    eng.dma_start(posi[:, :], I["positions_2"].broadcast_to([P, TX])).then_inc(m.sem("pos_in"), 16)
                    sig("pos_in", 1, "positions in")
            for u in range(4):
                eng.wait_ge(*at(("free", ("final", u, 1))))
                eng.dma_start(out[0, u * P:(u + 1) * P, :], xout[:, u, :]).then_inc(m.sem("out_done"), 16)
            eng.wait_ge(m.sem("out_done"), 16 * 4)

        return m.at


_INS = ['x', 'c', 'ctx', 'c_ctx', 'norm_g', 'w_mod', 'b_mod', 'w_in', 'b_in', 'conv_dw_w', 'conv_dw_b', 'conv_ln_g',
        'conv_ln_b', 'w_conv_out', 'gla_w_gate', 'gla_b_gate', 'gla_norm_g', 'w_gla_out', 'q_norm_g', 'k_norm_g',
        'w_attn_out', 'w_out', 'c_2', 'positions_2', 'w_ada_2', 'b_ada_2', 'norm_g_2', 'w_in_2', 'conv_w_2', 'conv_b_2',
        'b_igate_2', 'b_fgate_2', 'gn_m_2', 'gn_r_2', 'w_out_2', 'final_g_2']


def kernel(**inputs):
    import numpy as _np
    import concourse.bacc as _bacc
    from concourse import mybir as _mybir
    from concourse.bass_utils import run_bass_kernel_spmd as _run

    arrays = {}
    const, gscan, rope = shape_constants()
    given = [(n, _np.ascontiguousarray(inputs[n])) for n in _INS] + [("const", const), ("gscan", gscan), ("rope", rope)]
    for name, a in given:
        arrays[f"in_{name}"] = a

    def program(known):
        nc = _bacc.Bacc("TRN2", target_bir_lowering=False, num_devices=1)
        args = {name: nc.dram_tensor(f"in_{name}", a.shape, _mybir.dt.from_np(a.dtype), kind="ExternalInput").ap()
                for name, a in given}
        out = nc.dram_tensor("out_0", (1, TX, D), F32, kind="ExternalOutput").ap()
        return nc, write_program(nc, args, out, known)

    nc, _ = program(program(None)[1])
    r = _run(nc, [arrays], core_ids=[0])
    return r.results[0]["out_0"]
```
